# Optimizing a Trainium2 kernel written in Bass

```python
import jax, jax.numpy as jnp
from jax import lax
import numpy as np
import math
import jax
import jax.numpy as jnp

D_MODEL = 1024
BATCH = 1
SEQ = 512
DEPTH = 1

D_MIX = D_MODEL
A_WIDTH = D_MIX // 4
A_GROUPS = 4
A_GROUP_DIM = A_WIDTH // A_GROUPS
A_CHUNK = 128
B_WIDTH = D_MIX // 4
B_EXPAND = 64
B_HEADS = B_WIDTH // B_EXPAND
B_KDIM = B_EXPAND
B_VDIM = B_WIDTH // B_HEADS
B_FDIM = B_HEADS * B_KDIM
B_CHUNK = 128
C_WIDTH = D_MIX - A_WIDTH - B_WIDTH
C_HEAD_DIM = 64
C_HEADS = C_WIDTH // C_HEAD_DIM
C_BLOCK = 128
COL_WIDTHS = (A_WIDTH, A_WIDTH, A_WIDTH,
              B_FDIM, B_FDIM, B_WIDTH, B_WIDTH,
              C_WIDTH, C_WIDTH, C_WIDTH, C_WIDTH, C_HEADS)
D_IN = 3 * A_WIDTH + 2 * B_FDIM + 2 * B_WIDTH + 4 * C_WIDTH + C_HEADS
NORM_EPS = 1e-6
F_FLOOR = 1e-30


def _rmsnorm(x, g):
    xf = x.astype(jnp.float32)
    y = xf * lax.rsqrt(jnp.mean(xf * xf, axis=-1, keepdims=True) + NORM_EPS)
    return (y * g.astype(jnp.float32)).astype(x.dtype)

def _split_cols(proj):
    offsets = []
    acc = 0
    for w in COL_WIDTHS[:-1]:
        acc += w
        offsets.append(acc)
    return jnp.split(proj, offsets, axis=-1)

def _gmlp_mixer(u, v, ln_g, ln_b, w_s, b_s):
    bsz, seq, _ = u.shape
    nc = seq // A_CHUNK
    u = jax.nn.gelu(u)
    v = jax.nn.gelu(v).reshape(bsz, nc, A_CHUNK, A_GROUPS, A_GROUP_DIM)
    vf = v.astype(jnp.float32)
    mu = jnp.mean(vf, axis=-1, keepdims=True)
    var = jnp.mean(jnp.square(vf - mu), axis=-1, keepdims=True)
    vn = (vf - mu) * lax.rsqrt(var + NORM_EPS) * ln_g.astype(jnp.float32) + ln_b.astype(jnp.float32)
    causal = jnp.tril(jnp.ones((A_CHUNK, A_CHUNK), dtype=bool))
    w = jnp.where(causal[None], w_s.astype(jnp.float32), 0.0)
    mixed = jnp.einsum('gts,bnsgc->bntgc', w, vn)
    mixed = mixed + jnp.transpose(b_s.astype(jnp.float32))[None, None, :, :, None]
    return u * mixed.reshape(bsz, seq, A_WIDTH).astype(u.dtype)

def _hgrn2_mixer(q, f_logit, i, lb, onorm_g):
    bsz, seq, _ = q.shape
    nc = seq // B_CHUNK
    qf = jax.nn.silu(q.astype(jnp.float32)) * (B_KDIM ** -0.5)
    z = f_logit.astype(jnp.float32)
    f = lb + (1.0 - lb) * jax.nn.sigmoid(z)
    log_f = jnp.log(jnp.maximum(f, F_FLOOR))
    kf = (1.0 - lb) * jax.nn.sigmoid(-z)
    vf = i.astype(jnp.float32)

    def to_chunks(t, d):
        return t.reshape(bsz, nc, B_CHUNK, B_HEADS, d).transpose(1, 0, 3, 2, 4)

    qc, kc, gc = to_chunks(qf, B_KDIM), to_chunks(kf, B_KDIM), to_chunks(log_f, B_KDIM)
    vc = to_chunks(vf, B_VDIM)
    causal = jnp.tril(jnp.ones((B_CHUNK, B_CHUNK), dtype=bool))[None, None, :, :, None]

    def step(state, inp):
        qx, kx, vx, gx = inp
        b = jnp.cumsum(gx, axis=2)
        o_inter = jnp.einsum('bhtk,bhkv->bhtv', qx * jnp.exp(b), state)
        diff = b[:, :, :, None, :] - b[:, :, None, :, :]
        decay = jnp.exp(jnp.where(causal, diff, -jnp.inf))
        scores = jnp.einsum('bhtk,bhsk,bhtsk->bhts', qx, kx, decay)
        o_intra = jnp.einsum('bhts,bhsv->bhtv', scores, vx)
        b_last = b[:, :, -1:, :]
        new_state = (jnp.exp(b_last[:, :, 0, :])[..., None] * state
                     + jnp.einsum('bhsk,bhsv->bhkv', kx * jnp.exp(b_last - b), vx))
        return new_state, o_inter + o_intra

    state0 = jnp.zeros((bsz, B_HEADS, B_KDIM, B_VDIM), jnp.float32)
    _, ys = lax.scan(step, state0, (qc, kc, vc, gc))
    o = ys.transpose(1, 0, 3, 2, 4).reshape(bsz, seq, B_HEADS, B_VDIM)
    o = o * lax.rsqrt(jnp.mean(o * o, axis=-1, keepdims=True) + NORM_EPS) * onorm_g.astype(jnp.float32)
    return o.reshape(bsz, seq, B_WIDTH).astype(q.dtype)

def _fox_mixer(q, k, v, f_logit, b_f):
    bsz, seq, _ = q.shape

    def heads(t):
        return t.reshape(bsz, seq, C_HEADS, C_HEAD_DIM).transpose(0, 2, 1, 3)

    qh, kh, vh = heads(q), heads(k), heads(v)
    log_f = jax.nn.log_sigmoid(f_logit.astype(jnp.float32) + b_f.astype(jnp.float32))
    c = jnp.cumsum(jnp.transpose(log_f, (0, 2, 1)), axis=-1)
    scale = C_HEAD_DIM ** -0.5
    diag_mask = jnp.tril(jnp.ones((C_BLOCK, C_BLOCK), dtype=bool))
    outs = []
    for blk in range(seq // C_BLOCK):
        q0 = blk * C_BLOCK
        q1 = q0 + C_BLOCK
        s = jnp.einsum('bhqd,bhkd->bhqk', qh[:, :, q0:q1], kh[:, :, :q1]).astype(jnp.float32) * scale
        s = s + c[:, :, q0:q1, None] - c[:, :, None, :q1]
        mask = jnp.concatenate([jnp.ones((C_BLOCK, q0), dtype=bool), diag_mask], axis=1)
        s = jnp.where(mask[None, None], s, -jnp.inf)
        p = jax.nn.softmax(s, axis=-1)
        outs.append(jnp.einsum('bhqk,bhkd->bhqd', p.astype(vh.dtype), vh[:, :, :q1]))
    o = jnp.concatenate(outs, axis=2)
    return o.transpose(0, 2, 1, 3).reshape(bsz, seq, C_WIDTH)

def first_inputs(seed: int = 0) -> dict:
    key = jax.random.key(seed)
    ks = jax.random.split(key, 13)
    f32 = jnp.float32
    x = jax.random.normal(ks[0], (BATCH, SEQ, D_MODEL), f32)
    norm_g = 1.0 + 0.05 * jax.random.normal(ks[1], (DEPTH, D_MODEL), f32)
    w_in = jax.random.normal(ks[2], (DEPTH, D_MODEL, D_IN), f32) * D_MODEL ** -0.5
    w_out = jax.random.normal(ks[3], (DEPTH, D_MIX, D_MODEL), f32) * (D_MIX ** -0.5) * (2 * DEPTH) ** -0.5
    gmlp_ln_g = 1.0 + 0.05 * jax.random.normal(ks[4], (DEPTH, A_GROUPS, A_GROUP_DIM), f32)
    gmlp_ln_b = 0.02 * jax.random.normal(ks[5], (DEPTH, A_GROUPS, A_GROUP_DIM), f32)
    gmlp_w_s = jax.random.normal(ks[6], (DEPTH, A_GROUPS, A_CHUNK, A_CHUNK), f32) * A_CHUNK ** -0.5
    gmlp_b_s = 1.0 + 0.1 * jax.random.normal(ks[7], (DEPTH, A_GROUPS, A_CHUNK), f32)
    hgrn_lb = 0.1 * jax.random.normal(ks[8], (DEPTH, B_FDIM), f32)
    hgrn_onorm_g = 1.0 + 0.05 * jax.random.normal(ks[9], (DEPTH, B_VDIM), f32)
    fox_b_f = jax.random.uniform(ks[10], (DEPTH, C_HEADS), f32, 0.0, 3.0)
    final_norm_g = 1.0 + 0.05 * jax.random.normal(ks[11], (D_MODEL,), f32)
    return {"x": x, "norm_g": norm_g, "w_in": w_in, "w_out": w_out,
            "gmlp_ln_g": gmlp_ln_g, "gmlp_ln_b": gmlp_ln_b, "gmlp_w_s": gmlp_w_s,
            "gmlp_b_s": gmlp_b_s, "hgrn_lb": hgrn_lb, "hgrn_onorm_g": hgrn_onorm_g,
            "fox_b_f": fox_b_f, "final_norm_g": final_norm_g}

def first_block(x, norm_g, w_in, w_out, gmlp_ln_g, gmlp_ln_b, gmlp_w_s, gmlp_b_s,
              hgrn_lb, hgrn_onorm_g, fox_b_f, final_norm_g):
    p = jax.nn.softmax(hgrn_lb.astype(jnp.float32), axis=0)
    lb_all = jnp.clip(jnp.cumsum(p, axis=0) - p[0:1], 0.0, 1.0 - 1e-6)
    for layer in range(DEPTH):
        h = _rmsnorm(x, norm_g[layer])
        proj = jnp.einsum('bsd,de->bse', h, w_in[layer])
        (a_u, a_v, a_z, b_q, b_fl, b_i, b_z,
         c_q, c_k, c_v, c_z, c_fl) = _split_cols(proj)
        y_a = _gmlp_mixer(a_u, a_v, gmlp_ln_g[layer], gmlp_ln_b[layer],
                          gmlp_w_s[layer], gmlp_b_s[layer]) * jax.nn.silu(a_z)
        y_b = _hgrn2_mixer(b_q, b_fl, b_i, lb_all[layer], hgrn_onorm_g[layer]) * jax.nn.silu(b_z)
        y_c = _fox_mixer(c_q, c_k, c_v, c_fl, fox_b_f[layer]) * jax.nn.silu(c_z)
        y = jnp.concatenate([y_a, y_b, y_c], axis=-1)
        x = x + jnp.einsum('bse,ed->bsd', y, w_out[layer])
    return _rmsnorm(x, final_norm_g)


DEPTH_2 = 2

GRID_W = 64
BLOCK_Q = 128
EPS = 1e-6
N_BRANCH = 4

A_HEADS = 4
A_DH = 128
A_WIDTH_2 = A_HEADS * A_DH
A_CONV = 3
B_HEADS_2 = 8
B_KV = 2
B_DH = 64
B_WIDTH_2 = B_HEADS_2 * B_DH
ROPE_THETA = 10000.0
C_HEADS_2 = 8
C_DH = 64
C_WIDTH_2 = C_HEADS_2 * C_DH
C_WIN_R = 8
C_WIN_C = 16
D_HEADS = 4
D_DH = 64
D_DV = 2 * D_DH
D_WIDTH = D_HEADS * D_DV
D_FF = ((8 * D_MODEL + 3 * 256 - 1) // (3 * 256)) * 256

SPLIT_SIZES = (
    A_WIDTH_2, A_WIDTH_2, A_WIDTH_2, A_WIDTH_2, 4 * A_HEADS,
    B_WIDTH_2, B_KV * B_DH, B_KV * B_DH,
    C_WIDTH_2, C_WIDTH_2, C_WIDTH_2,
    2 * D_HEADS * D_DH, 2 * D_HEADS * D_DH, D_WIDTH,
    N_BRANCH * D_MODEL,
)
D_IN_2 = sum(SPLIT_SIZES)


F32 = jnp.float32

def rms_norm(x, g):
    xf = x.astype(F32)
    y = xf * lax.rsqrt(jnp.mean(xf * xf, axis=-1, keepdims=True) + EPS)
    return (y * g.astype(F32)).astype(x.dtype)

def centred_dwconv(x, w):
    k = w.shape[0]
    p = k // 2
    s = x.shape[1]
    xp = jnp.pad(x, ((0, 0), (p, p), (0, 0)))
    return sum(xp[:, j:j + s, :] * w[j] for j in range(k))

def sweep_query_blocks(fn, q):
    bsz, s = q.shape[:2]
    nb = s // BLOCK_Q
    qb = jnp.moveaxis(q.reshape((bsz, nb, BLOCK_Q) + q.shape[2:]), 1, 0)
    out = lax.map(lambda a: fn(a[0], a[1]), (jnp.arange(nb), qb))
    return jnp.moveaxis(out, 0, 1).reshape((bsz, s) + out.shape[3:])

def mlstm_scan(q, k, v, li, lf):
    bsz, nh, s, d = q.shape
    nc = s // A_CHUNK

    def chunks(t):
        t = t.reshape(t.shape[:2] + (nc, A_CHUNK) + t.shape[3:])
        return jnp.moveaxis(t, 2, 0)

    qc, kc, vc, lic = chunks(q), chunks(k), chunks(v), chunks(li)
    bc = jnp.cumsum(chunks(lf), axis=-1)
    lower = jnp.tril(jnp.ones((A_CHUNK, A_CHUNK), dtype=bool))

    def step(carry, xs):
        c_mat, n_vec, m = carry
        qt, kt, vt, it, bt = xs
        dmat = jnp.where(lower, bt[..., :, None] - bt[..., None, :] + it[..., None, :], -jnp.inf)
        inter = bt + m[..., None]
        mt = jnp.maximum(inter, dmat.max(-1))
        w_inter = jnp.exp(inter - mt)
        sqk = jnp.einsum('bhtd,bhsd->bhts', qt, kt) * jnp.exp(dmat - mt[..., None])
        num = (w_inter[..., None] * jnp.einsum('bhtk,bhkv->bhtv', qt, c_mat)
               + jnp.einsum('bhts,bhsv->bhtv', sqk, vt))
        den = w_inter * jnp.einsum('bhtk,bhk->bht', qt, n_vec) + sqk.sum(-1)
        ht = num / jnp.maximum(jnp.abs(den), jnp.exp(-mt))[..., None]
        bl = bt[..., -1]
        g = bl[..., None] - bt + it
        m_new = jnp.maximum(bl + m, g.max(-1))
        wc = jnp.exp(bl + m - m_new)
        ws = jnp.exp(g - m_new[..., None])
        c_new = wc[..., None, None] * c_mat + jnp.einsum('bhs,bhsk,bhsv->bhkv', ws, kt, vt)
        n_new = wc[..., None] * n_vec + jnp.einsum('bhs,bhsk->bhk', ws, kt)
        return (c_new, n_new, m_new), ht

    init = (jnp.zeros((bsz, nh, d, d), F32), jnp.zeros((bsz, nh, d), F32), jnp.zeros((bsz, nh), F32))
    _, h = lax.scan(step, init, (qc, kc, vc, lic, bc))
    return jnp.moveaxis(h, 0, 2).reshape(bsz, nh, s, d)

def mlstm_branch(q, k, v, o, gates, conv_w, gate_bias, norm_g):
    bsz, s, _ = q.shape
    dt = q.dtype
    qk = jax.nn.silu(centred_dwconv(jnp.concatenate([q, k], axis=-1), conv_w))
    q, k = jnp.split(qk, 2, axis=-1)

    def heads(t):
        return t.reshape(bsz, s, A_HEADS, A_DH).transpose(0, 2, 1, 3).astype(F32)

    qh, kh, vh = heads(q), heads(k) * (A_DH ** -0.5), heads(v)
    g = (gates.astype(F32) + gate_bias.astype(F32)).reshape(bsz, s, 4, A_HEADS).transpose(2, 0, 3, 1)
    i_fwd, f_fwd, i_bwd, f_bwd = g[0], g[1], g[2], g[3]
    h_fwd = mlstm_scan(qh, kh, vh, i_fwd, jax.nn.log_sigmoid(f_fwd))
    flip = lambda t: jnp.flip(t, axis=2)
    h_bwd = flip(mlstm_scan(flip(qh), flip(kh), flip(vh), flip(i_bwd), flip(jax.nn.log_sigmoid(f_bwd))))
    h = h_fwd + h_bwd
    mu = jnp.mean(h, axis=-1, keepdims=True)
    var = jnp.mean(jnp.square(h - mu), axis=-1, keepdims=True)
    h = (h - mu) * lax.rsqrt(var + EPS)
    h = h.transpose(0, 2, 1, 3).reshape(bsz, s, A_WIDTH_2) * norm_g.astype(F32)
    return (h * jax.nn.sigmoid(o.astype(F32))).astype(dt)

def axial_rope_angles(s):
    t = jnp.arange(s)
    row = (t // GRID_W).astype(F32)
    col = (t % GRID_W).astype(F32)
    n_freq = B_DH // 4
    inv = ROPE_THETA ** (-jnp.arange(n_freq, dtype=F32) / n_freq)
    return row[:, None] * inv, col[:, None] * inv

def rotate_half_rope(x, ang):
    x1, x2 = jnp.split(x, 2, axis=-1)
    c = jnp.cos(ang)[None, :, None, :]
    sn = jnp.sin(ang)[None, :, None, :]
    return jnp.concatenate([x1 * c - x2 * sn, x2 * c + x1 * sn], axis=-1)

def axial_rope(x, ang_r, ang_c):
    xr, xc = jnp.split(x, 2, axis=-1)
    return jnp.concatenate([rotate_half_rope(xr, ang_r), rotate_half_rope(xc, ang_c)], axis=-1)

def gqa_branch(q, k, v, qn_g, kn_g):
    bsz, s, _ = q.shape
    dt = q.dtype
    q = rms_norm(q.reshape(bsz, s, B_HEADS_2, B_DH), qn_g).astype(F32)
    k = rms_norm(k.reshape(bsz, s, B_KV, B_DH), kn_g).astype(F32)
    v = v.reshape(bsz, s, B_KV, B_DH).astype(F32)
    ang_r, ang_c = axial_rope_angles(s)
    q = axial_rope(q, ang_r, ang_c).reshape(bsz, s, B_KV, B_HEADS_2 // B_KV, B_DH) * (B_DH ** -0.5)
    k = axial_rope(k, ang_r, ang_c)

    def block(_, qb):
        sc = jnp.einsum('bqgrd,bkgd->bgrqk', qb, k)
        p = jax.nn.softmax(sc, axis=-1)
        return jnp.einsum('bgrqk,bkgd->bqgrd', p, v)

    o = sweep_query_blocks(block, q)
    return o.reshape(bsz, s, B_WIDTH_2).astype(dt)

def natten_indices(s):
    rows = s // GRID_W
    wr = min(C_WIN_R, rows)
    t = jnp.arange(s)
    r = t // GRID_W
    c = t % GRID_W
    rs = jnp.clip(r - wr // 2, 0, rows - wr)
    cs = jnp.clip(c - C_WIN_C // 2, 0, GRID_W - C_WIN_C)
    kr = rs[:, None, None] + jnp.arange(wr)[None, :, None]
    kc = cs[:, None, None] + jnp.arange(C_WIN_C)[None, None, :]
    shape = (s, wr, C_WIN_C)
    idx = jnp.broadcast_to(kr * GRID_W + kc, shape).reshape(s, wr * C_WIN_C)
    off_r = jnp.broadcast_to(kr - r[:, None, None] + (C_WIN_R - 1), shape).reshape(s, wr * C_WIN_C)
    off_c = jnp.broadcast_to(kc - c[:, None, None] + (C_WIN_C - 1), shape).reshape(s, wr * C_WIN_C)
    return idx, off_r, off_c

def natten_branch(q, k, v, rpb):
    bsz, s, _ = q.shape
    dt = q.dtype
    rows = s // GRID_W
    idx, off_r, off_c = natten_indices(s)
    nk = idx.shape[-1]
    bias = rpb.astype(F32)[:, off_r, off_c]
    q = q.reshape(bsz, rows, GRID_W, C_HEADS_2, C_DH).astype(F32) * (C_DH ** -0.5)
    k = k.reshape(bsz, s, C_HEADS_2, C_DH).astype(F32)
    v = v.reshape(bsz, s, C_HEADS_2, C_DH).astype(F32)
    idx_rows = idx.reshape(rows, GRID_W, nk)
    bias_rows = jnp.moveaxis(bias.reshape(C_HEADS_2, rows, GRID_W, nk), 1, 0)

    def row_block(args):
        qr, ir, br = args
        kg = jnp.take(k, ir, axis=1)
        vg = jnp.take(v, ir, axis=1)
        sc = jnp.einsum('bqhd,bqnhd->bhqn', qr, kg) + br[None]
        p = jax.nn.softmax(sc, axis=-1)
        return jnp.einsum('bhqn,bqnhd->bqhd', p, vg)

    o = lax.map(row_block, (jnp.moveaxis(q, 1, 0), idx_rows, bias_rows))
    return jnp.moveaxis(o, 0, 1).reshape(bsz, s, C_WIDTH_2).astype(dt)

def diff_branch(q, k, v, lq1, lk1, lq2, lk2, subln_g, lambda_init):
    bsz, s, _ = q.shape
    dt = q.dtype
    q = q.reshape(bsz, s, 2, D_HEADS, D_DH).astype(F32) * (D_DH ** -0.5)
    k = k.reshape(bsz, s, 2, D_HEADS, D_DH).astype(F32)
    v = v.reshape(bsz, s, D_HEADS, D_DV).astype(F32)
    lam = (jnp.exp(jnp.sum(lq1.astype(F32) * lk1.astype(F32)))
           - jnp.exp(jnp.sum(lq2.astype(F32) * lk2.astype(F32))) + lambda_init)
    slopes = 2.0 ** (-8.0 * jnp.arange(1, D_HEADS + 1, dtype=F32) / D_HEADS)
    kpos = jnp.arange(s, dtype=F32)

    def block(i, qb):
        qpos = (i * BLOCK_Q + jnp.arange(BLOCK_Q)).astype(F32)
        alibi = -slopes[:, None, None] * jnp.abs(qpos[:, None] - kpos[None, :])
        sc = jnp.einsum('bqchd,bkchd->bchqk', qb, k) + alibi[None, None]
        p = jax.nn.softmax(sc, axis=-1)
        a = p[:, 0] - lam * p[:, 1]
        return jnp.einsum('bhqk,bkhv->bqhv', a, v)

    o = sweep_query_blocks(block, q)
    o = rms_norm(o, subln_g) * (1.0 - lambda_init)
    return o.reshape(bsz, s, D_WIDTH).astype(dt)

def hybrid_layer(x, layer_idx, norm1_g, w_in, a_conv_w, a_gate_bias, a_norm_g, b_qnorm_g, b_knorm_g,
                 c_rpb, d_lq1, d_lk1, d_lq2, d_lk2, d_subln_g, w_up_a, w_up_b, w_up_c, w_up_d,
                 w_out, norm2_g, w_ffn_gate, w_ffn_up, w_ffn_down):
    bsz, s, _ = x.shape
    dt = x.dtype
    h = rms_norm(x, norm1_g)
    proj = jnp.einsum('bsd,de->bse', h, w_in)
    points = [sum(SPLIT_SIZES[:i + 1]) for i in range(len(SPLIT_SIZES) - 1)]
    (aq, ak, av, ao, ag, bq, bk, bv, cq, ck, cv, dq, dk, dv, gl) = jnp.split(proj, points, axis=-1)
    y_a = mlstm_branch(aq, ak, av, ao, ag, a_conv_w, a_gate_bias, a_norm_g)
    y_b = gqa_branch(bq, bk, bv, b_qnorm_g, b_knorm_g)
    y_c = natten_branch(cq, ck, cv, c_rpb)
    lambda_init = 0.8 - 0.6 * math.exp(-0.3 * layer_idx)
    y_d = diff_branch(dq, dk, dv, d_lq1, d_lk1, d_lq2, d_lk2, d_subln_g, lambda_init)
    g = jax.nn.sigmoid(gl.astype(F32)).reshape(bsz, s, N_BRANCH, D_MODEL)
    merged = (g[:, :, 0] * (y_a @ w_up_a) + g[:, :, 1] * (y_b @ w_up_b)
              + g[:, :, 2] * (y_c @ w_up_c) + g[:, :, 3] * (y_d @ w_up_d))
    x = x + merged.astype(dt) @ w_out
    h2 = rms_norm(x, norm2_g)
    ffn = (jax.nn.silu(h2 @ w_ffn_gate) * (h2 @ w_ffn_up)) @ w_ffn_down
    return x + ffn

def second_inputs(seed: int = 0) -> dict:
    key = jax.random.key(seed)
    ks = jax.random.split(key, 26)
    L = DEPTH_2
    nrm = lambda k, shape, scale: jax.random.normal(k, shape, F32) * scale
    gain = lambda k, shape: 1.0 + 0.02 * jax.random.normal(k, shape, F32)
    fb = jnp.linspace(3.0, 6.0, A_HEADS, dtype=F32)
    zh = jnp.zeros((A_HEADS,), F32)
    gate_offset = jnp.concatenate([zh, fb, zh, fb])
    return {
        "x": jax.random.normal(ks[0], (BATCH, SEQ, D_MODEL), F32),
        "norm1_g": gain(ks[1], (L, D_MODEL)),
        "w_in": nrm(ks[2], (L, D_MODEL, D_IN_2), D_MODEL ** -0.5),
        "a_conv_w": nrm(ks[3], (L, A_CONV, 2 * A_WIDTH_2), A_CONV ** -0.5),
        "a_gate_bias": gate_offset[None] + nrm(ks[4], (L, 4 * A_HEADS), 0.1),
        "a_norm_g": gain(ks[5], (L, A_WIDTH_2)),
        "b_qnorm_g": gain(ks[6], (L, B_DH)),
        "b_knorm_g": gain(ks[7], (L, B_DH)),
        "c_rpb": nrm(ks[8], (L, C_HEADS_2, 2 * C_WIN_R - 1, 2 * C_WIN_C - 1), 0.02),
        "d_lambda_q1": nrm(ks[9], (L, D_DH), 0.1),
        "d_lambda_k1": nrm(ks[10], (L, D_DH), 0.1),
        "d_lambda_q2": nrm(ks[11], (L, D_DH), 0.1),
        "d_lambda_k2": nrm(ks[12], (L, D_DH), 0.1),
        "d_subln_g": gain(ks[13], (L, D_DV)),
        "w_up_a": nrm(ks[14], (L, A_WIDTH_2, D_MODEL), A_WIDTH_2 ** -0.5),
        "w_up_b": nrm(ks[15], (L, B_WIDTH_2, D_MODEL), B_WIDTH_2 ** -0.5),
        "w_up_c": nrm(ks[16], (L, C_WIDTH_2, D_MODEL), C_WIDTH_2 ** -0.5),
        "w_up_d": nrm(ks[17], (L, D_WIDTH, D_MODEL), D_WIDTH ** -0.5),
        "w_out": nrm(ks[18], (L, D_MODEL, D_MODEL), D_MODEL ** -0.5),
        "norm2_g": gain(ks[19], (L, D_MODEL)),
        "w_ffn_gate": nrm(ks[20], (L, D_MODEL, D_FF), D_MODEL ** -0.5),
        "w_ffn_up": nrm(ks[21], (L, D_MODEL, D_FF), D_MODEL ** -0.5),
        "w_ffn_down": nrm(ks[22], (L, D_FF, D_MODEL), D_FF ** -0.5),
        "final_g": gain(ks[23], (D_MODEL,)),
    }

def second_block(x, norm1_g, w_in, a_conv_w, a_gate_bias, a_norm_g, b_qnorm_g, b_knorm_g, c_rpb,
              d_lambda_q1, d_lambda_k1, d_lambda_q2, d_lambda_k2, d_subln_g,
              w_up_a, w_up_b, w_up_c, w_up_d, w_out, norm2_g, w_ffn_gate, w_ffn_up, w_ffn_down, final_g):
    for l in range(DEPTH_2):
        x = hybrid_layer(x, l, norm1_g[l], w_in[l], a_conv_w[l], a_gate_bias[l], a_norm_g[l],
                         b_qnorm_g[l], b_knorm_g[l], c_rpb[l],
                         d_lambda_q1[l], d_lambda_k1[l], d_lambda_q2[l], d_lambda_k2[l], d_subln_g[l],
                         w_up_a[l], w_up_b[l], w_up_c[l], w_up_d[l], w_out[l],
                         norm2_g[l], w_ffn_gate[l], w_ffn_up[l], w_ffn_down[l])
    return rms_norm(x, final_g)


def setup_inputs(seed=0):
    out = dict(first_inputs(seed))
    for name, value in second_inputs(seed + 1).items():
        if name != "x":
            out[name + "_2"] = value
    return out


def reference(
    x, norm_g, w_in, w_out, gmlp_ln_g, gmlp_ln_b, gmlp_w_s, gmlp_b_s, hgrn_lb, hgrn_onorm_g,
    fox_b_f, final_norm_g, norm1_g_2, w_in_2, a_conv_w_2, a_gate_bias_2, a_norm_g_2,
    b_qnorm_g_2, b_knorm_g_2, c_rpb_2, d_lambda_q1_2, d_lambda_k1_2, d_lambda_q2_2,
    d_lambda_k2_2, d_subln_g_2, w_up_a_2, w_up_b_2, w_up_c_2, w_up_d_2, w_out_2, norm2_g_2,
    w_ffn_gate_2, w_ffn_up_2, w_ffn_down_2, final_g_2,
):
    x = first_block(
        x, norm_g, w_in, w_out, gmlp_ln_g, gmlp_ln_b, gmlp_w_s, gmlp_b_s, hgrn_lb, hgrn_onorm_g,
        fox_b_f, final_norm_g,
    )
    return second_block(
        x, norm1_g_2, w_in_2, a_conv_w_2, a_gate_bias_2, a_norm_g_2, b_qnorm_g_2, b_knorm_g_2,
        c_rpb_2, d_lambda_q1_2, d_lambda_k1_2, d_lambda_q2_2, d_lambda_k2_2, d_subln_g_2,
        w_up_a_2, w_up_b_2, w_up_c_2, w_up_d_2, w_out_2, norm2_g_2, w_ffn_gate_2, w_ffn_up_2,
        w_ffn_down_2, final_g_2,
    )


_drawn_inputs = setup_inputs


def setup_inputs(seed=0):
    import zlib

    import numpy as np

    out = dict(_drawn_inputs(seed))
    spreads = {}
    factors = {'gmlp_ln_g': 8.0,
     'gmlp_ln_b': 8.0,
     'gmlp_b_s': 2.868,
     'hgrn_onorm_g': 3.458,
     'a_norm_g_2': 6.76,
     'b_qnorm_g_2': 8.0,
     'b_knorm_g_2': 8.0,
     'c_rpb_2': 51.767,
     'd_lambda_k1_2': 3.116,
     'd_subln_g_2': 4.403,
     'norm2_g_2': 2.961,
     'final_g_2': 8.186}
    for name, (base, spread) in spreads.items():
        noise = np.random.default_rng([zlib.crc32(name.encode()), seed]).standard_normal(out[name].shape)
        drawn = base * np.exp(spread * noise) if base else spread * noise
        out[name] = jnp.asarray(drawn.astype(out[name].dtype))
    for name, factor in factors.items():
        out[name] = (out[name] * factor).astype(out[name].dtype)
    return out
```

```python
from contextlib import ExitStack

import numpy as np

import concourse.bass as bass
from concourse import mybir

F32 = mybir.dt.float32
F32R = mybir.dt.float32r
U32 = mybir.dt.uint32
ACT = mybir.ActivationFunctionType
ALU = mybir.AluOpType
AX = mybir.AxisListType.X

P = 128
SEQ = 512
NT = SEQ // P
D = 1024
KD = D // P
DEPTH = 2
EPS = 1e-6
BIG = 1e30

W1_COLS = 3848
W2_COLS = 10000
D_FF = 2816
DH = 64
SCALE = DH ** -0.5
HEADS = 8
GELU_C = 0.7978845608028654
GELU_A = 0.044715
CHUNK = 128
LEVELS = 7

RAW_SLOTS = 3
W_SLOTS = 2
LOOK = 1
TABW = 896
RPB_PAD = 64
RPB_HEAD = 15 * 31
RPB_LEN = HEADS * RPB_HEAD
GATE_ROWS = 36


class Block:

    def __init__(self, name, weight, row0, kchunks, col0, cols, orient, src="h", gates=False):
        self.name, self.weight, self.row0, self.kchunks = name, weight, row0, kchunks
        self.col0, self.cols, self.orient, self.src, self.gates = col0, cols, orient, src, gates
        if gates:
            self.banks, self.units = 1, [(0, kchunks)]
        else:
            self.banks = NT if orient == "tok" else cols // P
            self.units = [(k, 2) for k in range(0, kchunks, 2)]


def block1_dense():
    w, o = "w_in", "w_out"
    return {
        "FL": Block("FL", w, 0, KD, 3840, 8, "feat", gates=True),
        "BF": Block("BF", w, 0, KD, 768, 512, "feat"),
        "BI": Block("BI", w, 0, KD, 1280, 512, "tok"),
        "UV": Block("UV", w, 0, KD, 0, 512, "tok"),
        "AZ": Block("AZ", w, 0, KD, 512, 256, "tok"),
        "CQ": Block("CQ", w, 0, KD, 1792, 512, "feat"),
        "CK": Block("CK", w, 0, KD, 2304, 512, "feat"),
        "CV": Block("CV", w, 0, KD, 2816, 512, "tok"),
        "CZ": Block("CZ", w, 0, KD, 3328, 512, "tok"),
        "O0": Block("O0", o, 0, KD, 0, 512, "tok"),
        "O1": Block("O1", o, 0, KD, 512, 512, "tok"),
    }


FFN_COLS = [512] * 5 + [256]
COL2 = dict(AQ=0, AK=512, AV=1024, AO=1536, AG=2048, BQ=2064, BKV=2576, CQ=2832, CK=3344,
            CV=3856, DQ=4368, DK=4880, DV=5392, GL=5904)


def block2_dense(l):
    w = f"w_in_2:{l}"
    out = {n: Block(n, w, 0, KD, COL2[n], 512, "feat" if n in ("AQ", "AK", "CQ", "CK", "DQ", "DK") else "tok")
           for n in ("AQ", "AK", "AV", "AO", "BQ", "CQ", "CK", "CV", "DQ", "DK", "DV")}
    out["AG"] = Block("AG", w, 0, KD, COL2["AG"], 16, "feat", gates=True)
    out["BKV"] = Block("BKV", w, 0, KD, COL2["BKV"], 256, "tok")
    for b in range(4):
        for half in range(2):
            out[f"G{b}{half}"] = Block(f"G{b}{half}", w, 0, KD, COL2["GL"] + 1024 * b + 512 * half, 512, "tok")
            out[f"U{b}{half}"] = Block(f"U{b}{half}", f"w_up_{'abcd'[b]}_2:{l}", 0, 4, 512 * half, 512, "tok", "y")
    for half in range(2):
        out[f"O{half}"] = Block(f"O{half}", f"w_out_2:{l}", 0, KD, 512 * half, 512, "tok")
    for f, n in enumerate(FFN_COLS):
        out[f"FG{f}"] = Block(f"FG{f}", f"w_ffn_gate_2:{l}", 0, KD, 512 * f, n, "feat")
        out[f"FU{f}"] = Block(f"FU{f}", f"w_ffn_up_2:{l}", 0, KD, 512 * f, n, "feat")
        for half in range(2):
            out[f"FD{f}{half}"] = Block(f"FD{f}{half}", f"w_ffn_down_2:{l}", 512 * f, n // P, 512 * half, 512,
                                        "tok", "y")
    return out


ORDER1 = ["FL", "BF", "BI", "UV", "AZ", "CQ", "CK", "CV", "CZ", "O0", "O1"]


def ffn_order():
    order = ["FG0", "FU0"]
    for f in range(1, len(FFN_COLS)):
        order += [f"FG{f}", f"FD{f-1}0", f"FD{f-1}1", f"FU{f}"]
    last = len(FFN_COLS) - 1
    return order + [f"FD{last}0", f"FD{last}1"]


ORDER2 = (["BQ", "BKV", "AG", "AQ", "AK", "AV", "G00", "G01", "CQ", "CK", "CV", "AO", "U00", "U01",
           "G10", "G11", "DQ", "DK", "DV", "U10", "U11", "G20", "G21", "U20", "U21", "G30", "G31",
           "U30", "U31", "O0", "O1"] + ffn_order())


def dense_plan():
    blocks = [block1_dense()[n] for n in ORDER1]
    for l in range(DEPTH):
        named = block2_dense(l)
        blocks += [named[n] for n in ORDER2]
    units, groups = [], 0
    used = [0] * NT
    for b in blocks:
        b.first_unit = len(units)
        b.nth = list(used)
        for k0, kn in b.units:
            groups += b.banks
            units.append((b, k0, kn, groups))
        b.groups_end = groups
        for j in range(b.banks):
            used[j] += 1
    return blocks, units


class Count:

    def __init__(self):
        self.seen = {}

    def __call__(self, name, more=1):
        self.seen[name] = self.seen.get(name, 0) + more
        return self.seen[name]

    def at(self, name):
        return self.seen.get(name, 0)


def fox_items():
    return [dict(kind="fox", h=h, t=t, comp=0, kmax=(t + 1) * P, head=h, q=(h // 2, h % 2), k=(h // 2, h % 2),
                 v=(h * DH, DH), y=h * DH) for h in range(HEADS) for t in range(NT)]


def gqa_items():
    return [dict(kind="gqa", h=h, t=t, comp=0, kmax=SEQ, head=h, q=(h // 2, h % 2), k=(h // 4, h % 2),
                 v=((h // 4) * DH, DH), y=h * DH) for h in range(HEADS) for t in range(NT)]


def nat_items():
    return [dict(kind="nat", h=h, t=t, comp=0, kmax=SEQ, head=h, q=(h // 2, h % 2), k=(h // 2, h % 2),
                 v=(h * DH, DH), y=h * DH) for h in range(HEADS) for t in range(NT)]


def diff_items():
    return [dict(kind="diff", h=h, t=t, comp=c, kmax=SEQ, head=h, q=((4 * c + h) // 2, h % 2),
                 k=((4 * c + h) // 2, h % 2), v=(h * P, P), y=h * P)
            for h in range(4) for t in range(NT) for c in range(2)]


def lambda_init(l):
    return 0.8 - 0.6 * float(np.exp(-0.3 * l))


def build(nc, a, out):
    blocks, units = dense_plan()
    by_name = {}
    for i, b in enumerate(blocks):
        l = 0 if i < len(ORDER1) else 1 + (i - len(ORDER1)) // len(ORDER2)
        by_name[(l, b.name)] = b

    ctx = ExitStack()
    with ctx:
        def sb(name, shape, dt=F32):
            return ctx.enter_context(nc.sbuf_tensor(name, shape, dt))

        x = sb("x", [P, NT, D])
        merged = sb("merged", [P, NT, D])
        hH = sb("hH", [P, KD, SEQ], F32R)
        hL = sb("hL", [P, KD, SEQ], F32R)
        yH = sb("yH", [P, 4, SEQ], F32R)
        yL = sb("yL", [P, 4, SEQ], F32R)
        wraw = sb("wraw", [P, RAW_SLOTS, 2 * SEQ])
        wH = sb("wH", [P, W_SLOTS, 2 * SEQ], F32R)
        wL = sb("wL", [P, W_SLOTS, 2 * SEQ], F32R)
        set1 = sb("set1", [P, 6160])
        set2 = sb("set2", [P, 6144])
        gbuf = sb("gbuf", [P, NT, D])
        ytok = sb("ytok", [P, NT, SEQ])
        tab = sb("tab", [P, 2, TABW])
        sbufS = sb("sbufS", [P, 2, SEQ])
        sbufPT = sb("sbufPT", [P, 2, SEQ])
        ident = sb("ident", [P, P])
        causal = sb("causal", [P, P])
        anti = sb("anti", [P, P])
        nat_mask = sb("nat_mask", [P, DH])
        rope = sb("rope", [P, 2, NT, DH])
        small = sb("small", [P, 900])

        at = [0]

        def cols(n):
            at[0] += n
            assert at[0] <= 900
            return small[:, at[0] - n:at[0]]

        g_norm = [cols(KD) for _ in range(1 + 2 * DEPTH)]
        g_conv = [cols(24) for _ in range(DEPTH)]
        g_bias = [cols(2) for _ in range(DEPTH)]
        g_anorm = [cols(4) for _ in range(DEPTH)]
        g_sub = [cols(1) for _ in range(DEPTH)]
        g_q = [cols(DH) for _ in range(DEPTH)]
        g_k = [cols(DH) for _ in range(DEPTH)]
        lam = [cols(1) for _ in range(DEPTH)]
        lam_tmp = cols(4)
        lbt = cols(2)
        lb = cols(2)
        oml = cols(2)
        bf_col = cols(1)
        bs_t = cols(4)
        ss = cols(NT)
        rstd = cols(NT)
        mx = cols(4)
        nm = cols(4)
        lsum = cols(4)
        rs = cols(4)
        onorm = cols(DH)
        st32 = cols(32)
        st32b = cols(32)
        st32c = cols(32)
        wcol = cols(NT * 8)
        mcol = cols(NT * 8)
        hden = cols(4)
        one_col = cols(1)
        st40 = cols(40)
        ebl = cols(8)

        def view(t, off, shape):
            n = int(np.prod(shape))
            v = t[:, off:off + n]
            if len(shape) == 1:
                return v
            names = "abcd"[:len(shape)]
            kw = {names[i]: shape[i] for i in range(len(shape))}
            return v.rearrange("p (" + " ".join(names) + ") -> p " + " ".join(names), **kw)

        xn = merged
        gflat = gbuf[:, :, :].rearrange("p t d -> p (t d)")
        yflat = ytok[:, :, :].rearrange("p t d -> p (t d)")
        tflat = tab[:, :, :].rearrange("p t d -> p (t d)")
        sflat = sbufS[:, :, :].rearrange("p t d -> p (t d)")
        ptflat = sbufPT[:, :, :].rearrange("p t d -> p (t d)")
        mflat = merged[:, :, :].rearrange("p t d -> p (t d)")
        q1, k1, v1 = view(set1, 0, (4, SEQ)), view(set1, 2048, (4, SEQ)), view(set1, 4096, (NT, SEQ))
        v1a = view(set1, 4096, (NT, 4, P + 1))
        q2, k2, v2 = view(set2, 0, (4, SEQ)), view(set2, 2048, (4, SEQ)), view(set2, 4096, (NT, SEQ))
        k2b = view(set2, 2048, (2, SEQ))
        v2b = view(set2, 3072, (NT, P))
        qraw = view(gflat, 0, (NT, SEQ))
        kraw = view(gflat, 2048, (NT, P))
        qs, ks, bb = view(set1, 0, (2, SEQ)), view(set1, 1024, (2, SEQ)), view(set1, 2048, (2, SEQ))
        vi, uu, vv = view(set1, 3072, (NT, 256)), view(set1, 4096, (NT, 256)), view(set1, 5120, (NT, 256))
        ssc = view(yflat, 0, (4, NT, P))

        bank = [ctx.enter_context(nc.psum_tensor(f"bank{i}", [P, SEQ], F32)) for i in range(8)]
        SC, TP, PV = 4, 6, 7

        qlev = [view(gflat, 2048 * i, (2, SEQ)) for i in range(2)]
        klev = [view(gflat, 2048 * i + 1024, (2, SEQ)) for i in range(2)]
        qe, ke = view(gflat, 0, (2, SEQ)), view(gflat, 1024, (2, SEQ))
        keT = view(gflat, 2048, (3, 2, P))
        states = view(gflat, 2816, (3, 2, DH))
        fox_c = tflat[:, 1024:1536]
        row_i, row_f, row_w, row_m = (yflat[0:GATE_ROWS, 512 * i:512 * i + 512] for i in range(4))
        row_b = gflat[0:GATE_ROWS, 2560:3072]
        row_nm = tflat[0:GATE_ROWS, 1024:1536]
        cq_t, sq_t, ck_t, sk_t = (view(tflat, 256 * i, (NT, DH)) for i in range(4))
        rope_c, rope_s = gflat[:, 3072:3584], gflat[:, 3584:4096]
        pmat = view(mflat, 0, (2, 4, SEQ))

        names = """
            consts landed0 landed1 landed2 w_hi w_lo groups free0 free1 free2 free3
            act_step dve_step gp_step
            norm_sq norm_ms norm_sd xn_ready tp_done tp_hi tp_free x_ready x_done
            sc_done mx_done ex_done pt_done ptev pv_done y_done
            tab_dma0 tab_dma1 mb_done e_done qk_done p_done o_done hh_done
            sq_ready ms_ready sd_ready conv_tanh qk_ready row_abs row_log rows_ready rowt_done rowt_read mcol_ready
            tanh_ready silu_out ropeq_ready y_ready hid_prod hid_hi hid_ready
            z_ready ez_ready ln_ready lb_ready d_ready ed_ready lvl_ready lvl_done lvl_used
            ke_ready keT_done keT_read upd_done st_ready ho_done ho_read late gin gsq gin2 sq_taken
            vn_ready mix_done lam_dot lam_exp out_done
        """.split()
        S = {n: ctx.enter_context(nc.semaphore(n)) for n in names}
        landed = [S["landed0"], S["landed1"], S["landed2"]]
        free = [S[f"free{j}"] for j in range(4)]

        block = ctx.enter_context(nc.Block())

        def wsrc(b, k0, kn):
            name, _, l = b.weight.partition(":")
            w = a[name]
            w = w[int(l) if l else 0]
            return w[b.row0 + k0 * P:b.row0 + (k0 + kn) * P, b.col0:b.col0 + b.cols].rearrange(
                "(k p) n -> p k n", p=P)

        def raw_view(u):
            b, k0, kn, _ = units[u]
            return wraw[:, u % RAW_SLOTS, 0:kn * b.cols].rearrange("p (k n) -> p k n", k=kn)

        def w_views(u):
            b, k0, kn, _ = units[u]
            width = P if b.gates else b.cols
            return [w[:, u % W_SLOTS, 0:kn * width].rearrange("p (k n) -> p k n", k=kn) for w in (wH, wL)]

        def gate_parts(u):
            b = units[u][0]
            if b.cols == 8:
                return [(0, 8, 0)]
            return [(0, 4, 0), (64, 4, 4), (32, 4, 8), (96, 4, 12)]

        def bcast_rows(name_ap, n):
            return bass.AP(tensor=name_ap.tensor, offset=name_ap.offset, ap=[[0, P], [1, n]])

        def small_loads():
            out = [(ident[:, :], a["ident"]), (causal[:, :], a["causal"]), (anti[:, :], a["anti"]),
                   (nat_mask[:, :], a["nat_mask"]), (rope[:, :, :, :], a["rope"]),
                   (g_norm[0], a["norm_gT"]), (lbt, a["lbT"]), (bf_col[0:8, :], a["fox_bT"]), (bs_t, a["bsT"])]
            out.append((onorm, bcast_rows(a["hgrn_onorm_g"][0], DH)))
            for l in range(DEPTH):
                out += [(g_norm[1 + 2 * l], a["norm1_gT"][l]), (g_norm[2 + 2 * l], a["norm2_gT"][l]),
                        (g_conv[l], a["convT"][l]), (g_bias[l][0:GATE_ROWS, :], a["gate_biasT"][l]),
                        (g_anorm[l], a["a_normT"][l]), (g_sub[l], a["sublnT"][l]),
                        (g_q[l], bcast_rows(a["b_qnorm_g_2"][l], DH)), (g_k[l], bcast_rows(a["b_knorm_g_2"][l], DH))]
                for i, n in enumerate(("d_lambda_q1_2", "d_lambda_k1_2", "d_lambda_q2_2", "d_lambda_k2_2")):
                    out.append((gflat[:, (4 * l + i) * DH:(4 * l + i + 1) * DH], bcast_rows(a[n][l], DH)))
            out.append((view(tflat, 0, (LEVELS + 1, P)), a["level_masks"]))
            return out

        loads = small_loads()
        CONSTS = 16 * (NT + len(loads))

        @block.sync
        def _(sp):
            n = Count()
            for t in range(NT):
                sp.dma_start(x[:, t, :], a["x"][0, t * P:(t + 1) * P, :]).then_inc(S["consts"], 16)

            def weight(u):
                b, k0, kn, _ = units[u]
                if u >= RAW_SLOTS:
                    sp.wait_ge(S["w_lo"], u - RAW_SLOTS + 1)
                sp.dma_start(raw_view(u), wsrc(b, k0, kn)).then_inc(landed[u % RAW_SLOTS], 16)

            for u in range(RAW_SLOTS):
                weight(u)
            for dst, src in loads:
                sp.dma_start(dst, src).then_inc(S["consts"], 16)
            for u in range(RAW_SLOTS, len(units)):
                weight(u)
            sp.wait_ge(S["x_done"], NT)
            for t in range(NT):
                sp.dma_start(out[0, t * P:(t + 1) * P, :], x[:, t, :]).then_inc(S["out_done"], 16)
            sp.wait_ge(S["out_done"], 16 * NT)

        @block.gpsimd
        def _(pool):
            pool.wait_ge(S["late"], 1)
            pool.dma_start(view(gflat, 0, (4, P)), a["w_sT"]).then_inc(S["gp_step"], 16)
            for i, name in enumerate(("gmlp_ln_g", "gmlp_ln_b")):
                pool.dma_start(gflat[:, 512 + 256 * i:768 + 256 * i], bcast_rows(a[name][0], 256)).then_inc(
                    S["gp_step"], 16)
            pool.dma_start(view(gflat, 1024, (4, P)), a["keep4"]).then_inc(S["gp_step"], 16)
            pool.dma_start(yflat[:, 0:D], bcast_rows(a["final_norm_g"], D)).then_inc(S["gp_step"], 16)
            for l in range(DEPTH):
                gqa0 = 32 + 96 * l
                nat0, diff0 = gqa0 + 32, gqa0 + 64
                for h in range(HEADS):
                    pool.wait_ge(S["mx_done"], gqa0 + 1 if h < 2 else nat0 + 4 * (h - 1))
                    for half in range(2):
                        off = l * (RPB_LEN + 2 * RPB_PAD) + RPB_PAD + RPB_LEN - 1 - RPB_HEAD * h - (14 - half) * 31 - 78
                        src = bass.AP(tensor=a["rpb_rev"].tensor, offset=off, ap=[[1, 64], [31, 14], [1, 64]])
                        pool.dma_start(tab[64 * half:64 * half + 64, h % 2, :].rearrange("p (e k) -> p e k", e=14),
                                       src).then_inc(S[f"tab_dma{h % 2}"], 16)
                for h in range(4):
                    pool.wait_ge(S["mx_done"], nat0 + 28 + 4 * h if h < 2 else diff0 + 8 * (h - 1))
                    pool.dma_start(tab[:, h % 2, :], a["alibi"][h]).then_inc(S[f"tab_dma{h % 2}"], 16)
            pool.wait_ge(S["late"], 2)
            pool.dma_start(yflat[:, 0:D], bcast_rows(a["final_g_2"], D)).then_inc(S["gp_step"], 16)

        @block.tensor
        def _(pe):
            n = Count()
            unit = [0]

            def group(b, i, t):
                u = b.first_unit + i
                _, k0, kn, _ = units[u]
                if t == 0:
                    pe.wait_ge(S["w_lo"], u + 1)
                if i == 0 and b.nth[t]:
                    pe.wait_ge(free[t], b.nth[t])
                H, L = (hH, hL) if b.src == "h" else (yH, yL)
                vh, vl = w_views(u)
                for kk in range(kn):
                    k = k0 + kk
                    for j in range(3):
                        act_part = (H, L, H)[j]
                        w_part = (vh, vh, vl)[j]
                        first = i == 0 and kk == 0 and j == 0
                        last = i == len(b.units) - 1 and kk == kn - 1 and j == 2
                        if b.orient == "tok":
                            mm = pe.matmul(bank[t][:, 0:b.cols], act_part[:, k, t * P:(t + 1) * P], w_part[:, kk, :],
                                           start=first, stop=last)
                        else:
                            mm = pe.matmul(bank[t][:, :], w_part[:, kk, t * P:(t + 1) * P], act_part[:, k, :],
                                           start=first, stop=last)
                mm.then_inc(S["groups"], 1)

            def dense(l, name):
                b = by_name[(l, name)]
                for i in range(len(b.units)):
                    for t in range(b.banks):
                        group(b, i, t)

            def transposes(src, chunks, ready, count):
                if ready:
                    pe.wait_ge(S[ready], n(ready, count))
                for k in range(chunks):
                    i = n("tp") - 1
                    if i >= 2:
                        pe.wait_ge(S["tp_free"], i - 1)
                    for t in range(NT):
                        mm = pe.transpose(bank[SC + i % 2][:, t * P:(t + 1) * P], src[:, t, k * P:(k + 1) * P],
                                          ident[:, :])
                    mm.then_inc(S["tp_done"], 1)

            def h_ready():
                pe.wait_ge(S["tp_free"], n.at("tp"))

            def softmax(items, q, k, v, beside):
                i0 = n("items", len(items)) - len(items)
                side = [(b, i, t) for b in beside for i in range(len(b.units)) for t in range(NT)]
                pe.wait_ge(S["tp_free"], n.at("tp"))
                for s in range(max(len(items) + 2, len(side))):
                    if s < len(items):
                        it, i = items[s], i0 + s
                        if i >= 2:
                            pe.wait_ge(S["ex_done"], i - 1)
                        r = slice(DH * it["q"][1], DH * it["q"][1] + DH)
                        kmax, dst = it["kmax"], bank[SC + i % 2]
                        fox = it["kind"] == "fox"
                        mm = pe.matmul(dst[:, 0:kmax], q[r, it["q"][0], it["t"] * P:(it["t"] + 1) * P],
                                       k[r, it["k"][0], 0:kmax], start=True, stop=not fox)
                        if fox:
                            pe.matmul(dst[:, 0:kmax], ident[0:8, it["h"]:it["h"] + 1].to_broadcast([8, P]),
                                      fox_c[0:8, 0:kmax], start=False, stop=True)
                            mm = pe.matmul(dst[:, kmax - P:kmax], ident[:, :], causal[:, :], start=False, stop=True,
                                           skip_group_check=True)
                        mm.then_inc(S["sc_done"], 1)
                    if s < len(side):
                        group(*side[s])
                    if 1 <= s <= len(items):
                        it, i = items[s - 1], i0 + s - 1
                        pe.wait_ge(S["ex_done"], i + 1)
                        if i >= 1:
                            pe.wait_ge(S["ptev"], i)
                        for c in range(it["kmax"] // P):
                            mm = pe.transpose(bank[TP][:, c * P:(c + 1) * P], sbufS[:, i % 2, c * P:(c + 1) * P],
                                              ident[:, :])
                        mm.then_inc(S["pt_done"], 1)
                    if 2 <= s < len(items) + 2:
                        it, i = items[s - 2], i0 + s - 2
                        pe.wait_ge(S["ptev"], i + 1)
                        if i >= 1:
                            pe.wait_ge(S["y_done"], i)
                        nk = it["kmax"] // P
                        c0, w = it["v"]
                        for c in range(nk):
                            mm = pe.matmul(bank[PV][:, 0:w], sbufPT[:, i % 2, c * P:(c + 1) * P],
                                           v[:, c, c0:c0 + w], start=c == 0, stop=c == nk - 1)
                        mm.then_inc(S["pv_done"], 1)

            def evacuated(b):
                for j in range(b.banks):
                    pe.wait_ge(free[j], b.nth[j] + 1)

            def mlstm(l, beside):
                side = [(b, i, t) for b in beside for i in range(4) for t in range(NT)]
                i0 = 32 * l
                for s in range(36):
                    c, j = s // 4, s % 4
                    if c < 8:
                        i, h, back = i0 + s, c // 2, c % 2
                        lo, hi = (0, (j + 1) * P) if back else (j * P, SEQ)
                        row = 32 * back + h
                        if i >= 1:
                            pe.wait_ge(S["e_done"], i)
                        pe.matmul(bank[TP][:, lo:hi], ident[0:GATE_ROWS, row:row + 1].to_broadcast([GATE_ROWS, P]),
                                  row_nm[:, lo:hi], start=True, stop=True)
                        pe.matmul(bank[TP][:, j * P:(j + 1) * P], ident[:, :], (causal if back else anti)[:, :],
                                  start=False, stop=True, skip_group_check=True).then_inc(S["mb_done"], 1)
                        if i >= 2:
                            pe.wait_ge(S["p_done"], i - 1)
                        pe.matmul(bank[SC + i % 2][:, lo:hi], k1[:, h, j * P:(j + 1) * P], q1[:, h, lo:hi],
                                  start=True, stop=True).then_inc(S["qk_done"], 1)
                    if s < len(side):
                        group(*side[s])
                    if c >= 1:
                        i, h, back = i0 + s - 4, (c - 1) // 2, (c - 1) % 2
                        pe.wait_ge(S["p_done"], i0 + 4 * c)
                        if i >= 1:
                            pe.wait_ge(S["hh_done"], i)
                        srcs = range(j, NT) if back else range(j + 1)
                        for sj in srcs:
                            mm = pe.matmul(bank[PV][:, 0:P + 1], pmat[:, (c - 1) % 2, sj, j * P:(j + 1) * P],
                                           v1a[:, sj, h, :], start=sj == srcs[0], stop=sj == srcs[-1])
                        mm.then_inc(S["o_done"], 1)

            def hgrn():
                for lev in range(LEVELS + 1):
                    pe.wait_ge(S["lvl_ready"], lev + 1)
                    ql, kl = (qlev[lev % 2], klev[lev % 2]) if lev < LEVELS else (qs, ks)
                    for h in range(4):
                        c = 4 * lev + h
                        if c >= 2:
                            pe.wait_ge(S["lvl_used"], c - 1)
                        r = slice(DH * (h % 2), DH * (h % 2) + DH)
                        for m in range(NT):
                            tok = slice(m * P, (m + 1) * P)
                            mm = pe.matmul(bank[SC + c % 2][:, tok], kl[r, h // 2, tok], ql[r, h // 2, tok],
                                           start=True, stop=True)
                        mm.then_inc(S["lvl_done"], 1)
                pe.wait_ge(S["ke_ready"], 1)
                for m in range(3):
                    for g in range(2):
                        mm = pe.transpose(bank[TP + m // 2][:, (2 * (m % 2) + g) * P:(2 * (m % 2) + g + 1) * P],
                                          ke[:, g, m * P:(m + 1) * P], ident[:, :])
                    mm.then_inc(S["keT_done"], 1)
                pe.wait_ge(S["keT_read"], 2)
                pe.wait_ge(S["lvl_used"], 4 * (LEVELS + 1))
                for m in range(3):
                    for g in range(2):
                        mm = pe.matmul(bank[SC + m // 2][:, (2 * (m % 2) + g) * P:(2 * (m % 2) + g + 1) * P],
                                       keT[:, m, g, :], vi[:, m, g * P:(g + 1) * P], start=True, stop=True)
                    mm.then_inc(S["upd_done"], 1)
                pe.wait_ge(S["st_ready"], 1)
                for m in range(NT):
                    if m:
                        pe.wait_ge(S["ho_read"], 2 * m)
                    tok = slice(m * P, (m + 1) * P)
                    for h in range(4):
                        r = slice(DH * (h % 2), DH * (h % 2) + DH)
                        dst = bank[TP + h % 2][:, (h // 2) * DH:(h // 2 + 1) * DH]
                        mm = pe.matmul(dst, ssc[:, h, m, :], vi[:, m, h * DH:(h + 1) * DH], start=True, stop=m == 0)
                        if m:
                            mm = pe.matmul(dst, qe[r, h // 2, tok], states[r, m - 1, h // 2, :],
                                           start=False, stop=True)
                    mm.then_inc(S["ho_done"], 1)

            def gmlp():
                pe.wait_ge(S["vn_ready"], 1)
                for g in range(4):
                    mm = pe.matmul(bank[TP + g // 2][:, (g % 2) * 256:(g % 2) * 256 + 256],
                                   gflat[:, g * P:(g + 1) * P], vv[:, :, g * DH:(g + 1) * DH], start=True, stop=True)
                    mm.then_inc(S["mix_done"], 1)

            pe.wait_ge(S["consts"], CONSTS)
            transposes(xn, KD, "xn_ready", NT)
            h_ready()
            for name in ORDER1[:9]:
                dense(0, name)
            hgrn()
            gmlp()
            for name in ("CQ", "CK", "CV"):
                evacuated(by_name[(0, name)])
            pe.wait_ge(S["mix_done"], 4)
            softmax(fox_items(), q2, k2, v2, [])
            pe.wait_ge(S["y_done"], n.at("items"))
            transposes(merged, KD, None, 0)
            h_ready()
            dense(0, "O0")
            dense(0, "O1")

            for l in range(DEPTH):
                L = l + 1

                def B(*names):
                    return [by_name[(L, name)] for name in names]

                transposes(xn, KD, "xn_ready", NT)
                h_ready()
                dense(L, "BQ")
                dense(L, "BKV")
                dense(L, "AG")
                dense(L, "AQ")
                pe.wait_ge(S["rows_ready"], l + 1)
                for t in range(NT):
                    for w, row in enumerate((row_w, row_m)):
                        mm = pe.transpose(bank[TP][:, (2 * t + w) * GATE_ROWS:(2 * t + w + 1) * GATE_ROWS],
                                          row[:, t * P:(t + 1) * P], ident[0:GATE_ROWS, 0:GATE_ROWS])
                mm.then_inc(S["rowt_done"], 1)
                dense(L, "AK")
                transposes(qraw, 4, "ropeq_ready", NT)
                transposes(kraw, 1, None, 0)
                dense(L, "AV")
                evacuated(B("AV")[0])
                pe.wait_ge(S["tp_free"], n.at("tp"))
                pe.wait_ge(S["qk_ready"], 9 * (l + 1))
                pe.wait_ge(S["rowt_read"], l + 1)
                mlstm(l, B("G00", "G01"))
                for name in ("CQ", "CK", "CV", "AO"):
                    dense(L, name)
                transposes(ytok, 4, "y_ready", NT)
                h_ready()
                dense(L, "U00")
                dense(L, "U01")
                softmax(gqa_items(), q2, k2b, v2b, B("G10", "G11"))
                for name in ("DQ", "DK", "DV"):
                    dense(L, name)
                pe.wait_ge(S["y_done"], n.at("items"))
                transposes(ytok, 4, None, 0)
                h_ready()
                dense(L, "U10")
                dense(L, "U11")
                for b in B("CQ", "CK", "CV"):
                    evacuated(b)
                softmax(nat_items(), q1, k1, v1, B("G20", "G21"))
                pe.wait_ge(S["y_done"], n.at("items"))
                transposes(ytok, 4, None, 0)
                h_ready()
                dense(L, "U20")
                dense(L, "U21")
                for b in B("DQ", "DK", "DV"):
                    evacuated(b)
                softmax(diff_items(), q2, k2, v2, B("G30", "G31"))
                transposes(ytok, 4, "y_ready", NT)
                h_ready()
                dense(L, "U30")
                dense(L, "U31")
                transposes(merged, KD, "y_ready", NT)
                h_ready()
                dense(L, "O0")
                dense(L, "O1")
                transposes(xn, KD, "xn_ready", NT)
                h_ready()
                for name in ffn_order():
                    if name.startswith("FD") and name.endswith("0"):
                        banks = B("FU" + name[2])[0].banks
                        pe.wait_ge(S["hid_ready"], n("hid_ready", banks))
                    dense(L, name)

        @block.scalar
        def _(act):
            n = Count()
            A = nc.scalar.activation

            def step(ins):
                ins.then_inc(S["act_step"], 1)
                act.wait_ge(S["act_step"], n("act_step"))

            def split(u):
                if u >= len(units):
                    return
                b, k0, kn, _ = units[u]
                act.wait_ge(landed[u % RAW_SLOTS], 16 * (u // RAW_SLOTS + 1))
                if u >= W_SLOTS:
                    act.wait_ge(S["groups"], units[u - W_SLOTS][3])
                if b.gates:
                    act.wait_ge(S["gin"], n("gin"))
                    raw, (hi, _lo) = raw_view(u), w_views(u)
                    for c, w, r in gate_parts(u):
                        ins = A(hi[:, :, c:c + w], raw[:, :, r:r + w], ACT.Copy)
                    ins.then_inc(S["w_hi"], 1)
                else:
                    width = kn * b.cols
                    A(wH[:, u % W_SLOTS, 0:width], wraw[:, u % RAW_SLOTS, 0:width], ACT.Copy).then_inc(S["w_hi"], 1)

            def ready(b, t):
                act.wait_ge(S["groups"], b.groups_end - (b.banks - 1 - t))

            def dense(l, name, evac=None):
                b = by_name[(l, name)]
                for i in range(len(b.units)):
                    split(b.first_unit + i + LOOK)
                if evac:
                    for t in range(b.banks):
                        ready(b, t)
                        evac(b, t)

            def copy_to(dst):
                def evac(b, t):
                    A(dst(t), bank[t][:, 0:b.cols] if b.orient == "tok" else bank[t][:, :], ACT.Copy).then_inc(free[t], 1)
                return evac

            taken = []

            def scratch_free():
                if len(taken) >= 2:
                    b, t = taken[-2]
                    act.wait_ge(free[t], b.nth[t] + 1)

            def tanh_half(b, t, cols):
                scratch_free()
                src = bank[t][:, cols]
                A(sbufPT[:, len(taken) % 2, 0:src.shape[1]], src, ACT.Tanh, scale=0.5).then_inc(S["tanh_ready"], 1)
                taken.append((b, t))

            def rms(source):
                for t in range(NT):
                    source(t)
                    A(sflat, x[:, t, :], ACT.Square, accum_out=ss[:, t:t + 1]).then_inc(S["norm_sq"], 1)
                    act.wait_ge(S["norm_sq"], n("norm_sq"))
                act.wait_ge(S["norm_ms"], n("norm_ms"))
                A(ss, ss, ACT.Sqrt).then_inc(S["norm_sd"], 1)

            def after(b):
                return lambda t: act.wait_ge(free[t], b.nth[t] + 1)

            def hi_chunks(chunks, dst, scale):
                for k in range(chunks):
                    i = n("tp") - 1
                    act.wait_ge(S["tp_done"], i + 1)
                    A(dst[:, k, :], bank[SC + i % 2][:, :], ACT.Copy, scale=scale(k)).then_inc(S["tp_hi"], 1)

            def gates(b, s):
                side = [(bb, i, t) for bb in b for i in range(4) for t in range(NT)]
                if s < len(side):
                    bb, i, t = side[s]
                    if t == 0:
                        split(bb.first_unit + i + LOOK)
                    if i == 3:
                        half = b.index(bb)
                        ready(bb, t)
                        A(gbuf[:, t, half * SEQ:(half + 1) * SEQ], bank[t][:, :], ACT.Tanh, scale=0.5).then_inc(
                            free[t], 1)

            def softmax(items, beside):
                i0 = n("items", len(items)) - len(items)
                for s in range(max(len(items) + 2, 32 if beside else 0)):
                    if s < len(items):
                        it, i = items[s], i0 + s
                        act.wait_ge(S["mx_done"], i + 1)
                        if i >= 2:
                            act.wait_ge(S["pt_done"], i - 1)
                        if i >= 4:
                            act.wait_ge(S["y_done"], i - 3)
                        kmax = it["kmax"]
                        biased = it["kind"] in ("nat", "diff")
                        src = sbufS[:, i % 2, 0:kmax] if biased else bank[SC + i % 2][:, 0:kmax]
                        A(sbufS[:, i % 2, 0:kmax], src, ACT.Exp, bias=nm[:, i % 4:i % 4 + 1],
                          scale=1.0 if biased else SCALE, accum_out=lsum[:, i % 4:i % 4 + 1]).then_inc(S["ex_done"], 1)
                    if 1 <= s <= len(items):
                        it, i = items[s - 1], i0 + s - 1
                        act.wait_ge(S["pt_done"], i + 1)
                        if i >= 2:
                            act.wait_ge(S["pv_done"], i - 1)
                        A(sbufPT[:, i % 2, 0:it["kmax"]], bank[TP][:, 0:it["kmax"]], ACT.Copy).then_inc(S["ptev"], 1)
                    if beside:
                        gates(beside, s)

            for u in range(LOOK):
                split(u)
            act.wait_ge(S["consts"], CONSTS)
            rms(lambda t: None)
            act.wait_ge(S["lam_dot"], 1)
            A(lam_tmp, lam_tmp, ACT.Exp).then_inc(S["lam_exp"], 1)
            A(lb, lb, ACT.Exp).then_inc(S["lb_ready"], 1)
            hi_chunks(KD, hH, lambda k: g_norm[0][:, k:k + 1])
            dense(0, "FL")
            act.wait_ge(S["row_abs"], n("row_abs"))
            step(A(yflat[0:8, 1024:1536], yflat[0:8, 512:1024], ACT.Exp, scale=-1.0))
            A(yflat[0:8, 1024:1536], yflat[0:8, 1024:1536], ACT.Ln, bias=1.0).then_inc(S["row_log"], 1)

            def bf_evac(b, t):
                if t < 2:
                    tanh_half(b, t, slice(0, SEQ))
            dense(0, "BF", bf_evac)
            act.wait_ge(S["z_ready"], 1)
            A(gflat[:, 1024:2048], gflat[:, 0:1024], ACT.Exp, scale=-1.0).then_inc(S["ez_ready"], 1)
            act.wait_ge(S["z_ready"], 2)
            A(gflat[:, 2048:3072], gflat[:, 2048:3072], ACT.Ln).then_inc(S["ln_ready"], 1)
            A(gflat[:, 3072:4096], gflat[:, 3072:4096], ACT.Ln).then_inc(S["ln_ready"], 1)

            def bi_evac(b, t):
                A(vi[:, t, :], bank[t][:, 0:256], ACT.Copy)
                tanh_half(b, t, slice(256, 512))
            dense(0, "BI", bi_evac)

            def uv_evac(b, t):
                scratch_free()
                slot = len(taken) % 2
                A(sbufS[:, slot, :], bank[t][:, :], ACT.Square).then_inc(S["gsq"], 1)
                act.wait_ge(S["gin2"], n("gin2"))
                A(sbufPT[:, slot, :], sbufS[:, slot, :], ACT.Tanh, scale=GELU_C).then_inc(S["tanh_ready"], 1)
                taken.append((b, t))
            dense(0, "UV", uv_evac)

            dense(0, "AZ", lambda b, t: tanh_half(b, t, slice(0, 256)))
            for name, dst in (("CQ", q2), ("CK", k2), ("CV", v2)):
                dense(0, name, copy_to(lambda t, dst=dst: dst[:, t, :]))
            dense(0, "CZ", lambda b, t: tanh_half(b, t, slice(0, SEQ)))
            for lev in range(LEVELS):
                act.wait_ge(S["d_ready"], lev + 1)
                A(sflat, sflat, ACT.Exp).then_inc(S["ed_ready"], 1)
            act.wait_ge(S["d_ready"], LEVELS + 1)
            A(qe, bb, ACT.Exp).then_inc(S["ed_ready"], 1)
            A(ke, ke, ACT.Exp).then_inc(S["ed_ready"], 1)
            act.wait_ge(S["keT_done"], 3)
            A(gflat[:, 2048:2560], bank[TP][:, :], ACT.Copy).then_inc(S["keT_read"], 1)
            A(gflat[:, 2560:2816], bank[PV][:, 0:256], ACT.Copy).then_inc(S["keT_read"], 1)
            for m in range(NT):
                act.wait_ge(S["ho_done"], m + 1)
                for half in range(2):
                    A(sflat[:, m * 256:(m + 1) * 256].rearrange("p (g h d) -> p g h d", g=2, h=2)[:, :, half, :],
                      bank[TP + half][:, 0:2 * DH].rearrange("p (g d) -> p g d", g=2), ACT.Copy).then_inc(S["ho_read"], 1)
            act.wait_ge(S["ho_read"], 2 * NT)
            A(ptflat, sflat, ACT.Square).then_inc(S["sq_ready"], 1)
            n("sq_ready")
            act.wait_ge(S["ms_ready"], n("ms_ready"))
            A(st32[:, 0:16], st32[:, 0:16], ACT.Sqrt).then_inc(S["sd_ready"], 1)
            act.wait_ge(S["ms_ready"], n("ms_ready"))
            A(ptflat, vv, ACT.Square).then_inc(S["sq_ready"], 1)
            act.wait_ge(S["ms_ready"], n("ms_ready"))
            A(st32[:, 0:16], st32[:, 0:16], ACT.Sqrt).then_inc(S["sd_ready"], 1)
            softmax(fox_items(), [])
            hi_chunks(KD, hH, lambda k: 0.5)
            dense(0, "O0")
            dense(0, "O1")
            rms(after(by_name[(0, "O1")]))

            for l in range(DEPTH):
                L = l + 1

                def B(*names):
                    return [by_name[(L, name)] for name in names]

                if l == 0:
                    rms(lambda t: act.wait_ge(S["x_ready"], t + 1))
                else:
                    rms(after(by_name[(l, ffn_order()[-1])]))
                hi_chunks(KD, hH, lambda k: g_norm[1 + 2 * l][:, k:k + 1])
                dense(L, "BQ", copy_to(lambda t: qraw[:, t, :]))

                def bkv_evac(b, t):
                    A(kraw[:, t, :], bank[t][:, 0:P], ACT.Copy)
                    A(v2b[:, t, :], bank[t][:, P:2 * P], ACT.Copy).then_inc(free[t], 1)
                dense(L, "BKV", bkv_evac)
                for t in range(NT):
                    if t >= 2:
                        act.wait_ge(S["sq_taken"], n("sq_taken"))
                    act.wait_ge(free[t], by_name[(L, "BKV")].nth[t] + 1)
                    A(sbufS[:, t % 2, :], qraw[:, t, :], ACT.Square)
                    A(sbufPT[:, t % 2, 0:P], kraw[:, t, :], ACT.Square).then_inc(S["sq_ready"], 1)
                n("sq_taken", 2)
                dense(L, "AG")
                act.wait_ge(S["ms_ready"], n("ms_ready"))
                A(st40, st40, ACT.Sqrt).then_inc(S["sd_ready"], 1)
                act.wait_ge(S["row_abs"], n("row_abs"))
                step(A(row_m, row_w, ACT.Exp, scale=-1.0))
                A(row_m, row_m, ACT.Ln, bias=1.0).then_inc(S["row_log"], 1)

                def conv_tanh(b, t):
                    act.wait_ge(free[t], b.nth[t] + 1)
                    A(sbufPT[:, t % 2, :], sbufS[:, t % 2, :], ACT.Tanh, scale=0.5).then_inc(S["conv_tanh"], 1)
                dense(L, "AQ", conv_tanh)
                act.wait_ge(S["rowt_read"], l + 1)
                A(mcol, mcol, ACT.Exp).then_inc(S["mcol_ready"], 1)
                dense(L, "AK", conv_tanh)
                for k in range(4):
                    i = n("tp") - 1
                    act.wait_ge(S["tp_done"], i + 1)
                    A(q2[:, k, :], bank[SC + i % 2][:, :], ACT.Copy).then_inc(S["tp_free"], 1)
                i = n("tp") - 1
                act.wait_ge(S["tp_done"], i + 1)
                for g in range(2):
                    for half in range(2):
                        ins = A(k2b[64 * half:64 * half + 64, g, :], bank[SC + i % 2][64 * g:64 * g + 64, :], ACT.Copy)
                        if (g, half) != (1, 1):
                            step(ins)
                ins.then_inc(S["tp_free"], 1)
                dense(L, "AV", lambda b, t: A(v1a[:, t, :, 0:P], bank[t][:, :].rearrange("p (h d) -> p h d", h=4),
                                              ACT.Copy).then_inc(free[t], 1))
                for s in range(36):
                    c, j = s // 4, s % 4
                    if c < 8:
                        i, h, back = 32 * l + s, c // 2, c % 2
                        lo, hi = (0, (j + 1) * P) if back else (j * P, SEQ)
                        act.wait_ge(S["mb_done"], i + 1)
                        if i >= 2:
                            act.wait_ge(S["p_done"], i - 1)
                        if s < 2:
                            act.wait_ge(S["qk_ready"], 9 * (l + 1))
                        col = j * 8 + back * 4 + h
                        A(sbufS[:, i % 2, lo:hi], bank[TP][:, lo:hi], ACT.Exp, bias=wcol[:, col:col + 1]).then_inc(
                            S["e_done"], 1)
                    gates(B("G00", "G01"), s)
                def ln_sq():
                    act.wait_ge(S["ms_ready"], n("ms_ready"))
                    A(mflat[:, 0:2048], yflat, ACT.Square).then_inc(S["sq_ready"], 1)
                    act.wait_ge(S["ms_ready"], n("ms_ready"))
                    A(st32[:, 0:16], st32[:, 0:16], ACT.Sqrt).then_inc(S["sd_ready"], 1)
                dense(L, "CQ", copy_to(lambda t: q1[:, t, :]))
                ln_sq()
                dense(L, "CK", copy_to(lambda t: k1[:, t, :]))
                dense(L, "CV", copy_to(lambda t: v1[:, t, :]))

                dense(L, "AO", lambda b, t: tanh_half(b, t, slice(0, SEQ)))
                hi_chunks(4, yH, lambda k: g_anorm[l][:, k:k + 1])
                dense(L, "U00")
                dense(L, "U01")
                softmax(gqa_items(), B("G10", "G11"))
                for name, dst in (("DQ", q2), ("DK", k2), ("DV", v2)):
                    dense(L, name, copy_to(lambda t, dst=dst: dst[:, t, :]))
                hi_chunks(4, yH, lambda k: 1.0)
                dense(L, "U10")
                dense(L, "U11")
                softmax(nat_items(), B("G20", "G21"))
                hi_chunks(4, yH, lambda k: 1.0)
                dense(L, "U20")
                dense(L, "U21")
                softmax(diff_items(), B("G30", "G31"))
                for t in range(NT):
                    act.wait_ge(S["y_done"], n.at("items"))
                    if t >= 2:
                        act.wait_ge(S["sq_taken"], n("sq_taken"))
                    A(sbufPT[:, t % 2, :], ytok[:, t, :], ACT.Square).then_inc(S["sq_ready"], 1)
                n("sq_taken", 2)
                act.wait_ge(S["ms_ready"], n("ms_ready"))
                A(st32[:, 0:16], st32[:, 0:16], ACT.Sqrt).then_inc(S["sd_ready"], 1)
                hi_chunks(4, yH, lambda k: g_sub[l])
                dense(L, "U30")
                dense(L, "U31")
                hi_chunks(KD, hH, lambda k: 0.5)
                dense(L, "O0")
                dense(L, "O1")
                rms(after(by_name[(L, "O1")]))
                hi_chunks(KD, hH, lambda k: g_norm[2 + 2 * l][:, k:k + 1])
                for name in ffn_order():
                    if name[:2] == "FG":
                        dense(L, name, lambda b, t: tanh_half(b, t, slice(0, SEQ)))
                    elif name[:2] == "FU":
                        def fu_evac(b, t):
                            act.wait_ge(free[t], b.nth[t] + 1)
                            A(yH[:, t, :], sbufS[:, t % 2, :], ACT.Copy).then_inc(S["hid_hi"], 1)
                        dense(L, name, fu_evac)
                    else:
                        dense(L, name)
            rms(after(by_name[(DEPTH, ffn_order()[-1])]))

        @block.vector
        def _(dve):
            n = Count()
            V = nc.vector

            def then(ins):
                ins.then_inc(S["dve_step"], 1)
                dve.wait_ge(S["dve_step"], n("dve_step"))

            def split(u):
                if u >= len(units):
                    return
                b, k0, kn, _ = units[u]
                if b.gates:
                    if u >= W_SLOTS:
                        dve.wait_ge(S["groups"], units[u - W_SLOTS][3])
                    V.memset(wL[:, u % W_SLOTS, 0:kn * P].bitcast(F32), 0.0)
                    V.memset(wH[:, u % W_SLOTS, 0:kn * P].bitcast(F32), 0.0).then_inc(S["gin"], 1)
                dve.wait_ge(S["w_hi"], u + 1)
                if b.gates:
                    raw, (hi, lo) = raw_view(u), w_views(u)
                    for c, w, r in gate_parts(u):
                        ins = V.tensor_tensor(lo[:, :, c:c + w], raw[:, :, r:r + w], hi[:, :, c:c + w].bitcast(F32),
                                              ALU.subtract)
                    ins.then_inc(S["w_lo"], 1)
                else:
                    width = kn * b.cols
                    V.tensor_tensor(wL[:, u % W_SLOTS, 0:width], wraw[:, u % RAW_SLOTS, 0:width],
                                    wH[:, u % W_SLOTS, 0:width].bitcast(F32), ALU.subtract).then_inc(S["w_lo"], 1)

            def ready(b, t):
                dve.wait_ge(S["groups"], b.groups_end - (b.banks - 1 - t))

            def evacuated(b, t):
                dve.wait_ge(free[t], b.nth[t] + 1)

            def dense(l, name, evac=None, between=None):
                b = by_name[(l, name)]
                for i in range(len(b.units)):
                    split(b.first_unit + i + LOOK)
                    if between:
                        between(i)
                if evac:
                    for t in range(b.banks):
                        ready(b, t)
                        evac(b, t)

            def norm_rows(dst):
                dve.wait_ge(S["norm_sq"], n("norm_sq", NT))
                V.tensor_scalar(ss, ss, 1.0 / D, EPS, ALU.mult, ALU.add).then_inc(S["norm_ms"], 1)
                dve.wait_ge(S["norm_sd"], n("norm_sd"))
                then(V.reciprocal(rstd, ss))
                for t in range(NT):
                    dst(t, rstd[:, t:t + 1])

            def to_xn(t, r):
                V.tensor_scalar(xn[:, t, :], x[:, t, :], r, None, ALU.mult).then_inc(S["xn_ready"], 1)

            def lo_chunks(chunks, hi, lo, scale):
                for k in range(chunks):
                    i = n("tp") - 1
                    dve.wait_ge(S["tp_hi"], n("tp_hi"))
                    V.scalar_tensor_tensor(out=lo[:, k, :], in0=bank[SC + i % 2][:, :], scalar=scale(k),
                                           in1=hi[:, k, :].bitcast(F32), op0=ALU.mult, op1=ALU.subtract).then_inc(
                        S["tp_free"], 1)

            tanhs = [0]

            def silu(dst, src, b, t):
                dve.wait_ge(S["tanh_ready"], n("tanh_ready"))
                slot = tanhs[0] % 2
                tanhs[0] += 1
                V.scalar_tensor_tensor(out=dst, in0=sbufPT[:, slot, 0:src.shape[1]], scalar=1.0, in1=src,
                                       op0=ALU.add, op1=ALU.mult).then_inc(free[t], 1)

            def residual(half):
                def evac(b, t):
                    V.tensor_tensor(x[:, t, half * SEQ:(half + 1) * SEQ], x[:, t, half * SEQ:(half + 1) * SEQ],
                                    bank[t][:, :], ALU.add).then_inc(free[t], 1)
                return evac

            def log_sigmoid(f, tmp, e):
                V.scalar_tensor_tensor(out=tmp, in0=f, scalar=-1.0, in1=f, op0=ALU.mult, op1=ALU.max).then_inc(
                    S["row_abs"], 1)
                dve.wait_ge(S["row_log"], n("row_log"))
                then(V.scalar_tensor_tensor(out=f, in0=f, scalar=0.0, in1=e, op0=ALU.min, op1=ALU.subtract))

            def group_sums(dst, src, groups):
                then(V.tensor_reduce(dst, src.rearrange("p (g d) -> p g d", g=groups), AX, ALU.add))

            def per_group(dst, src, col, groups):
                w = src.shape[1] // groups
                return (dst.rearrange("p (g d) -> p g d", g=groups), src.rearrange("p (g d) -> p g d", g=groups),
                        col.unsqueeze(2).to_broadcast([P, groups, w]))

            def softmax(l, items, beside):
                i0 = n("items", len(items)) - len(items)
                for s in range(max(len(items) + 2, 32 if beside else 0)):
                    if s < len(items):
                        it, i = items[s], i0 + s
                        kmax, col = it["kmax"], i % 4
                        kind, per = it["kind"], 8 if it["kind"] == "diff" else 4
                        if kind == "nat" and (s == 0 or s % per == 1):
                            for h in ([0] if s == 0 else [s // per + 1] if s // per + 1 < HEADS else []):
                                dve.wait_ge(S[f"tab_dma{h % 2}"], n(f"tab{h % 2}", 32))
                                then(V.scalar_tensor_tensor(
                                    out=tab[:, h % 2, :].rearrange("p (e k) -> p e k", e=14),
                                    in0=tab[:, h % 2, :].rearrange("p (e k) -> p e k", e=14), scalar=1.0 / SCALE,
                                    in1=nat_mask[:, :].unsqueeze(1).to_broadcast([P, 14, DH]),
                                    op0=ALU.mult, op1=ALU.add))
                        if kind == "diff" and s % per == 0:
                            h = it["h"]
                            dve.wait_ge(S[f"tab_dma{h % 2}"], n(f"tab{h % 2}", 16))
                        dve.wait_ge(S["sc_done"], i + 1)
                        if kind in ("nat", "diff"):
                            if i >= 2:
                                dve.wait_ge(S["pt_done"], i - 1)
                            table = tab[:, it["h"] % 2, it["t"] * P:it["t"] * P + SEQ][:, ::-1]
                            then(V.tensor_tensor_reduce(sbufS[:, i % 2, :], bank[SC + i % 2][:, :], table, SCALE, -BIG,
                                                        ALU.add, ALU.max, mx[:, col:col + 1]))
                            V.tensor_scalar(nm[:, col:col + 1], mx[:, col:col + 1], -1.0, None, ALU.mult).then_inc(
                                S["mx_done"], 1)
                        else:
                            then(V.tensor_reduce(mx[:, col:col + 1], bank[SC + i % 2][:, 0:kmax], AX, ALU.max))
                            V.tensor_scalar(nm[:, col:col + 1], mx[:, col:col + 1], -SCALE, None, ALU.mult).then_inc(
                                S["mx_done"], 1)
                    if 2 <= s < len(items) + 2:
                        it, i = items[s - 2], i0 + s - 2
                        col, w = i % 4, it["v"][1]
                        dve.wait_ge(S["pv_done"], i + 1)
                        then(V.reciprocal(rs[:, col:col + 1], lsum[:, col:col + 1]))
                        r, src = rs[:, col:col + 1], bank[PV][:, 0:w]
                        if it["kind"] == "fox":
                            dst = merged[:, it["t"], SEQ + it["y"]:SEQ + it["y"] + w]
                            V.scalar_tensor_tensor(out=dst, in0=src, scalar=r, in1=dst, op0=ALU.mult,
                                                   op1=ALU.mult).then_inc(S["y_done"], 1)
                        else:
                            dst = ytok[:, it["t"], it["y"]:it["y"] + w]
                            if it["comp"] == 0:
                                V.tensor_scalar(dst, src, r, None, ALU.mult).then_inc(S["y_done"], 1)
                            else:
                                then(V.tensor_tensor(r, r, lam[l], ALU.mult))
                                V.scalar_tensor_tensor(out=dst, in0=src, scalar=r, in1=dst, op0=ALU.mult,
                                                       op1=ALU.add).then_inc(S["y_done"], 1)
                    if beside and s % 4 == 0 and s < 32:
                        split(beside[s // 16].first_unit + (s // 4) % 4 + LOOK)

            def merge(l, br, half):
                gate = by_name[(l, f"G{br}{half}")]

                def evac(b, t):
                    evacuated(gate, t)
                    cols = slice(half * SEQ, (half + 1) * SEQ)
                    if br == 0:
                        V.scalar_tensor_tensor(out=merged[:, t, cols], in0=gbuf[:, t, cols], scalar=1.0,
                                               in1=bank[t][:, :], op0=ALU.add, op1=ALU.mult).then_inc(free[t], 1)
                        return
                    V.scalar_tensor_tensor(out=sbufS[:, t % 2, :], in0=gbuf[:, t, cols], scalar=1.0,
                                           in1=bank[t][:, :], op0=ALU.add, op1=ALU.mult).then_inc(free[t], 1)
                    evacuated(b, t)
                    add = V.tensor_tensor(merged[:, t, cols], merged[:, t, cols], sbufS[:, t % 2, :], ALU.add)
                    if br == 3 and half == 1:
                        add.then_inc(S["y_ready"], 1)
                return evac

            for u in range(LOOK):
                split(u)
            dve.wait_ge(S["consts"], CONSTS)
            norm_rows(to_xn)
            for i in range(2 * DEPTH):
                ins = V.tensor_tensor_reduce(gflat[:, 2048 + DH * i:2048 + DH * (i + 1)], gflat[:, 2 * i * DH:(2 * i + 1) * DH],
                                             gflat[:, (2 * i + 1) * DH:(2 * i + 2) * DH], 1.0, 0.0, ALU.mult, ALU.add,
                                             lam_tmp[:, i:i + 1])
            V.tensor_tensor(lb, lbt, lbt, ALU.subtract).then_inc(S["lam_dot"], 1)
            lo_chunks(KD, hH, hL, lambda k: g_norm[0][:, k:k + 1])
            dve.wait_ge(S["lam_exp"], 1)
            for l in range(DEPTH):
                then(V.tensor_tensor(lam[l], lam_tmp[:, 2 * l + 1:2 * l + 2], lam_tmp[:, 2 * l:2 * l + 1], ALU.subtract))
                V.tensor_scalar(lam[l], lam[l], -lambda_init(l), None, ALU.add)
            dve.wait_ge(S["lb_ready"], 1)
            then(V.reciprocal(oml, lb))
            then(V.tensor_tensor(lb, lb, oml, ALU.mult))
            then(V.tensor_tensor(lb, lb, lb, ALU.subtract))
            then(V.tensor_scalar(lb, lb, 0.0, 1.0 - 1e-6, ALU.max, ALU.min))
            then(V.tensor_scalar(oml, lb, -1.0, 1.0, ALU.mult, ALU.add))

            def fl_evac(b, t):
                f, tmp, e, ones = (yflat[0:8, 512 * i:512 * i + 512] for i in range(4))
                V.memset(ones, 1.0)
                V.tensor_scalar(f, bank[0][0:8, :], bf_col[0:8, :], None, ALU.add).then_inc(free[0], 1)
                evacuated(b, 0)
                log_sigmoid(f, tmp, e)
                then(V.tensor_tensor_scan(tmp, ones, f, 0.0, ALU.mult, ALU.add))
                then(V.tensor_scalar(fox_c[0:8, :], tmp, -1.0 / SCALE, None, ALU.mult))
            dense(0, "FL", fl_evac)

            def bf_evac(b, t):
                if t < 2:
                    silu(qs[:, t, :], bank[t][:, :], b, t)
                else:
                    ins = V.tensor_scalar(gflat[:, (t - 2) * SEQ:(t - 1) * SEQ], bank[t][:, :], -80.0, None, ALU.max)
                    ins.then_inc(free[t], 1)
            dense(0, "BF", bf_evac)
            for t in range(4):
                evacuated(by_name[(0, "BF")], t)
            qs_f, ks_f = set1[:, 0:1024], set1[:, 1024:2048]
            V.tensor_scalar(qs_f, qs_f, 0.5 * DH ** -0.5, None, ALU.mult).then_inc(S["z_ready"], 1)
            dve.wait_ge(S["ez_ready"], 1)
            then(V.tensor_scalar(gflat[:, 0:1024], gflat[:, 1024:2048], 1.0, None, ALU.add))
            then(V.reciprocal(gflat[:, 0:1024], gflat[:, 0:1024]))
            for g in range(2):
                cols_g = slice(g * SEQ, (g + 1) * SEQ)
                V.tensor_scalar(gflat[:, 2048 + g * SEQ:2560 + g * SEQ], gflat[:, cols_g], oml[:, g:g + 1], lb[:, g:g + 1],
                                ALU.mult, ALU.add)
                then(V.scalar_tensor_tensor(out=ks[:, g, :], in0=gflat[:, 1024 + g * SEQ:1536 + g * SEQ],
                                            scalar=oml[:, g:g + 1], in1=gflat[:, cols_g], op0=ALU.mult, op1=ALU.mult))
            then(V.tensor_scalar(gflat[:, 3072:4096], gflat[:, 2048:3072], 1e-30, 2.0 ** 60, ALU.max, ALU.mult))
            then(V.tensor_scalar(gflat[:, 3072:4096], gflat[:, 3072:4096], 1.0, None, ALU.min))
            V.tensor_scalar(gflat[:, 2048:3072], gflat[:, 2048:3072], 2.0 ** -60, None, ALU.max).then_inc(S["z_ready"], 1)
            dve.wait_ge(S["ln_ready"], 2)
            V.memset(gflat[:, 0:1024], 1.0)
            then(V.tensor_tensor(gflat[:, 2048:3072], gflat[:, 2048:3072], gflat[:, 3072:4096], ALU.add))
            for c in range(8):
                tok = slice(c * P, (c + 1) * P)
                ins = V.tensor_tensor_scan(set1[:, 2048 + c * P:2048 + (c + 1) * P], gflat[:, tok],
                                           gflat[:, 2048 + c * P:2048 + (c + 1) * P], 0.0, ALU.mult, ALU.add)
            then(ins)
            dense(0, "BI", lambda b, t: silu(merged[:, t, 256:512], bank[t][:, 256:512], b, t))

            def uv_evac(b, t):
                slot = tanhs[0] % 2
                dve.wait_ge(S["gsq"], n("gsq"))
                then(V.tensor_scalar(sbufS[:, slot, :], sbufS[:, slot, :], GELU_A, 1.0, ALU.mult, ALU.add))
                V.tensor_tensor(sbufS[:, slot, :], sbufS[:, slot, :], bank[t][:, :], ALU.mult).then_inc(S["gin2"], 1)
                dve.wait_ge(S["tanh_ready"], n("tanh_ready"))
                tanhs[0] += 1
                V.scalar_tensor_tensor(out=uu[:, t, :], in0=sbufPT[:, slot, 0:256], scalar=1.0,
                                       in1=bank[t][:, 0:256], op0=ALU.add, op1=ALU.mult)
                V.scalar_tensor_tensor(out=vv[:, t, :], in0=sbufPT[:, slot, 256:512], scalar=1.0,
                                       in1=bank[t][:, 256:512], op0=ALU.add, op1=ALU.mult).then_inc(free[t], 1)
            dense(0, "UV", uv_evac)
            dense(0, "AZ", lambda b, t: silu(merged[:, t, 0:256], bank[t][:, 0:256], b, t))
            dense(0, "CQ")
            dense(0, "CK")
            dense(0, "CV")
            dense(0, "CZ", lambda b, t: silu(merged[:, t, 512:1024], bank[t][:, :], b, t))

            then(V.memset(gflat, 0.0))
            then(V.memset(yflat, 0.0))
            masks = tflat[:, 0:1024].rearrange("p (l t) -> p l t", t=P)
            bflat = set1[:, 2048:3072]

            def level(lev):
                m = CHUNK >> (lev + 1)
                halves = [z.rearrange("p (n h m) -> p n h m", h=2, m=m)
                          for z in (bflat, qs_f, ks_f, gflat[:, 2048 * (lev % 2):2048 * (lev % 2) + 1024],
                                    gflat[:, 2048 * (lev % 2) + 1024:2048 * (lev % 2) + 2048])]
                bh, qh, kh, ql, kl = halves
                nb = 1024 // (2 * m)
                border = bh[:, :, 0, m - 1:m].to_broadcast([P, nb, m])
                dq = sflat[:, 0:512].rearrange("p (n m) -> p n m", m=m)
                dk = sflat[:, 512:1024].rearrange("p (n m) -> p n m", m=m)
                V.tensor_tensor(dq, bh[:, :, 1, :], border, ALU.subtract)
                V.tensor_tensor(dk, border, bh[:, :, 0, :], ALU.subtract).then_inc(S["d_ready"], 1)
                dve.wait_ge(S["ed_ready"], lev + 1)
                V.tensor_tensor(ql[:, :, 1, :], qh[:, :, 1, :], dq, ALU.mult)
                V.tensor_tensor(kl[:, :, 0, :], kh[:, :, 0, :], dk, ALU.mult).then_inc(S["lvl_ready"], 1)
                dve.wait_ge(S["lvl_ready"], lev + 1)

            level(0)
            for lev in range(LEVELS + 1):
                if lev + 1 < LEVELS:
                    level(lev + 1)
                elif lev + 1 == LEVELS:
                    V.memset(rs[:, 0:1], 0.0).then_inc(S["lvl_ready"], 1)
                for h in range(4):
                    c = 4 * lev + h
                    dve.wait_ge(S["lvl_done"], c + 1)
                    V.copy_predicated(ssc[:, h, :, :], masks[:, lev, :].bitcast(U32).unsqueeze(1).to_broadcast([P, NT, P]),
                                      bank[SC + c % 2][:, :].rearrange("p (n t) -> p n t", n=NT)).then_inc(
                        S["lvl_used"], 1)
            dve.wait_ge(S["lvl_used"], 4 * (LEVELS + 1))
            b8 = bflat.rearrange("p (c t) -> p c t", t=P)
            V.tensor_tensor(gflat[:, 1024:2048].rearrange("p (c t) -> p c t", t=P),
                            b8[:, :, P - 1:P].to_broadcast([P, 8, P]), b8, ALU.subtract).then_inc(S["d_ready"], 1)
            dve.wait_ge(S["ed_ready"], LEVELS + 2)
            V.tensor_copy(ebl, gflat[:, 0:1024].rearrange("p (c t) -> p c t", t=P)[:, :, P - 1])
            then(V.tensor_tensor(gflat[:, 1024:2048], gflat[:, 1024:2048], ks_f, ALU.mult))
            V.tensor_tensor(gflat[:, 0:1024], gflat[:, 0:1024], qs_f, ALU.mult).then_inc(S["ke_ready"], 1)
            dve.wait_ge(S["upd_done"], 3)
            for m in range(3):
                for g in range(2):
                    for half in range(2):
                        r = slice(DH * half, DH * half + DH)
                        upd = bank[SC + m // 2][r, (2 * (m % 2) + g) * P + DH * half:(2 * (m % 2) + g) * P + DH * half + DH]
                        if m == 0:
                            then(V.tensor_copy(states[r, m, g, :], upd))
                        else:
                            then(V.scalar_tensor_tensor(out=states[r, m, g, :], in0=states[r, m - 1, g, :],
                                                        scalar=ebl[r, 4 * g + m:4 * g + m + 1], in1=upd,
                                                        op0=ALU.mult, op1=ALU.add))
            V.memset(rs[:, 1:2], 0.0).then_inc(S["st_ready"], 1)
            dve.wait_ge(S["sq_ready"], n("sq_ready"))
            group_sums(st32[:, 0:16], ptflat, 16)
            V.tensor_scalar(st32[:, 0:16], st32[:, 0:16], 1.0 / DH, EPS, ALU.mult, ALU.add).then_inc(S["ms_ready"], 1)
            dve.wait_ge(S["sd_ready"], n("sd_ready"))
            then(V.reciprocal(st32b[:, 0:16], st32[:, 0:16]))
            o_g, _, r_g = per_group(sflat, sflat, st32b[:, 0:16], 16)
            then(V.tensor_tensor(o_g, o_g, r_g, ALU.mult))
            then(V.tensor_tensor(o_g, o_g, onorm.unsqueeze(1).to_broadcast([P, 16, DH]), ALU.mult))
            V.tensor_tensor(merged[:, :, 256:512], merged[:, :, 256:512],
                            sflat.rearrange("p (t d) -> p t d", t=NT), ALU.mult).then_inc(S["late"], 1)

            v_f = set1[:, 5120:6144]
            group_sums(st32c[:, 0:16], v_f, 16)
            then(V.tensor_scalar(st32c[:, 0:16], st32c[:, 0:16], 1.0 / DH, None, ALU.mult))
            v_g, _, mean = per_group(v_f, v_f, st32c[:, 0:16], 16)
            V.tensor_tensor(v_g, v_g, mean, ALU.subtract).then_inc(S["ms_ready"], 1)
            dve.wait_ge(S["sq_ready"], n("sq_ready"))
            group_sums(st32[:, 0:16], ptflat, 16)
            V.tensor_scalar(st32[:, 0:16], st32[:, 0:16], 1.0 / DH, 4 * EPS, ALU.mult, ALU.add).then_inc(S["ms_ready"], 1)
            dve.wait_ge(S["sd_ready"], n("sd_ready"))
            then(V.reciprocal(st32b[:, 0:16], st32[:, 0:16]))
            then(V.tensor_tensor(v_g, v_g, st32b[:, 0:16].unsqueeze(2).to_broadcast([P, 16, DH]), ALU.mult))
            dve.wait_ge(S["gp_step"], 16 * 5)
            then(V.tensor_tensor(gflat[:, 0:512], gflat[:, 0:512], gflat[:, 1024:1536], ALU.mult))
            then(V.tensor_tensor(vv, vv, gflat[:, 512:768].unsqueeze(1).to_broadcast([P, NT, 256]), ALU.mult))
            V.tensor_tensor(vv, vv, gflat[:, 768:1024].unsqueeze(1).to_broadcast([P, NT, 256]), ALU.add).then_inc(
                S["vn_ready"], 1)
            for g in range(4):
                dve.wait_ge(S["mix_done"], g + 1)
            for g in range(4):
                tmp = view(sflat, 256 * g, (NT, DH))
                then(V.scalar_tensor_tensor(out=tmp, in0=bank[TP + g // 2][:, (g % 2) * 256:(g % 2) * 256 + 256].rearrange(
                    "p (n d) -> p n d", n=NT), scalar=bs_t[:, g:g + 1], in1=uu[:, :, g * DH:(g + 1) * DH],
                    op0=ALU.add, op1=ALU.mult))
                dst = merged[:, :, g * DH:(g + 1) * DH]
                then(V.scalar_tensor_tensor(out=dst, in0=tmp, scalar=0.5, in1=dst, op0=ALU.mult, op1=ALU.mult))
            softmax(0, fox_items(), [])
            lo_chunks(KD, hH, hL, lambda k: 0.5)
            dense(0, "O0", residual(0))
            dense(0, "O1", residual(1))

            def to_x(sem):
                def dst(t, r):
                    V.scalar_tensor_tensor(out=x[:, t, :], in0=x[:, t, :], scalar=r, in1=yflat[:, 0:D], op0=ALU.mult,
                                           op1=ALU.mult).then_inc(S[sem], 1)
                return dst
            norm_rows(to_x("x_ready"))
            dve.wait_ge(S["x_ready"], NT)

            for l in range(DEPTH):
                L = l + 1

                def B(*names):
                    return [by_name[(L, name)] for name in names]

                norm_rows(to_xn)
                lo_chunks(KD, hH, hL, lambda k: g_norm[1 + 2 * l][:, k:k + 1])
                for tc, ts, gain in ((cq_t, sq_t, g_q[l]), (ck_t, sk_t, g_k[l])):
                    V.tensor_tensor(tc, rope[:, 0, :, :], gain.unsqueeze(1).to_broadcast([P, NT, DH]), ALU.mult)
                    for j in range(2):
                        def pick(z, jj):
                            return z.rearrange("p t (g j d) -> p t g j d", g=2, j=2)[:, :, :, jj, :]
                        gsw = gain.rearrange("p (g j d) -> p g j d", g=2, j=2)[:, :, 1 - j, :]
                        for gg in range(2):
                            V.tensor_tensor(pick(ts, j)[:, :, gg, :], pick(rope[:, 1, :, :], j)[:, :, gg, :],
                                            gsw[:, gg, :].unsqueeze(1).to_broadcast([P, NT, 16]), ALU.mult)
                dense(L, "BQ")
                dense(L, "BKV")
                for t in range(NT):
                    dve.wait_ge(S["sq_ready"], n("sq_ready"))
                    V.tensor_reduce(st40[:, 8 * t:8 * t + 8], sbufS[:, t % 2, :].rearrange("p (g d) -> p g d", g=8), AX, ALU.add)
                    V.tensor_reduce(st40[:, 32 + 2 * t:34 + 2 * t], sbufPT[:, t % 2, 0:P].rearrange("p (g d) -> p g d", g=2),
                                    AX, ALU.add).then_inc(S["sq_taken"], 1)
                dve.wait_ge(S["sq_taken"], n("sq_taken", NT))
                V.tensor_scalar(st40, st40, 1.0 / DH, EPS, ALU.mult, ALU.add).then_inc(S["ms_ready"], 1)

                def ag_evac(b, t):
                    V.memset(row_b, 0.0)
                    V.tensor_scalar(row_i, bank[0][0:GATE_ROWS, :], g_bias[l][0:GATE_ROWS, 0:1], None, ALU.add)
                    V.tensor_scalar(row_f, bank[0][64:64 + GATE_ROWS, :], g_bias[l][0:GATE_ROWS, 1:2], None,
                                    ALU.add).then_inc(free[0], 1)
                    evacuated(b, 0)
                    log_sigmoid(row_f, row_w, row_m)
                    then(V.memset(row_w, 1.0))
                    for r, d in ((slice(0, 4), 1), (slice(32, 36), -1)):
                        then(V.tensor_tensor_scan(row_b[r, ::d], row_w[r, ::d], row_f[r, ::d], 0.0, ALU.mult, ALU.add))
                    then(V.tensor_tensor(row_w, row_i, row_b, ALU.subtract))
                    for r, d in ((slice(0, 4), 1), (slice(32, 36), -1)):
                        then(V.tensor_tensor_scan(row_f[r, ::d], row_w[r, ::d], row_w[r, ::d], 0.0, ALU.max, ALU.max))
                    V.tensor_scalar(row_nm, row_f, -1.0, None, ALU.mult)
                    then(V.tensor_tensor(row_m, row_b, row_f, ALU.add))
                    V.tensor_scalar(row_m, row_m, -1.0, 85.0, ALU.mult, ALU.min).then_inc(S["rows_ready"], 1)
                dense(L, "AG", ag_evac)
                dve.wait_ge(S["sd_ready"], n("sd_ready"))
                then(V.reciprocal(st40, st40))

                def rotate(t):
                    for z, heads, tc, ts, r, at_c in ((qraw[:, t, :], 8, cq_t, sq_t, st40[:, 8 * t:8 * t + 8], 0),
                                                      (kraw[:, t, :], 2, ck_t, sk_t, st40[:, 32 + 2 * t:34 + 2 * t], 0)):
                        w = heads * DH
                        xc, xs = rope_c[:, 0:w], rope_s[:, 0:w]
                        z3 = z.rearrange("p (h d) -> p h d", h=heads)
                        V.tensor_tensor(xc.rearrange("p (h d) -> p h d", h=heads), z3,
                                        tc[:, t, :].unsqueeze(1).to_broadcast([P, heads, DH]), ALU.mult)
                        for g in range(2):
                            for j in range(2):
                                lo = 32 * g + 16 * j
                                sw = 32 * g + 16 * (1 - j)
                                ins = V.tensor_tensor(xs.rearrange("p (h d) -> p h d", h=heads)[:, :, lo:lo + 16],
                                                      z3[:, :, sw:sw + 16],
                                                      ts[:, t, lo:lo + 16].unsqueeze(1).to_broadcast([P, heads, 16]), ALU.mult)
                        then(ins)
                        then(V.tensor_tensor(xc, xc, xs, ALU.add))
                        ins = V.tensor_tensor(z3, xc.rearrange("p (h d) -> p h d", h=heads),
                                              r.unsqueeze(2).to_broadcast([P, heads, DH]), ALU.mult)
                        if heads == 8:
                            then(ins)
                    ins.then_inc(S["ropeq_ready"], 1)
                    dve.wait_ge(S["ropeq_ready"], n("ropeq_ready"))

                def conv(j0, dst):
                    taps = g_conv[l].rearrange("p (j c) -> p j c", j=3)

                    def evac(b, t):
                        u, src = sbufS[:, t % 2, :], bank[t]
                        then(V.tensor_scalar(u, src[:, :], taps[:, 1, j0 + t:j0 + t + 1], None, ALU.mult))
                        then(V.scalar_tensor_tensor(out=u[:, 1:SEQ], in0=src[:, 0:SEQ - 1], scalar=taps[:, 0, j0 + t:j0 + t + 1],
                                                    in1=u[:, 1:SEQ], op0=ALU.mult, op1=ALU.add))
                        V.scalar_tensor_tensor(out=u[:, 0:SEQ - 1], in0=src[:, 1:SEQ], scalar=taps[:, 2, j0 + t:j0 + t + 1],
                                               in1=u[:, 0:SEQ - 1], op0=ALU.mult, op1=ALU.add).then_inc(free[t], 1)
                        evacuated(b, t)
                        dve.wait_ge(S["conv_tanh"], n("conv_tanh"))
                        V.scalar_tensor_tensor(out=dst[:, t, :], in0=sbufPT[:, t % 2, :], scalar=1.0, in1=u,
                                               op0=ALU.add, op1=ALU.mult).then_inc(S["qk_ready"], 1)
                    return evac
                dense(L, "AQ", conv(0, q1), between=rotate)
                dve.wait_ge(S["rowt_done"], l + 1)
                rows_t = bank[TP][:, 0:8 * GATE_ROWS].rearrange("p (t w r) -> p t w r", t=NT, w=2)
                for w, dst in ((0, wcol), (1, mcol)):
                    for d in range(2):
                        ins = V.tensor_copy(dst.rearrange("p (t d h) -> p t d h", t=NT, d=2)[:, :, d, :],
                                            rows_t[:, :, w, 32 * d:32 * d + 4])
                ins.then_inc(S["rowt_read"], 1)
                dense(L, "AK", conv(4, k1))
                n("tp", 5)
                V.memset(v1a[:, :, :, P:P + 1], 1.0).then_inc(S["qk_ready"], 1)
                dense(L, "AV")
                dve.wait_ge(S["mcol_ready"], l + 1)
                for s in range(36):
                    c, j = s // 4, s % 4
                    if c < 8:
                        i, h, back = 32 * l + s, c // 2, c % 2
                        lo, hi = (0, (j + 1) * P) if back else (j * P, SEQ)
                        dve.wait_ge(S["e_done"], i + 1)
                        dve.wait_ge(S["qk_done"], i + 1)
                        if c >= 2:
                            dve.wait_ge(S["o_done"], 32 * l + 4 * (c - 1))
                        V.scalar_tensor_tensor(out=pmat[:, c % 2, j, lo:hi], in0=bank[SC + i % 2][:, lo:hi],
                                               scalar=0.25 * P ** -0.5, in1=sbufS[:, i % 2, lo:hi],
                                               op0=ALU.mult, op1=ALU.mult).then_inc(S["p_done"], 1)
                    if c >= 1:
                        i, h, back = 32 * l + s - 4, (c - 1) // 2, (c - 1) % 2
                        dve.wait_ge(S["o_done"], i + 1)
                        den = bank[PV][:, P:P + 1]
                        col = j * 8 + back * 4 + h
                        then(V.tensor_scalar(hden[:, 0:1], den, -1.0, None, ALU.mult))
                        then(V.scalar_tensor_tensor(out=hden[:, 1:2], in0=den, scalar=mcol[:, col:col + 1],
                                                    in1=hden[:, 0:1], op0=ALU.max, op1=ALU.max))
                        then(V.reciprocal(hden[:, 2:3], hden[:, 1:2]))
                        dst = ytok[:, j, h * P:(h + 1) * P]
                        if back:
                            V.scalar_tensor_tensor(out=dst, in0=bank[PV][:, 0:P], scalar=hden[:, 2:3], in1=dst,
                                                   op0=ALU.mult, op1=ALU.add).then_inc(S["hh_done"], 1)
                        else:
                            V.tensor_scalar(dst, bank[PV][:, 0:P], hden[:, 2:3], None, ALU.mult).then_inc(S["hh_done"], 1)
                        dve.wait_ge(S["hh_done"], i + 1)
                    if s % 4 == 0 and s < 32:
                        split(B("G00", "G01")[s // 16].first_unit + (s // 4) % 4 + LOOK)
                y_g, _, mean = per_group(yflat, yflat, st32c[:, 0:16], 16)
                group_sums(st32c[:, 0:16], yflat, 16)
                then(V.tensor_scalar(st32c[:, 0:16], st32c[:, 0:16], 1.0 / P, None, ALU.mult))
                V.tensor_tensor(y_g, y_g, mean, ALU.subtract).then_inc(S["ms_ready"], 1)
                dense(L, "CQ")
                dve.wait_ge(S["sq_ready"], n("sq_ready"))
                group_sums(st32[:, 0:16], mflat[:, 0:2048], 16)
                V.tensor_scalar(st32[:, 0:16], st32[:, 0:16], 1.0 / P, EPS, ALU.mult, ALU.add).then_inc(S["ms_ready"], 1)
                dve.wait_ge(S["sd_ready"], n("sd_ready"))
                then(V.reciprocal(st32b[:, 0:16], st32[:, 0:16]))
                then(V.tensor_scalar(st32b[:, 0:16], st32b[:, 0:16], 0.5, None, ALU.mult))
                dense(L, "CK")
                dense(L, "CV")

                def ao_evac(b, t):
                    silu(ytok[:, t, :], ytok[:, t, :], b, t)
                    evacuated(b, t)
                    z, _, r = per_group(ytok[:, t, :], ytok[:, t, :], st32b[:, 4 * t:4 * t + 4], 4)
                    V.tensor_tensor(z, z, r, ALU.mult).then_inc(S["y_ready"], 1)
                dense(L, "AO", ao_evac)
                lo_chunks(4, yH, yL, lambda k: g_anorm[l][:, k:k + 1])
                dense(L, "U00", merge(L, 0, 0))
                dense(L, "U01", merge(L, 0, 1))
                softmax(l, gqa_items(), B("G10", "G11"))
                for name in ("DQ", "DK", "DV"):
                    dense(L, name)
                lo_chunks(4, yH, yL, lambda k: 1.0)
                dense(L, "U10", merge(L, 1, 0))
                dense(L, "U11", merge(L, 1, 1))
                softmax(l, nat_items(), B("G20", "G21"))
                lo_chunks(4, yH, yL, lambda k: 1.0)
                dense(L, "U20", merge(L, 2, 0))
                dense(L, "U21", merge(L, 2, 1))
                softmax(l, diff_items(), B("G30", "G31"))
                for t in range(NT):
                    dve.wait_ge(S["sq_ready"], n("sq_ready"))
                    V.tensor_reduce(st32[:, 4 * t:4 * t + 4], sbufPT[:, t % 2, :].rearrange("p (g d) -> p g d", g=4), AX,
                                    ALU.add).then_inc(S["sq_taken"], 1)
                dve.wait_ge(S["sq_taken"], n("sq_taken", NT))
                V.tensor_scalar(st32[:, 0:16], st32[:, 0:16], 1.0 / P, EPS, ALU.mult, ALU.add).then_inc(S["ms_ready"], 1)
                dve.wait_ge(S["sd_ready"], n("sd_ready"))
                then(V.reciprocal(st32b[:, 0:16], st32[:, 0:16]))
                then(V.tensor_scalar(st32b[:, 0:16], st32b[:, 0:16], 1.0 - lambda_init(l), None, ALU.mult))
                for t in range(NT):
                    z, _, r = per_group(ytok[:, t, :], ytok[:, t, :], st32b[:, 4 * t:4 * t + 4], 4)
                    V.tensor_tensor(z, z, r, ALU.mult).then_inc(S["y_ready"], 1)
                lo_chunks(4, yH, yL, lambda k: g_sub[l])
                dense(L, "U30", merge(L, 3, 0))
                dense(L, "U31", merge(L, 3, 1))
                lo_chunks(KD, hH, hL, lambda k: 0.5)
                dense(L, "O0", residual(0))
                dense(L, "O1", residual(1))
                norm_rows(to_xn)
                lo_chunks(KD, hH, hL, lambda k: g_norm[2 + 2 * l][:, k:k + 1])
                for name in ffn_order():
                    if name[:2] == "FG":
                        dense(L, name, lambda b, t: silu(ytok[:, t, :], bank[t][:, :], b, t))
                    elif name[:2] == "FU":
                        def fu_evac(b, t):
                            V.scalar_tensor_tensor(out=sbufS[:, t % 2, :], in0=bank[t][:, :], scalar=0.5,
                                                   in1=ytok[:, t, :], op0=ALU.mult, op1=ALU.mult).then_inc(free[t], 1)
                            dve.wait_ge(S["hid_hi"], n("hid_hi"))
                            V.tensor_tensor(yL[:, t, :], sbufS[:, t % 2, :], yH[:, t, :].bitcast(F32),
                                            ALU.subtract).then_inc(S["hid_ready"], 1)
                        dense(L, name, fu_evac)
                    else:
                        dense(L, name, residual(int(name[3])))
            dve.wait_ge(S["hid_ready"], 0 + n.at("hid_hi"))
            V.memset(rs[:, 2:3], 0.0).then_inc(S["late"], 1)
            dve.wait_ge(S["gp_step"], 16 * 6)
            norm_rows(to_x("x_done"))


def constants():
    i = np.arange(P)
    f = np.float32
    ident = np.eye(P, dtype=f)
    causal = np.where(i[None, :] > i[:, None], f(-BIG), f(0)).astype(f)
    c = np.arange(DH)
    start = np.clip(c - 8, 0, DH - 16)
    inside = (c[None, :] >= start[:, None]) & (c[None, :] < start[:, None] + 16)
    nat = np.where(inside[:, ::-1], f(0), f(-BIG)).astype(f)
    tok = np.arange(SEQ)
    inv = (f(10000.0) ** (-np.arange(16, dtype=f) / f(16))).astype(f)
    ang = [(z.astype(f)[:, None] * inv).astype(f) for z in (tok // 64, tok % 64)]
    cos = np.concatenate([np.cos(z) for z in ang for _ in range(2)], 1).astype(f)
    sin = np.concatenate([s * np.sin(z) for z in ang for s in (-1, 1)], 1).astype(f)
    rope = np.stack([z.reshape(NT, P, DH).transpose(1, 0, 2) for z in (cos, sin)], 1)
    masks = np.zeros((P, LEVELS + 1, P), f)
    s_, t_ = i[:, None], i[None, :]
    for lev in range(LEVELS):
        m = CHUNK >> (lev + 1)
        masks[:, lev] = (s_ // (2 * m) == t_ // (2 * m)) & (s_ % (2 * m) < m) & (t_ % (2 * m) >= m)
    masks[:, LEVELS] = s_ == t_
    slopes = 2.0 ** (-8.0 * np.arange(1, 5) / 4)
    dist = np.abs(np.arange(TABW)[None, :] + i[:, None] - 511)
    alibi = (-(slopes[:, None, None] * dist) / SCALE).astype(f)
    keep4 = np.repeat((t_ >= s_).astype(f)[:, None, :], 4, 1)
    return dict(ident=ident, causal=causal, anti=np.ascontiguousarray(causal.T), nat_mask=np.concatenate([nat, nat], 0),
                rope=rope, level_masks=masks, alibi=alibi, keep4=keep4)


def laid_out(inputs):
    g = {k: np.asarray(v) for k, v in inputs.items()}
    direct = ["x", "w_in", "w_out", "gmlp_ln_g", "gmlp_ln_b", "hgrn_onorm_g", "final_norm_g", "w_in_2", "b_qnorm_g_2",
              "b_knorm_g_2", "d_lambda_q1_2", "d_lambda_k1_2", "d_lambda_q2_2", "d_lambda_k2_2", "w_up_a_2", "w_up_b_2",
              "w_up_c_2", "w_up_d_2", "w_out_2", "w_ffn_gate_2", "w_ffn_up_2", "w_ffn_down_2", "final_g_2"]
    out = {k: g[k] for k in direct}
    out["gmlp_ln_g"] = g["gmlp_ln_g"].reshape(1, 256)
    out["gmlp_ln_b"] = g["gmlp_ln_b"].reshape(1, 256)
    out["norm_gT"] = g["norm_g"][0].reshape(KD, P).T
    out["norm1_gT"] = g["norm1_g_2"].reshape(DEPTH, KD, P).transpose(0, 2, 1)
    out["norm2_gT"] = g["norm2_g_2"].reshape(DEPTH, KD, P).transpose(0, 2, 1)
    out["convT"] = g["a_conv_w_2"].reshape(DEPTH, 3, KD, P).transpose(0, 3, 1, 2).reshape(DEPTH, P, 24)
    gb = g["a_gate_bias_2"].reshape(DEPTH, 2, 2, 4)
    rows = np.zeros((DEPTH, GATE_ROWS, 2), gb.dtype)
    rows[:, 0:4] = gb[:, 0].transpose(0, 2, 1)
    rows[:, 32:36] = gb[:, 1].transpose(0, 2, 1)
    out["gate_biasT"] = rows
    out["a_normT"] = g["a_norm_g_2"].reshape(DEPTH, 4, P).transpose(0, 2, 1)
    out["sublnT"] = g["d_subln_g_2"].reshape(DEPTH, P, 1)
    out["lbT"] = g["hgrn_lb"][0].reshape(2, P).T
    out["fox_bT"] = g["fox_b_f"].reshape(8, 1)
    out["bsT"] = g["gmlp_b_s"][0].T
    out["w_sT"] = g["gmlp_w_s"][0].transpose(2, 0, 1)
    rpb = g["c_rpb_2"].reshape(DEPTH, RPB_LEN)[:, ::-1]
    out["rpb_rev"] = np.pad(rpb, ((0, 0), (RPB_PAD, RPB_PAD)))
    out.update(constants())
    return {k: np.ascontiguousarray(v) for k, v in out.items()}


def kernel(**inputs):
    import concourse.bacc as _bacc
    from concourse.bass_utils import run_bass_kernel_spmd as _run

    nc = _bacc.Bacc("TRN2", target_bir_lowering=False, num_devices=1)
    arrays, aps = {}, {}
    for name, v in laid_out(inputs).items():
        arrays[f"in_{name}_dram"] = v
        aps[name] = nc.dram_tensor(f"in_{name}_dram", v.shape, mybir.dt.from_np(v.dtype), kind="ExternalInput").ap()
    out = nc.dram_tensor("out_0_dram", (1, SEQ, D), F32, kind="ExternalOutput").ap()
    build(nc, aps, out)
    r = _run(nc, [arrays], core_ids=[0])
    return r.results[0]["out_0_dram"]
```

```python
from contextlib import ExitStack

import numpy as np

import concourse.bass as bass
from concourse import mybir

F32 = mybir.dt.float32
F32R = mybir.dt.float32r
BF16 = mybir.dt.bfloat16
U32 = mybir.dt.uint32
ACT = mybir.ActivationFunctionType
ALU = mybir.AluOpType
AX = mybir.AxisListType.X

P = 128
SEQ = 512
NT = SEQ // P
D = 1024
KD = D // P
DEPTH = 2
EPS = 1e-6
BIG = 1e30

W1_COLS = 3848
W2_COLS = 10000
D_FF = 2816
DH = 64
SCALE = DH ** -0.5
HEADS = 8
GELU_C = 0.7978845608028654
GELU_A = 0.044715
CHUNK = 128
LEVELS = 7

RAW_SLOTS = 3
W_SLOTS = 2
TR_BANKS = 4
LOOK = 1
TABW = 896
RPB_PAD = 64
RPB_HEAD = 15 * 31
RPB_LEN = HEADS * RPB_HEAD
GATE_ROWS = 36

SPLIT_ROWS = 64 + GATE_ROWS


class Block:

    def __init__(self, name, weight, row0, kchunks, col0, cols, orient, src="h", gates=False, order=None):
        self.name, self.weight, self.row0, self.kchunks = name, weight, row0, kchunks
        self.col0, self.cols, self.orient, self.src, self.gates = col0, cols, orient, src, gates
        if gates:
            self.banks, self.bank0, self.units = 1, NT - 1, [(0, kchunks)]
        else:
            self.banks, self.bank0 = NT if orient == "tok" else cols // P, 0
            self.units = [(k, 2) for k in order or range(0, kchunks, 2)]


def block1_dense():
    w, o = "w_in", "w_out"
    return {
        "FL": Block("FL", w, 0, KD, 3840, 8, "feat", gates=True),
        "BF": Block("BF", w, 0, KD, 768, 512, "feat"),
        "BI": Block("BI", w, 0, KD, 1280, 512, "tok"),
        "UV": Block("UV", w, 0, KD, 0, 512, "tok"),
        "AZ": Block("AZ", w, 0, KD, 512, 256, "tok"),
        "CQ": Block("CQ", w, 0, KD, 1792, 512, "feat"),
        "CK": Block("CK", w, 0, KD, 2304, 512, "feat"),
        "CV": Block("CV", w, 0, KD, 2816, 512, "tok"),
        "CZ": Block("CZ", w, 0, KD, 3328, 512, "tok"),
        "O0": Block("O0", o, 0, KD, 0, 512, "tok", order=(0, 4, 6, 2)),
        "O1": Block("O1", o, 0, KD, 512, 512, "tok"),
    }


FFN_COLS = [512] * 5 + [256]
COL2 = dict(AQ=0, AK=512, AV=1024, AO=1536, AG=2048, BQ=2064, BKV=2576, CQ=2832, CK=3344,
            CV=3856, DQ=4368, DK=4880, DV=5392, GL=5904)


def block2_dense(l):
    w = f"w_in_2:{l}"
    out = {n: Block(n, w, 0, KD, COL2[n], 512, "feat" if n in ("AQ", "AK", "CQ", "CK", "DQ", "DK") else "tok")
           for n in ("AQ", "AK", "AV", "AO", "BQ", "CQ", "CK", "CV", "DQ", "DK", "DV")}
    out["AG"] = Block("AG", w, 0, KD, COL2["AG"], 16, "feat", gates=True)
    out["BKV"] = Block("BKV", w, 0, KD, COL2["BKV"], 256, "tok")
    for b in range(4):
        for half in range(2):
            out[f"G{b}{half}"] = Block(f"G{b}{half}", w, 0, KD, COL2["GL"] + 1024 * b + 512 * half, 512, "tok")
            out[f"U{b}{half}"] = Block(f"U{b}{half}", f"w_up_{'abcd'[b]}_2:{l}", 0, 4, 512 * half, 512, "tok", "y")
    for half in range(2):
        out[f"O{half}"] = Block(f"O{half}", f"w_out_2:{l}", 0, KD, 512 * half, 512, "tok")
    for f, n in enumerate(FFN_COLS):
        out[f"FG{f}"] = Block(f"FG{f}", f"w_ffn_gate_2:{l}", 0, KD, 512 * f, n, "feat")
        out[f"FU{f}"] = Block(f"FU{f}", f"w_ffn_up_2:{l}", 0, KD, 512 * f, n, "feat")
        for half in range(2):
            out[f"FD{f}{half}"] = Block(f"FD{f}{half}", f"w_ffn_down_2:{l}", 512 * f, n // P, 512 * half, 512,
                                        "tok", "y")
    return out


ORDER1 = ["FL", "BF", "BI", "UV", "AZ", "CQ", "CK", "CV", "CZ", "O0", "O1"]


def ffn_order():
    order = ["FG0", "FU0"]
    for f in range(1, len(FFN_COLS)):
        order += [f"FG{f}", f"FD{f-1}0", f"FD{f-1}1", f"FU{f}"]
    last = len(FFN_COLS) - 1
    return order + [f"FD{last}0", f"FD{last}1"]


ORDER2 = (["AQ", "AG", "BQ", "BKV", "AK", "AV", "G00", "G01", "CQ", "AO", "U00", "U01",
           "CK", "CV", "G10", "G11", "U10", "U11", "DQ", "DK", "G20", "G21", "U20", "U21", "DV", "G30", "G31",
           "U30", "U31", "O0", "O1"] + ffn_order())


def dense_plan():
    blocks = [block1_dense()[n] for n in ORDER1]
    for l in range(DEPTH):
        named = block2_dense(l)
        blocks += [named[n] for n in ORDER2]
    units, groups = [], 0
    used = [0] * NT
    for b in blocks:
        b.first_unit = len(units)
        b.nth = list(used)
        for k0, kn in b.units:
            groups += b.banks
            units.append((b, k0, kn, groups))
        b.groups_end = groups
        for j in range(b.bank0, b.bank0 + b.banks):
            used[j] += 1
    return blocks, units


class Count:

    def __init__(self):
        self.seen = {}

    def __call__(self, name, more=1):
        self.seen[name] = self.seen.get(name, 0) + more
        return self.seen[name]

    def at(self, name):
        return self.seen.get(name, 0)


def fox_items():
    return [dict(kind="fox", h=h, t=t, comp=0, kmax=(t + 1) * P, head=h, q=(h // 2, h % 2), k=(h // 2, h % 2),
                 v=(h * DH, DH), y=h * DH) for h in range(HEADS) for t in range(NT)]


def gqa_items():
    return [dict(kind="gqa", h=h, t=t, comp=0, kmax=SEQ, head=h, q=(h // 2, h % 2), k=(h // 4, h % 2),
                 v=((h // 4) * DH, DH), y=h * DH) for h in range(HEADS) for t in range(NT)]


def nat_items():
    return [dict(kind="nat", h=h, t=t, comp=0, kmax=SEQ, head=h, q=(h // 2, h % 2), k=(h // 2, h % 2),
                 v=(h * DH, DH), y=h * DH) for h in range(HEADS) for t in range(NT)]


def diff_items():
    return [dict(kind="diff", h=h, t=t, comp=c, kmax=SEQ, head=h, q=((4 * c + h) // 2, h % 2),
                 k=((4 * c + h) // 2, h % 2), v=(h * P, P), y=h * P)
            for h in range(4) for c in range(2) for t in range(NT)]


def row_groups(items):
    return [(it["q"], it["k"]) for it in items[::NT]]


def lambda_init(l):
    return 0.8 - 0.6 * float(np.exp(-0.3 * l))


def build(nc, a, out):
    blocks, units = dense_plan()
    by_name = {}
    for i, b in enumerate(blocks):
        l = 0 if i < len(ORDER1) else 1 + (i - len(ORDER1)) // len(ORDER2)
        by_name[(l, b.name)] = b

    ctx = ExitStack()
    with ctx:
        def sb(name, shape, dt=F32):
            return ctx.enter_context(nc.sbuf_tensor(name, shape, dt))

        x = sb("x", [P, NT, D])
        merged = sb("merged", [P, NT, D])
        hH = sb("hH", [P, KD, SEQ], F32R)
        hL = sb("hL", [P, KD, SEQ], F32R)
        yH = sb("yH", [P, 4, SEQ], F32R)
        yL = sb("yL", [P, 4, SEQ], F32R)
        wraw = sb("wraw", [P, RAW_SLOTS, 2 * SEQ])
        wH = sb("wH", [P, W_SLOTS, 2 * SEQ], F32R)
        wL = sb("wL", [P, W_SLOTS, 2 * SEQ], F32R)
        set1 = sb("set1", [P, 6160])
        set2 = sb("set2", [P, 6144])
        gbuf = sb("gbuf", [P, NT, D])
        ytok = sb("ytok", [P, NT, SEQ])
        tab = sb("tab", [P, 2, TABW])
        sbufS = sb("sbufS", [P, 2, SEQ])
        sbufPT = sb("sbufPT", [P, 2, SEQ])
        ident = sb("ident", [P, P])
        ident16 = sb("ident16", [P, P], BF16)
        causal16 = sb("causal16", [P, P], BF16)
        anti16 = sb("anti16", [P, P], BF16)
        row_sel = sb("row_sel", [P, GATE_ROWS], F32R)
        row_nm = sb("row_nm", [P, SEQ], F32R)
        nat_mask = sb("nat_mask", [P, DH])
        rope = sb("rope", [P, 2, NT, DH])
        small = sb("small", [P, 900])

        at = [0]

        def cols(n):
            at[0] += n
            assert at[0] <= 900
            return small[:, at[0] - n:at[0]]

        g_norm = [cols(KD) for _ in range(1 + 2 * DEPTH)]
        g_conv = [cols(24) for _ in range(DEPTH)]
        g_bias = [cols(2) for _ in range(DEPTH)]
        g_anorm = [cols(4) for _ in range(DEPTH)]
        g_sub = [cols(1) for _ in range(DEPTH)]
        g_q = [cols(DH) for _ in range(DEPTH)]
        g_k = [cols(DH) for _ in range(DEPTH)]
        lam = [cols(1) for _ in range(DEPTH)]
        lam_tmp = cols(4)
        lbt = cols(2)
        lb = cols(2)
        oml = cols(2)
        bf_col = cols(1)
        bs_t = cols(4)
        ss0 = cols(NT)
        ss = cols(NT)
        rstd = cols(NT)
        mx = cols(4)
        nm = cols(4)
        lsum = cols(4)
        rs = cols(4)
        onorm = cols(DH)
        st32 = cols(32)
        st32b = cols(32)
        st32c = cols(32)
        wcol = cols(NT * 8)
        mcol = cols(NT * 8)
        hden = cols(4)
        one_col = cols(1)
        st40 = cols(40)
        ebl = cols(8)

        def view(t, off, shape):
            n = int(np.prod(shape))
            v = t[:, off:off + n]
            if len(shape) == 1:
                return v
            names = "abcd"[:len(shape)]
            kw = {names[i]: shape[i] for i in range(len(shape))}
            return v.rearrange("p (" + " ".join(names) + ") -> p " + " ".join(names), **kw)

        xn = merged
        gflat = gbuf[:, :, :].rearrange("p t d -> p (t d)")
        yflat = ytok[:, :, :].rearrange("p t d -> p (t d)")
        tflat = tab[:, :, :].rearrange("p t d -> p (t d)")
        sflat = sbufS[:, :, :].rearrange("p t d -> p (t d)")
        ptflat = sbufPT[:, :, :].rearrange("p t d -> p (t d)")
        mflat = merged[:, :, :].rearrange("p t d -> p (t d)")
        q1, k1, v1 = view(set1, 0, (4, SEQ)), view(set1, 2048, (4, SEQ)), view(set1, 4096, (NT, SEQ))
        v1a = view(set1, 4096, (NT, 4, P + 1))
        q2, k2, v2 = view(set2, 0, (4, SEQ)), view(set2, 2048, (4, SEQ)), view(set2, 4096, (NT, SEQ))
        k2b = view(set2, 2048, (2, SEQ))
        v2b = view(set2, 3072, (NT, P))
        qraw = view(gflat, 0, (NT, SEQ))
        kraw = view(gflat, 2048, (NT, P))
        qs, ks, bb = view(set1, 0, (2, SEQ)), view(set1, 1024, (2, SEQ)), view(set1, 2048, (2, SEQ))
        vi, uu, vv = view(set1, 3072, (NT, 256)), view(set1, 4096, (NT, 256)), view(set1, 5120, (NT, 256))
        ssc = view(yflat, 0, (4, NT, P))

        bank = [ctx.enter_context(nc.psum_tensor(f"bank{i}", [P, SEQ], F32)) for i in range(8)]
        SC, TP, PV = 4, 6, 7

        scaled = [gflat[:, 1024 * i:1024 * i + 1024] for i in range(2)]
        decay = set1[:, 4096:5120]
        ke, qe = view(gflat, 0, (2, SEQ)), view(gflat, 2048, (2, SEQ))
        keT = view(gflat, 1024, (3, 2, P))
        states = view(gflat, 3072, (3, 2, DH))
        row_i, row_f, row_w, row_m = (yflat[0:GATE_ROWS, 512 * i:512 * i + 512] for i in range(4))
        q_split, k_twice, k_low = ([t[:, j, :] for t in (yH, yL)] for j in range(3))
        row_b = gflat[0:GATE_ROWS, 2560:3072]
        cq_t, sq_t, ck_t, sk_t = (view(tflat, 256 * i, (NT, DH)) for i in range(4))
        rope_c, rope_s = gflat[:, 3072:3584], gflat[:, 3584:4096]
        pmat = view(mflat, 0, (2, 4, SEQ))

        names = """
            x_tile0 x_tile1 x_tile2 x_tile3 ident_norm consts masks_ready landed0 landed1 landed2 w_hi w_lo groups free0 free1 free2 free3
            act_step dve_step gp_step
            norm_sq norm_ms norm_sd xn_ready tp_done tp_hi tp_free x_ready x_done
            sc_done hi_done split_done mx_done ex_done pt_done ptev pv_done y_done
            tab_dma0 tab_dma1 mb_done e_done qk_done p_done o_done hh_done
            sq_ready ms_ready sd_ready conv_done conv_tanh qk_ready row_abs row_log rows_ready rowt_done rowt_read mcol_ready
            tanh_ready ropeq_ready y_ready hid_hi hid_ready
            z_ready ez_ready ln_ready lb_ready d_ready ed_ready lvl_ready lvl_done lvl_used
            ke_ready keT_done keT_read upd_done st_ready ho_done ho_read mix_read late gin gsq gin2 sq_taken
            vn_ready mix_done lam_dot lam_exp out_done
        """.split()
        S = {n: ctx.enter_context(nc.semaphore(n)) for n in names}
        landed = [S["landed0"], S["landed1"], S["landed2"]]
        free = [S[f"free{j}"] for j in range(4)]

        block = ctx.enter_context(nc.Block())

        def wsrc(b, k0, kn):
            name, _, l = b.weight.partition(":")
            w = a[name]
            w = w[int(l) if l else 0]
            return w[b.row0 + k0 * P:b.row0 + (k0 + kn) * P, b.col0:b.col0 + b.cols].rearrange(
                "(k p) n -> p k n", p=P)

        def raw_view(u):
            b, k0, kn, _ = units[u]
            return wraw[:, u % RAW_SLOTS, 0:kn * b.cols].rearrange("p (k n) -> p k n", k=kn)

        def w_views(u):
            b, k0, kn, _ = units[u]
            width = P if b.gates else b.cols
            return [w[:, u % W_SLOTS, 0:kn * width].rearrange("p (k n) -> p k n", k=kn) for w in (wH, wL)]

        def gate_parts(u):
            b = units[u][0]
            if b.cols == 8:
                return [(0, 8, 0)]
            return [(0, 4, 0), (64, 4, 4), (32, 4, 8), (96, 4, 12)]

        def bcast_rows(name_ap, n):
            return bass.AP(tensor=name_ap.tensor, offset=name_ap.offset, ap=[[0, P], [1, n]])

        def small_loads():
            out = [(gflat[:, 3072:3200], a["causal"]), (gflat[:, 3200:3328], a["anti"]),
                   (nat_mask[:, :], a["nat_mask"]), (rope[:, :, :, :], a["rope"]),
                   (lbt, a["lbT"]), (bf_col[0:8, :], a["fox_bT"]), (bs_t, a["bsT"])]
            out.append((onorm, bcast_rows(a["hgrn_onorm_g"][0], DH)))
            for l in range(DEPTH):
                out += [(g_norm[1 + 2 * l], a["norm1_gT"][l]), (g_norm[2 + 2 * l], a["norm2_gT"][l]),
                        (g_conv[l], a["convT"][l]), (g_bias[l][0:GATE_ROWS, :], a["gate_biasT"][l]),
                        (g_anorm[l], a["a_normT"][l]), (g_sub[l], a["sublnT"][l]),
                        (g_q[l], bcast_rows(a["b_qnorm_g_2"][l], DH)), (g_k[l], bcast_rows(a["b_knorm_g_2"][l], DH))]
                for i, n in enumerate(("d_lambda_q1_2", "d_lambda_k1_2", "d_lambda_q2_2", "d_lambda_k2_2")):
                    out.append((gflat[:, (4 * l + i) * DH:(4 * l + i + 1) * DH], bcast_rows(a[n][l], DH)))
            out.append((view(tflat, 0, (LEVELS + 1, P)), a["level_masks"]))
            return out

        loads = small_loads()
        CONSTS = 16 * len(loads)

        @block.sync
        def _(sp):
            n = Count()
            for t in range(NT):
                sp.dma_start(x[:, t, :], a["x"][0, t * P:(t + 1) * P, :]).then_inc(S[f"x_tile{t}"], 16)
            sp.dma_start(ident[:, :], a["ident"]).then_inc(S["ident_norm"], 16)
            sp.dma_start(g_norm[0], a["norm_gT"]).then_inc(S["ident_norm"], 16)

            def weight(u):
                b, k0, kn, _ = units[u]
                if u >= RAW_SLOTS:
                    sp.wait_ge(S["w_lo"], u - RAW_SLOTS + 1)
                sp.dma_start(raw_view(u), wsrc(b, k0, kn)).then_inc(landed[u % RAW_SLOTS], 16)

            for u in range(RAW_SLOTS):
                weight(u)
            for dst, src in loads:
                sp.dma_start(dst, src).then_inc(S["consts"], 16)
            for u in range(RAW_SLOTS, len(units)):
                weight(u)
            for t in range(NT):
                sp.wait_ge(S["x_done"], t + 1)
                sp.dma_start(out[0, t * P:(t + 1) * P, :], x[:, t, :]).then_inc(S["out_done"], 16)
            sp.wait_ge(S["out_done"], 16 * NT)

        @block.gpsimd
        def _(pool):
            pool.wait_ge(S["late"], 1)
            pool.dma_start(view(gflat, 0, (4, P)), a["w_sT"]).then_inc(S["gp_step"], 16)
            for i, name in enumerate(("gmlp_ln_g", "gmlp_ln_b")):
                pool.dma_start(gflat[:, 512 + 256 * i:768 + 256 * i], bcast_rows(a[name][0], 256)).then_inc(
                    S["gp_step"], 16)
            pool.dma_start(view(gflat, 1024, (4, P)), a["keep4"]).then_inc(S["gp_step"], 16)
            pool.wait_ge(S["y_ready"], 1)
            pool.dma_start(yflat[:, 0:D], bcast_rows(a["final_norm_g"], D)).then_inc(S["gp_step"], 16)
            for l in range(DEPTH):
                gqa0 = 32 + 96 * l
                nat0, diff0 = gqa0 + 32, gqa0 + 64
                for h in range(HEADS):
                    pool.wait_ge(S["mx_done"], gqa0 + 1 if h < 2 else nat0 + 4 * (h - 1))
                    for half in range(2):
                        off = l * (RPB_LEN + 2 * RPB_PAD) + RPB_PAD + RPB_LEN - 1 - RPB_HEAD * h - (14 - half) * 31 - 78
                        src = bass.AP(tensor=a["rpb_rev"].tensor, offset=off, ap=[[1, 64], [31, 14], [1, 64]])
                        pool.dma_start(tab[64 * half:64 * half + 64, h % 2, :].rearrange("p (e k) -> p e k", e=14),
                                       src).then_inc(S[f"tab_dma{h % 2}"], 16)
                for h in range(4):
                    pool.wait_ge(S["mx_done"], nat0 + 28 + 4 * h if h < 2 else diff0 + 8 * (h - 1))
                    pool.dma_start(tab[:, h % 2, :], a["alibi"][h]).then_inc(S[f"tab_dma{h % 2}"], 16)
            pool.wait_ge(S["late"], 2)
            pool.dma_start(yflat[:, 0:D], bcast_rows(a["final_g_2"], D)).then_inc(S["gp_step"], 16)

        @block.tensor
        def _(pe):
            n = Count()
            unit = [0]

            def group(b, i, t):
                u = b.first_unit + i
                _, k0, kn, _ = units[u]
                if t == 0:
                    pe.wait_ge(S["w_lo"], u + 1)
                if i == 0 and b.nth[b.bank0 + t]:
                    pe.wait_ge(free[b.bank0 + t], b.nth[b.bank0 + t])
                H, L = (hH, hL) if b.src == "h" else (yH, yL)
                vh, vl = w_views(u)
                for kk in range(kn):
                    k = k0 + kk
                    for j in range(3):
                        act_part = (H, L, H)[j]
                        w_part = (vh, vh, vl)[j]
                        first = i == 0 and kk == 0 and j == 0
                        last = i == len(b.units) - 1 and kk == kn - 1 and j == 2
                        if b.orient == "tok":
                            mm = pe.matmul(bank[t][:, 0:b.cols], act_part[:, k, t * P:(t + 1) * P], w_part[:, kk, :],
                                           start=first, stop=last)
                        else:
                            mm = pe.matmul(bank[b.bank0 + t][:, :], w_part[:, kk, t * P:(t + 1) * P], act_part[:, k, :],
                                           start=first, stop=last)
                mm.then_inc(S["groups"], 1)

            def dense(l, name, fresh=0, between=None):
                b = by_name[(l, name)]
                chunk = n.at("tp") - fresh
                for i, (_, kn) in enumerate(b.units):
                    chunk += kn
                    if fresh:
                        pe.wait_ge(S["tp_free"], chunk)
                    for t in range(b.banks):
                        group(b, i, t)
                    if between:
                        between(i)

            def transposes(src, chunks, ready, count, each=0):
                if count:
                    pe.wait_ge(S[ready], n(ready, count))
                for k in chunks if isinstance(chunks, tuple) else range(chunks):
                    if each:
                        pe.wait_ge(S[ready], n(ready, each))
                    i = n("tp") - 1
                    if i >= TR_BANKS:
                        pe.wait_ge(S["tp_free"], i - TR_BANKS + 1)
                    for t in range(NT):
                        mm = pe.transpose(bank[SC + i % TR_BANKS][:, t * P:(t + 1) * P], src[:, t, k * P:(k + 1) * P],
                                          ident[:, :])
                    mm.then_inc(S["tp_done"], 1)

            def xn_transposes():
                transposes(xn, (0, 1, 2, 3), "xn_ready", NT)
                transposes(xn, (4, 5, 6, 7), "xn_ready", NT)

            def softmax(items, v, beside, q=None, k=None, extra=None):
                i0 = n("items", len(items)) - len(items)
                side = [(b, i, t) for b in beside for i in range(len(b.units)) for t in range(NT)]
                pe.wait_ge(S["tp_free"], n.at("tp"))
                fox = items[0]["kind"] == "fox"
                for s in range(max(len(items) + 2, len(side))):
                    if s < len(items):
                        it, i = items[s], i0 + s
                        if i >= 2:
                            pe.wait_ge(S["ex_done"], i - 1)
                        r = slice(DH * it["q"][1], DH * it["q"][1] + DH)
                        kmax, dst = it["kmax"], bank[SC + i % 2]
                        tok = slice(it["t"] * P, (it["t"] + 1) * P)
                        if not fox:
                            slot = (s // NT) % 2
                            if s % NT == 0:
                                pe.wait_ge(S["split_done"], n("split_done"))
                            pe.matmul(dst[:, :], q_split[slot][:, tok], k_twice[slot], start=True, stop=False)
                            mm = pe.matmul(dst[:, :], q_split[slot][r, tok], k_low[slot][r, :], start=False, stop=True)
                        else:
                            pe.matmul(dst[:, 0:kmax], q[r, it["q"][0], tok], k[r, it["k"][0], 0:kmax], start=True,
                                      stop=False)
                            pe.matmul(dst[:, 0:kmax], row_sel[0:SPLIT_ROWS, it["h"]:it["h"] + 1].to_broadcast(
                                [SPLIT_ROWS, P]), row_nm[0:SPLIT_ROWS, 0:kmax], start=False, stop=True)
                            mm = pe.matmul(dst[:, kmax - P:kmax], ident16[:, :], causal16[:, :], start=False, stop=True,
                                           skip_group_check=True)
                        mm.then_inc(S["sc_done"], 1)
                    if s < len(side):
                        group(*side[s])
                    if extra:
                        extra(s)
                    if 1 <= s <= len(items):
                        it, i = items[s - 1], i0 + s - 1
                        pe.wait_ge(S["ex_done"], i + 1)
                        if i >= 1:
                            pe.wait_ge(S["ptev"], i)
                        for c in range(it["kmax"] // P):
                            mm = pe.transpose(bank[TP][:, c * P:(c + 1) * P], sbufS[:, i % 2, c * P:(c + 1) * P],
                                              ident[:, :])
                        mm.then_inc(S["pt_done"], 1)
                    if 2 <= s < len(items) + 2:
                        it, i = items[s - 2], i0 + s - 2
                        pe.wait_ge(S["ptev"], i + 1)
                        if i >= 1:
                            pe.wait_ge(S["y_done"], i)
                        nk = it["kmax"] // P
                        c0, w = it["v"]
                        for c in range(nk):
                            mm = pe.matmul(bank[PV][:, 0:w], sbufPT[:, i % 2, c * P:(c + 1) * P],
                                           v[:, c, c0:c0 + w], start=c == 0, stop=c == nk - 1)
                        mm.then_inc(S["pv_done"], 1)

            def evacuated(b):
                for j in range(b.banks):
                    pe.wait_ge(free[j], b.nth[j] + 1)

            def mlstm(l, beside):
                side = [(b, i, t) for b in beside for i in range(4) for t in range(NT)]
                i0 = 32 * l
                for s in range(36):
                    c, j = s // 4, s % 4
                    if c < 8:
                        i, h, back = i0 + s, c // 2, c % 2
                        lo, hi = (0, (j + 1) * P) if back else (j * P, SEQ)
                        row = 32 * back + h
                        if i >= 1:
                            pe.wait_ge(S["e_done"], i)
                        pe.matmul(bank[TP][:, lo:hi], row_sel[0:SPLIT_ROWS, row:row + 1].to_broadcast([SPLIT_ROWS, P]),
                                  row_nm[0:SPLIT_ROWS, lo:hi], start=True, stop=True)
                        pe.matmul(bank[TP][:, j * P:(j + 1) * P], ident16[:, :], (causal16 if back else anti16)[:, :],
                                  start=False, stop=True, skip_group_check=True).then_inc(S["mb_done"], 1)
                        if i >= 2:
                            pe.wait_ge(S["p_done"], i - 1)
                        if s % 8 == 0:
                            pe.wait_ge(S["qk_ready"], 9 * l + 6 + h)
                        pe.matmul(bank[SC + i % 2][:, lo:hi], k1[:, h, j * P:(j + 1) * P], q1[:, h, lo:hi],
                                  start=True, stop=True).then_inc(S["qk_done"], 1)
                    if s < len(side):
                        group(*side[s])
                    if c >= 1:
                        i, h, back = i0 + s - 4, (c - 1) // 2, (c - 1) % 2
                        pe.wait_ge(S["p_done"], i0 + 4 * c)
                        if s == 4:
                            evacuated(by_name[(l + 1, "AV")])
                        tail = s > 32
                        if tail:
                            pe.wait_ge(S["e_done"], i0 + 32)
                        if i >= 1:
                            pe.wait_ge(S["hh_done"], i - 1 if tail else i)
                        dst = bank[PV - (s % 2 if tail else 0)]
                        srcs = range(j, NT) if back else range(j + 1)
                        for sj in srcs:
                            mm = pe.matmul(dst[:, 0:P + 1], pmat[:, (c - 1) % 2, sj, j * P:(j + 1) * P],
                                           v1a[:, sj, h, :], start=sj == srcs[0], stop=sj == srcs[-1])
                        mm.then_inc(S["o_done"], 1)

            def hgrn_keys():
                pe.wait_ge(S["mix_read"], 1)
                pe.wait_ge(S["ke_ready"], 1)
                for m in range(3):
                    for g in range(2):
                        mm = pe.transpose(bank[TP + m // 2][:, (2 * (m % 2) + g) * P:(2 * (m % 2) + g + 1) * P],
                                          ke[:, g, m * P:(m + 1) * P], ident[:, :])
                    mm.then_inc(S["keT_done"], 1)

            def hgrn_scores(s):
                if s >= 4 * (LEVELS + 1):
                    return
                if s == 0:
                    evacuated(by_name[(0, "CZ")])
                if s == 1:
                    pe.wait_ge(S["keT_read"], 2)
                    for m in range(3):
                        for g in range(2):
                            mm = pe.matmul(bank[2 + m // 2][:, (2 * (m % 2) + g) * P:(2 * (m % 2) + g + 1) * P],
                                           keT[:, m, g, :], vi[:, m, g * P:(g + 1) * P], start=True, stop=True)
                        mm.then_inc(S["upd_done"], 1)
                if s == 2:
                    pe.wait_ge(S["st_ready"], 1)
                lev, h = s // 4, s % 4
                if lev < LEVELS:
                    pe.wait_ge(S["lvl_ready"], lev + 1)
                if s >= 4:
                    pe.wait_ge(S["lvl_used"], s - 3)
                r = slice(DH * (h % 2), DH * (h % 2) + DH)
                both = scaled[lev % 2].rearrange("p (g t) -> p g t", g=2)
                ql, kl = (both, both) if lev < LEVELS else (qs, ks)
                for m in range(NT):
                    tok = slice(m * P, (m + 1) * P)
                    mm = pe.matmul(bank[s % 4][:, tok], kl[r, h // 2, tok], ql[r, h // 2, tok], start=True, stop=True)
                mm.then_inc(S["lvl_done"], 1)

            def hgrn_out():
                pe.wait_ge(S["lvl_used"], 4 * (LEVELS + 1))
                for m in range(NT):
                    if m >= 2:
                        pe.wait_ge(S["ho_read"], 2 * (m - 1))
                    tok = slice(m * P, (m + 1) * P)
                    for h in range(4):
                        r = slice(DH * (h % 2), DH * (h % 2) + DH)
                        dst = bank[2 * (m % 2) + h % 2][:, (h // 2) * DH:(h // 2 + 1) * DH]
                        mm = pe.matmul(dst, ssc[:, h, m, :], vi[:, m, h * DH:(h + 1) * DH], start=True, stop=m == 0)
                        if m:
                            mm = pe.matmul(dst, qe[r, h // 2, tok], states[r, m - 1, h // 2, :],
                                           start=False, stop=True)
                    mm.then_inc(S["ho_done"], 1)

            def gmlp():
                pe.wait_ge(S["vn_ready"], 1)
                for g in range(4):
                    mm = pe.matmul(bank[TP + g // 2][:, (g % 2) * 256:(g % 2) * 256 + 256],
                                   gflat[:, g * P:(g + 1) * P], vv[:, :, g * DH:(g + 1) * DH], start=True, stop=True)
                    mm.then_inc(S["mix_done"], 1)

            pe.wait_ge(S["ident_norm"], 32)
            xn_transposes()
            dense(0, "FL", KD)
            for name in ORDER1[1:7]:
                dense(0, name)
            gmlp()
            dense(0, "CV")
            hgrn_keys()
            dense(0, "CZ")
            for name in ("CQ", "CK", "CV"):
                evacuated(by_name[(0, name)])
            pe.wait_ge(S["masks_ready"], 1)
            softmax(fox_items(), v2, [], q2, k2, hgrn_scores)
            hgrn_out()
            pe.wait_ge(S["y_done"], n.at("items"))
            transposes(merged, (0, 1, 4, 5, 6, 7), None, 0)
            pe.wait_ge(S["ho_read"], 2 * NT)

            def late_transposes(i):
                if i == 2:
                    transposes(merged, (2, 3), "y_ready", 1)
            dense(0, "O0", 6, late_transposes)
            dense(0, "O1")

            for l in range(DEPTH):
                L = l + 1

                def B(*names):
                    return [by_name[(L, name)] for name in names]

                xn_transposes()
                dense(L, "AQ", KD)
                dense(L, "AG")
                dense(L, "BQ")
                dense(L, "BKV")
                pe.wait_ge(S["rows_ready"], l + 1)
                for t in range(NT):
                    for w, row in enumerate((row_w, row_m)):
                        mm = pe.transpose(bank[TP][:, (2 * t + w) * GATE_ROWS:(2 * t + w + 1) * GATE_ROWS],
                                          row[:, t * P:(t + 1) * P], ident[0:GATE_ROWS, 0:GATE_ROWS])
                mm.then_inc(S["rowt_done"], 1)
                dense(L, "AK")

                def b_transposes(i):
                    if i == 1:
                        pe.wait_ge(S["rowt_read"], l + 1)
                        transposes(qraw, 4, "ropeq_ready", NT)
                    elif i == 2:
                        transposes(kraw, 1, None, 0)
                dense(L, "AV", between=b_transposes)
                pe.wait_ge(S["tp_free"], n.at("tp"))
                mlstm(l, B("G00", "G01"))
                dense(L, "CQ")
                dense(L, "AO")
                transposes(ytok, 4, "y_ready", NT)
                dense(L, "U00", 4)
                dense(L, "U01")
                dense(L, "CK")
                dense(L, "CV")
                softmax(gqa_items(), v2b, B("G10", "G11"))
                pe.wait_ge(S["y_done"], n.at("items"))
                transposes(ytok, 4, None, 0)
                dense(L, "U10", 4)
                dense(L, "U11")
                dense(L, "DQ")
                dense(L, "DK")
                evacuated(B("CV")[0])
                softmax(nat_items(), v1, B("G20", "G21"))
                pe.wait_ge(S["y_done"], n.at("items"))
                transposes(ytok, 4, None, 0)
                dense(L, "U20", 4)
                dense(L, "U21")
                dense(L, "DV")
                evacuated(B("DV")[0])
                softmax(diff_items(), v2, B("G30", "G31"))
                transposes(ytok, 4, "y_ready", 0, each=1)
                dense(L, "U30", 4)
                dense(L, "U31")
                transposes(merged, (0, 1, 2, 3), "y_ready", NT)
                transposes(merged, (4, 5, 6, 7), "y_ready", NT)
                dense(L, "O0", KD)
                dense(L, "O1")
                xn_transposes()
                for name in ffn_order():
                    if name.startswith("FD") and name.endswith("0"):
                        banks = B("FU" + name[2])[0].banks
                        pe.wait_ge(S["hid_ready"], n("hid_ready", banks))
                    dense(L, name, KD if name == "FG0" else 0)

        @block.scalar
        def _(act):
            n = Count()
            A = nc.scalar.activation

            def step(ins):
                ins.then_inc(S["act_step"], 1)
                act.wait_ge(S["act_step"], n("act_step"))

            def split(u):
                if u >= len(units):
                    return
                b, k0, kn, _ = units[u]
                act.wait_ge(landed[u % RAW_SLOTS], 16 * (u // RAW_SLOTS + 1))
                if u >= W_SLOTS:
                    act.wait_ge(S["groups"], units[u - W_SLOTS][3])
                if b.gates:
                    act.wait_ge(S["gin"], n("gin"))
                    raw, (hi, _lo) = raw_view(u), w_views(u)
                    for c, w, r in gate_parts(u):
                        ins = A(hi[:, :, c:c + w], raw[:, :, r:r + w], ACT.Copy)
                    ins.then_inc(S["w_hi"], 1)
                else:
                    width = kn * b.cols
                    A(wH[:, u % W_SLOTS, 0:width], wraw[:, u % RAW_SLOTS, 0:width], ACT.Copy).then_inc(S["w_hi"], 1)

            def ready(b, t):
                act.wait_ge(S["groups"], b.groups_end - (b.banks - 1 - t))

            def dense(l, name, evac=None, between=None):
                b = by_name[(l, name)]
                for i in range(len(b.units)):
                    split(b.first_unit + i + LOOK)
                    if between:
                        between(i)
                if evac:
                    for t in range(b.banks):
                        ready(b, t)
                        evac(b, t)

            def copy_to(dst):
                def evac(b, t):
                    A(dst(t), bank[t][:, 0:b.cols] if b.orient == "tok" else bank[t][:, :], ACT.Copy).then_inc(free[t], 1)
                return evac

            taken = []

            def scratch_free():
                if len(taken) >= 2:
                    b, t = taken[-2]
                    act.wait_ge(free[t], b.nth[t] + 1)

            def tanh_half(b, t, cols):
                scratch_free()
                src = bank[t][:, cols]
                A(sbufPT[:, len(taken) % 2, 0:src.shape[1]], src, ACT.Tanh, scale=0.5).then_inc(S["tanh_ready"], 1)
                taken.append((b, t))

            def square(t, half):
                A(sflat[:, 0:SEQ], x[:, t, half * SEQ:(half + 1) * SEQ], ACT.Square,
                  accum_out=(ss0, ss)[half][:, t:t + 1]).then_inc(S["norm_sq"], 1)
                act.wait_ge(S["norm_sq"], n("norm_sq"))

            def rms(source, halves=(0, 1)):
                for t in range(NT):
                    source(t)
                    for half in halves:
                        square(t, half)
                    if t == NT - 2:
                        act.wait_ge(S["norm_ms"], n("norm_ms"))
                        A(ss[:, 0:NT - 1], ss[:, 0:NT - 1], ACT.Sqrt).then_inc(S["norm_sd"], 1)
                act.wait_ge(S["norm_ms"], n("norm_ms"))
                A(ss[:, NT - 1:NT], ss[:, NT - 1:NT], ACT.Sqrt).then_inc(S["norm_sd"], 1)

            def first_half(b):
                def between(i):
                    if i == 0:
                        for t in range(NT):
                            act.wait_ge(free[t], b.nth[t] + 1)
                            square(t, 0)
                return between

            def after(b):
                return lambda t: act.wait_ge(free[t], b.nth[t] + 1)

            def hi_chunks(chunks, dst, scale):
                for k in chunks if isinstance(chunks, tuple) else range(chunks):
                    i = n("tp") - 1
                    act.wait_ge(S["tp_done"], i + 1)
                    A(dst[:, k, :], bank[SC + i % TR_BANKS][:, :], ACT.Copy, scale=scale(k)).then_inc(S["tp_hi"], 1)

            def gates(b, s):
                side = [(bb, i, t) for bb in b for i in range(4) for t in range(NT)]
                if s < len(side):
                    bb, i, t = side[s]
                    if t == 0:
                        split(bb.first_unit + i + LOOK)
                    if i == 3:
                        half = b.index(bb)
                        ready(bb, t)
                        A(gbuf[:, t, half * SEQ:(half + 1) * SEQ], bank[t][:, :], ACT.Tanh, scale=0.5).then_inc(
                            free[t], 1)

            def split_rows(items, g, q, k, blocks=(), after=None):
                for b in blocks:
                    for t in range(b.banks):
                        act.wait_ge(free[t], b.nth[t] + 1)
                (qi, half), (ki, _) = row_groups(items)[g]
                r = slice(DH * half, DH * half + DH)
                if g < 2:
                    act.wait_ge(S["groups"], after.groups_end)
                else:
                    act.wait_ge(S["sc_done"], n.at("items") - len(items) + NT * (g - 1))
                A(q_split[g % 2][r, :], q[r, qi, :], ACT.Copy)
                A(k_twice[g % 2][0:DH, :], k[r, ki, :], ACT.Copy)
                A(k_twice[g % 2][DH:P, :], k[r, ki, :], ACT.Copy).then_inc(S["hi_done"], 1)

            def first_rows(items, q, k, blocks, after):
                def between(i):
                    if i >= 2:
                        split_rows(items, i - 2, q, k, blocks, after)
                return between

            def softmax(items, beside, q=None, k=None, extra=None):
                i0 = n("items", len(items)) - len(items)
                for s in range(max(len(items) + 2, 32 if beside else 0)):
                    if beside and s % NT == 1 and NT < s < len(items) - NT:
                        split_rows(items, s // NT + 1, q, k)
                    if s < len(items):
                        it, i = items[s], i0 + s
                        act.wait_ge(S["mx_done"], i + 1)
                        if i >= 2:
                            act.wait_ge(S["pt_done"], i - 1)
                        if i >= 4:
                            act.wait_ge(S["y_done"], i - 3)
                        kmax = it["kmax"]
                        biased = it["kind"] in ("nat", "diff")
                        src = sbufS[:, i % 2, 0:kmax] if biased else bank[SC + i % 2][:, 0:kmax]
                        A(sbufS[:, i % 2, 0:kmax], src, ACT.Exp, bias=nm[:, i % 4:i % 4 + 1],
                          scale=1.0 if biased else SCALE, accum_out=lsum[:, i % 4:i % 4 + 1]).then_inc(S["ex_done"], 1)
                    if 1 <= s <= len(items):
                        it, i = items[s - 1], i0 + s - 1
                        act.wait_ge(S["pt_done"], i + 1)
                        if i >= 2:
                            act.wait_ge(S["pv_done"], i - 1)
                        A(sbufPT[:, i % 2, 0:it["kmax"]], bank[TP][:, 0:it["kmax"]], ACT.Copy).then_inc(S["ptev"], 1)
                    if beside:
                        gates(beside, s)
                    if extra:
                        extra(s)

            rms(lambda t: act.wait_ge(S[f"x_tile{t}"], 16))
            for u in range(LOOK):
                split(u)
            act.wait_ge(S["ident_norm"], 32)
            hi_chunks(KD, hH, lambda k: g_norm[0][:, k:k + 1])

            def lambdas(i):
                act.wait_ge(S["lam_dot"], 1)
                A(lam_tmp, lam_tmp, ACT.Exp).then_inc(S["lam_exp"], 1)
                A(lb, lb, ACT.Exp).then_inc(S["lb_ready"], 1)
            dense(0, "FL", between=lambdas)
            act.wait_ge(S["row_abs"], n("row_abs"))
            step(A(yflat[0:8, 1024:1536], yflat[0:8, 512:1024], ACT.Exp, scale=-1.0))
            A(yflat[0:8, 1024:1536], yflat[0:8, 1024:1536], ACT.Ln, bias=1.0).then_inc(S["row_log"], 1)

            def bf_evac(b, t):
                if t < 2:
                    tanh_half(b, t, slice(0, SEQ))
            dense(0, "BF", bf_evac)

            def gate_exp(i):
                if i == 0:
                    act.wait_ge(S["z_ready"], 1)
                    A(gflat[:, 1024:2048], gflat[:, 0:1024], ACT.Exp, scale=-1.0).then_inc(S["ez_ready"], 1)

            def gate_ln(i):
                if i == 0:
                    act.wait_ge(S["z_ready"], 2)
                    A(gflat[:, 2048:3072], gflat[:, 2048:3072], ACT.Ln).then_inc(S["ln_ready"], 1)
                    A(gflat[:, 3072:4096], gflat[:, 3072:4096], ACT.Ln).then_inc(S["ln_ready"], 1)

            def bi_evac(b, t):
                A(vi[:, t, :], bank[t][:, 0:256], ACT.Copy)
                tanh_half(b, t, slice(256, 512))
            dense(0, "BI", bi_evac, between=gate_exp)

            dense(0, "UV", between=gate_ln)
            uv = by_name[(0, "UV")]
            for t in range(NT + 1):
                if t < NT:
                    ready(uv, t)
                    if t >= 2:
                        act.wait_ge(S["tanh_ready"], len(taken))
                    else:
                        scratch_free()
                    A(sbufS[:, t % 2, :], bank[t][:, :], ACT.Square).then_inc(S["gsq"], 1)
                if t >= 1:
                    act.wait_ge(S["gin2"], n("gin2"))
                    scratch_free()
                    A(sbufPT[:, len(taken) % 2, :], sbufS[:, (t - 1) % 2, :], ACT.Tanh, scale=GELU_C).then_inc(
                        S["tanh_ready"], 1)
                    taken.append((uv, t - 1))

            dense(0, "AZ", lambda b, t: tanh_half(b, t, slice(0, 256)))
            def v_norm(i):
                if i == 0:
                    act.wait_ge(S["ms_ready"], n("ms_ready"))
                    A(ptflat, vv, ACT.Square).then_inc(S["sq_ready"], 1)
                    n("sq_ready")
                elif i == 1:
                    act.wait_ge(S["ms_ready"], n("ms_ready"))
                    A(st32[:, 0:16], st32[:, 0:16], ACT.Sqrt).then_inc(S["sd_ready"], 1)

            def chunk_decays(i):
                if i == 1:
                    act.wait_ge(S["d_ready"], 1)
                    A(qe, bb, ACT.Exp)
                    A(ke, ke, ACT.Exp).then_inc(S["ed_ready"], 1)

            def keys_and_level0(i):
                if i == 0:
                    act.wait_ge(S["keT_done"], 3)
                    A(gflat[:, 1024:1536], bank[TP][:, :], ACT.Copy).then_inc(S["keT_read"], 1)
                    A(gflat[:, 1536:1792], bank[PV][:, 0:256], ACT.Copy).then_inc(S["keT_read"], 1)
                elif i == 1:
                    level_decays(0)

            def level_decays(lev):
                act.wait_ge(S["d_ready"], lev + 2)
                A(decay, decay, ACT.Exp).then_inc(S["ed_ready"], 1)

            dense(0, "CQ", copy_to(lambda t: q2[:, t, :]), between=v_norm)
            dense(0, "CK", copy_to(lambda t: k2[:, t, :]))
            dense(0, "CV", copy_to(lambda t: v2[:, t, :]), between=chunk_decays)
            dense(0, "CZ", lambda b, t: tanh_half(b, t, slice(0, SEQ)), between=keys_and_level0)

            def next_level(s):
                if s % 4 == 0 and s // 4 + 1 < LEVELS:
                    level_decays(s // 4 + 1)
            softmax(fox_items(), [], extra=next_level)
            for m in range(NT):
                act.wait_ge(S["ho_done"], m + 1)
                for half in range(2):
                    A(sflat[:, m * 256:(m + 1) * 256].rearrange("p (g h d) -> p g h d", g=2, h=2)[:, :, half, :],
                      bank[2 * (m % 2) + half][:, 0:2 * DH].rearrange("p (g d) -> p g d", g=2),
                      ACT.Copy).then_inc(S["ho_read"], 1)
            hi_chunks((0, 1), hH, lambda k: 0.5)
            act.wait_ge(S["ho_read"], 2 * NT)
            A(ptflat, sflat, ACT.Square).then_inc(S["sq_ready"], 1)
            n("sq_ready")
            hi_chunks((4, 5, 6, 7), hH, lambda k: 0.5)

            def late_chunks(i):
                if i == 0:
                    act.wait_ge(S["ms_ready"], n("ms_ready"))
                    A(st32[:, 0:16], st32[:, 0:16], ACT.Sqrt).then_inc(S["sd_ready"], 1)
                elif i == 2:
                    hi_chunks((2, 3), hH, lambda k: 0.5)
            dense(0, "O0", between=late_chunks)
            dense(0, "O1", between=first_half(by_name[(0, "O0")]))
            rms(after(by_name[(0, "O1")]), (1,))

            for l in range(DEPTH):
                L = l + 1

                def B(*names):
                    return [by_name[(L, name)] for name in names]

                if l == 0:
                    rms(lambda t: act.wait_ge(S["x_ready"], t + 1))
                else:
                    rms(after(by_name[(l, ffn_order()[-1])]), (1,))
                hi_chunks(KD, hH, lambda k: g_norm[1 + 2 * l][:, k:k + 1])
                dense(L, "AQ", copy_to(lambda t: q1[:, t, :]))
                dense(L, "AG")

                def conv_tanh(i):
                    slot = (n("conv_done") - 1) % 2
                    act.wait_ge(S["conv_done"], n.at("conv_done"))
                    A(sbufPT[:, slot, :], sbufS[:, slot, :], ACT.Tanh, scale=0.5).then_inc(S["conv_tanh"], 1)

                def rows_and_conv(i):
                    if i == 0:
                        act.wait_ge(S["row_abs"], n("row_abs"))
                        step(A(row_m, row_w, ACT.Exp, scale=-1.0))
                        A(row_m, row_m, ACT.Ln, bias=1.0).then_inc(S["row_log"], 1)
                    conv_tanh(i)
                dense(L, "BQ", copy_to(lambda t: qraw[:, t, :]), between=rows_and_conv)

                def bkv_evac(b, t):
                    A(kraw[:, t, :], bank[t][:, 0:P], ACT.Copy)
                    A(v2b[:, t, :], bank[t][:, P:2 * P], ACT.Copy).then_inc(free[t], 1)
                def q_squares(i):
                    if i == 1:
                        act.wait_ge(S["qk_ready"], 9 * l + 5)
                    if i in (1, 3):
                        for t in (i - 1, i):
                            if t >= 2:
                                act.wait_ge(S["sq_taken"], n("sq_taken"))
                            else:
                                act.wait_ge(free[t + 2], by_name[(L, "BQ")].nth[t + 2] + 1)
                            A(sbufS[:, t % 2, :], qraw[:, t, :], ACT.Square).then_inc(S["sq_ready"], 1)
                dense(L, "BKV", bkv_evac, between=q_squares)
                n("sq_taken", 2)

                def squares(i):
                    if i == 0:
                        act.wait_ge(free[NT - 1], by_name[(L, "BKV")].nth[NT - 1] + 1)
                        A(sbufPT[:, 0, :], gflat[:, 2048:2560], ACT.Square).then_inc(S["sq_ready"], 1)
                        act.wait_ge(S["ms_ready"], n("ms_ready"))
                        A(st40, st40, ACT.Sqrt).then_inc(S["sd_ready"], 1)
                    elif i == 1:
                        act.wait_ge(S["rowt_read"], l + 1)
                        A(mcol, mcol, ACT.Exp).then_inc(S["mcol_ready"], 1)
                dense(L, "AK", copy_to(lambda t: k1[:, t, :]), between=squares)

                def av_between(i):
                    if i < 3:
                        conv_tanh(i)
                    if i == 1:
                        for k in range(4):
                            c = n("tp") - 1
                            act.wait_ge(S["tp_done"], c + 1)
                            A(q2[:, k, :], bank[SC + c % TR_BANKS][:, :], ACT.Copy).then_inc(S["tp_free"], 1)
                    elif i == 2:
                        c = n("tp") - 1
                        act.wait_ge(S["tp_done"], c + 1)
                        for g in range(2):
                            for half in range(2):
                                ins = A(k2b[64 * half:64 * half + 64, g, :],
                                        bank[SC + c % TR_BANKS][64 * g:64 * g + 64, :], ACT.Copy)
                                if (g, half) != (1, 1):
                                    step(ins)
                        ins.then_inc(S["tp_free"], 1)
                        conv_tanh(i)
                dense(L, "AV", lambda b, t: A(v1a[:, t, :, 0:P], bank[t][:, :].rearrange("p (h d) -> p h d", h=4),
                                              ACT.Copy).then_inc(free[t], 1), between=av_between)
                for s in range(36):
                    c, j = s // 4, s % 4
                    if c < 8:
                        i, h, back = 32 * l + s, c // 2, c % 2
                        lo, hi = (0, (j + 1) * P) if back else (j * P, SEQ)
                        act.wait_ge(S["mb_done"], i + 1)
                        if i >= 2:
                            act.wait_ge(S["p_done"], i - 1)
                        if s < 2:
                            act.wait_ge(S["qk_ready"], 9 * l + 8 + s)
                        col = j * 8 + back * 4 + h
                        A(sbufS[:, i % 2, lo:hi], bank[TP][:, lo:hi], ACT.Exp, bias=wcol[:, col:col + 1]).then_inc(
                            S["e_done"], 1)
                    gates(B("G00", "G01"), s)
                def ln_squares(i):
                    if i == 2:
                        act.wait_ge(S["ms_ready"], n("ms_ready"))
                        A(mflat[:, 0:2048], yflat, ACT.Square).then_inc(S["sq_ready"], 1)

                def ln_roots(i):
                    if i == 1:
                        act.wait_ge(S["ms_ready"], n("ms_ready"))
                        A(st32[:, 0:16], st32[:, 0:16], ACT.Sqrt).then_inc(S["sd_ready"], 1)
                dense(L, "CQ", copy_to(lambda t: q1[:, t, :]), ln_squares)
                dense(L, "AO", lambda b, t: tanh_half(b, t, slice(0, SEQ)), ln_roots)
                hi_chunks(4, yH, lambda k: g_anorm[l][:, k:k + 1])
                dense(L, "U00")
                dense(L, "U01")
                dense(L, "CK", copy_to(lambda t: k1[:, t, :]), first_rows(gqa_items(), q2, k2b, (), B("U01")[0]))
                dense(L, "CV", copy_to(lambda t: v1[:, t, :]))
                softmax(gqa_items(), B("G10", "G11"), q2, k2b)
                hi_chunks(4, yH, lambda k: 1.0)
                dense(L, "U10")
                dense(L, "U11")
                dense(L, "DQ", copy_to(lambda t: q2[:, t, :]), first_rows(nat_items(), q1, k1, B("CK"), B("U11")[0]))
                dense(L, "DK", copy_to(lambda t: k2[:, t, :]))
                softmax(nat_items(), B("G20", "G21"), q1, k1)
                hi_chunks(4, yH, lambda k: 1.0)
                dense(L, "U20")
                dense(L, "U21")
                dense(L, "DV", copy_to(lambda t: v2[:, t, :]), first_rows(diff_items(), q2, k2, B("DK"), B("U21")[0]))
                softmax(diff_items(), B("G30", "G31"), q2, k2)
                act.wait_ge(S["ms_ready"], n("ms_ready"))
                A(st32[:, 0:16], st32[:, 0:16], ACT.Sqrt).then_inc(S["sd_ready"], 1)
                hi_chunks(4, yH, lambda k: g_sub[l])
                dense(L, "U30")
                dense(L, "U31")
                hi_chunks(KD, hH, lambda k: 0.5)
                dense(L, "O0")
                dense(L, "O1", between=first_half(B("O0")[0]))
                rms(after(by_name[(L, "O1")]), (1,))
                hi_chunks(KD, hH, lambda k: g_norm[2 + 2 * l][:, k:k + 1])
                for name in ffn_order():
                    if name[:2] == "FG":
                        dense(L, name, lambda b, t: tanh_half(b, t, slice(0, SEQ)))
                    elif name[:2] == "FU":
                        def fu_evac(b, t):
                            act.wait_ge(free[t], b.nth[t] + 1)
                            A(yH[:, t, :], sbufS[:, t % 2, :], ACT.Copy).then_inc(S["hid_hi"], 1)
                        dense(L, name, fu_evac)
                    else:
                        last = name == ffn_order()[-1]
                        dense(L, name, between=first_half(B(ffn_order()[-2])[0]) if last else None)
            rms(after(by_name[(DEPTH, ffn_order()[-1])]), (1,))

        @block.vector
        def _(dve):
            n = Count()
            V = nc.vector

            def then(ins):
                ins.then_inc(S["dve_step"], 1)
                dve.wait_ge(S["dve_step"], n("dve_step"))

            def split(u):
                if u >= len(units):
                    return
                b, k0, kn, _ = units[u]
                if b.gates:
                    if u >= W_SLOTS:
                        dve.wait_ge(S["groups"], units[u - W_SLOTS][3])
                    V.memset(wL[:, u % W_SLOTS, 0:kn * P].bitcast(F32), 0.0)
                    V.memset(wH[:, u % W_SLOTS, 0:kn * P].bitcast(F32), 0.0).then_inc(S["gin"], 1)
                dve.wait_ge(S["w_hi"], u + 1)
                if b.gates:
                    raw, (hi, lo) = raw_view(u), w_views(u)
                    for c, w, r in gate_parts(u):
                        ins = V.tensor_tensor(lo[:, :, c:c + w], raw[:, :, r:r + w], hi[:, :, c:c + w].bitcast(F32),
                                              ALU.subtract)
                    ins.then_inc(S["w_lo"], 1)
                else:
                    width = kn * b.cols
                    V.tensor_tensor(wL[:, u % W_SLOTS, 0:width], wraw[:, u % RAW_SLOTS, 0:width],
                                    wH[:, u % W_SLOTS, 0:width].bitcast(F32), ALU.subtract).then_inc(S["w_lo"], 1)

            def ready(b, t):
                dve.wait_ge(S["groups"], b.groups_end - (b.banks - 1 - t))

            def evacuated(b, t):
                dve.wait_ge(free[t], b.nth[t] + 1)

            def dense(l, name, evac=None, between=None):
                b = by_name[(l, name)]
                for i in range(len(b.units)):
                    split(b.first_unit + i + LOOK)
                    if between:
                        between(i)
                if evac:
                    for t in range(b.banks):
                        ready(b, t)
                        evac(b, t)

            def norm_mean(part, squares=2 * NT):
                c = (slice(0, NT - 1), slice(NT - 1, NT))[part]
                dve.wait_ge(S["norm_sq"], n.at("norm_sq") + squares)
                if part:
                    n("norm_sq", squares)
                then(V.tensor_tensor(ss[:, c], ss[:, c], ss0[:, c], ALU.add))
                V.tensor_scalar(ss[:, c], ss[:, c], 1.0 / D, EPS, ALU.mult, ALU.add).then_inc(S["norm_ms"], 1)

            def norm_rows(dst):
                dve.wait_ge(S["norm_sd"], n("norm_sd"))
                then(V.reciprocal(rstd[:, 0:NT - 1], ss[:, 0:NT - 1]))
                for t in range(NT - 2):
                    dst(t, rstd[:, t:t + 1])
                norm_mean(1)
                dst(NT - 2, rstd[:, NT - 2:NT - 1])
                dve.wait_ge(S["norm_sd"], n("norm_sd"))
                then(V.reciprocal(rstd[:, NT - 1:NT], ss[:, NT - 1:NT]))
                dst(NT - 1, rstd[:, NT - 1:NT])

            def to_xn():
                def half_to_xn(half):
                    def dst(t, r):
                        V.tensor_scalar(xn[:, t, half * SEQ:(half + 1) * SEQ], x[:, t, half * SEQ:(half + 1) * SEQ], r,
                                        None, ALU.mult).then_inc(S["xn_ready"], 1)
                    return dst
                norm_rows(half_to_xn(0))
                for t in range(NT):
                    half_to_xn(1)(t, rstd[:, t:t + 1])

            def lo_chunks(chunks, hi, lo, scale):
                for k in chunks if isinstance(chunks, tuple) else range(chunks):
                    i = n("tp") - 1
                    dve.wait_ge(S["tp_hi"], n("tp_hi"))
                    V.scalar_tensor_tensor(out=lo[:, k, :], in0=bank[SC + i % TR_BANKS][:, :], scalar=scale(k),
                                           in1=hi[:, k, :].bitcast(F32), op0=ALU.mult, op1=ALU.subtract).then_inc(
                        S["tp_free"], 1)

            tanhs = [0]

            def silu(dst, src, b, t):
                dve.wait_ge(S["tanh_ready"], n("tanh_ready"))
                slot = tanhs[0] % 2
                tanhs[0] += 1
                V.scalar_tensor_tensor(out=dst, in0=sbufPT[:, slot, 0:src.shape[1]], scalar=1.0, in1=src,
                                       op0=ALU.add, op1=ALU.mult).then_inc(free[t], 1)

            def residual(half, norm_next=False):
                def evac(b, t):
                    V.tensor_tensor(x[:, t, half * SEQ:(half + 1) * SEQ], x[:, t, half * SEQ:(half + 1) * SEQ],
                                    bank[t][:, :], ALU.add).then_inc(free[t], 1)
                    if norm_next and t == NT - 2:
                        norm_mean(0, 2 * NT - 1)
                return evac

            def log_sigmoid(f, tmp, e):
                V.scalar_tensor_tensor(out=tmp, in0=f, scalar=-1.0, in1=f, op0=ALU.mult, op1=ALU.max).then_inc(
                    S["row_abs"], 1)
                dve.wait_ge(S["row_log"], n("row_log"))
                then(V.scalar_tensor_tensor(out=f, in0=f, scalar=0.0, in1=e, op0=ALU.min, op1=ALU.subtract))

            def group_sums(dst, src, groups):
                then(V.tensor_reduce(dst, src.rearrange("p (g d) -> p g d", g=groups), AX, ALU.add))

            def per_group(dst, src, col, groups):
                w = src.shape[1] // groups
                return (dst.rearrange("p (g d) -> p g d", g=groups), src.rearrange("p (g d) -> p g d", g=groups),
                        col.unsqueeze(2).to_broadcast([P, groups, w]))

            def split_rows(items, g, q, k):
                (qi, half), (ki, _) = row_groups(items)[g]
                r, other = slice(DH * half, DH * half + DH), slice(DH * (1 - half), DH * (1 - half) + DH)
                dve.wait_ge(S["hi_done"], n("hi_done"))
                V.tensor_tensor(q_split[g % 2][other, :], q[r, qi, :], q_split[g % 2][r, :].bitcast(F32), ALU.subtract)
                V.tensor_tensor(k_low[g % 2][r, :], k[r, ki, :], k_twice[g % 2][r, :].bitcast(F32),
                                ALU.subtract).then_inc(S["split_done"], 1)

            def first_rows(items, q, k):
                def between(i):
                    if i >= 2:
                        split_rows(items, i - 2, q, k)
                return between

            def nat_table(h, half):
                if half == 0:
                    dve.wait_ge(S[f"tab_dma{h % 2}"], n(f"tab{h % 2}", 32))
                part = tab[:, h % 2, :].rearrange("p (e k) -> p e k", e=14)[:, 7 * half:7 * half + 7, :]
                then(V.scalar_tensor_tensor(out=part, in0=part, scalar=1.0 / SCALE,
                                            in1=nat_mask[:, :].unsqueeze(1).to_broadcast([P, 7, DH]),
                                            op0=ALU.mult, op1=ALU.add))

            def softmax(l, items, beside, q=None, k=None, extra=None):
                i0 = n("items", len(items)) - len(items)
                for s in range(max(len(items) + 2, 32 if beside else 0)):
                    if beside and s % NT == 2 and NT < s < len(items) - NT:
                        split_rows(items, s // NT + 1, q, k)
                    if s < len(items):
                        it, i = items[s], i0 + s
                        kmax, col = it["kmax"], i % 4
                        kind, per = it["kind"], 8 if it["kind"] == "diff" else 4
                        if kind == "nat" and s % per in (1, 3) and it["h"] + 1 < HEADS:
                            nat_table(it["h"] + 1, s % per // 2)
                        if kind == "diff" and s % per == 0:
                            h = it["h"]
                            dve.wait_ge(S[f"tab_dma{h % 2}"], n(f"tab{h % 2}", 16))
                        dve.wait_ge(S["sc_done"], i + 1)
                        if kind in ("nat", "diff"):
                            if i >= 2:
                                dve.wait_ge(S["pt_done"], i - 1)
                            table = tab[:, it["h"] % 2, it["t"] * P:it["t"] * P + SEQ][:, ::-1]
                            then(V.tensor_tensor_reduce(sbufS[:, i % 2, :], bank[SC + i % 2][:, :], table, SCALE, -BIG,
                                                        ALU.add, ALU.max, mx[:, col:col + 1]))
                            V.tensor_scalar(nm[:, col:col + 1], mx[:, col:col + 1], -1.0, None, ALU.mult).then_inc(
                                S["mx_done"], 1)
                        else:
                            then(V.tensor_reduce(mx[:, col:col + 1], bank[SC + i % 2][:, 0:kmax], AX, ALU.max))
                            V.tensor_scalar(nm[:, col:col + 1], mx[:, col:col + 1], -SCALE, None, ALU.mult).then_inc(
                                S["mx_done"], 1)
                    if 2 <= s < len(items) + 2:
                        it, i = items[s - 2], i0 + s - 2
                        col, w = i % 4, it["v"][1]
                        dve.wait_ge(S["pv_done"], i + 1)
                        then(V.reciprocal(rs[:, col:col + 1], lsum[:, col:col + 1]))
                        r, src = rs[:, col:col + 1], bank[PV][:, 0:w]
                        if it["kind"] == "fox":
                            dst = merged[:, it["t"], SEQ + it["y"]:SEQ + it["y"] + w]
                            V.scalar_tensor_tensor(out=dst, in0=src, scalar=r, in1=dst, op0=ALU.mult,
                                                   op1=ALU.mult).then_inc(S["y_done"], 1)
                        else:
                            dst = ytok[:, it["t"], it["y"]:it["y"] + w]
                            if it["comp"] == 0:
                                V.tensor_scalar(dst, src, r, None, ALU.mult).then_inc(S["y_done"], 1)
                            else:
                                then(V.tensor_tensor(r, r, lam[l], ALU.mult))
                                V.scalar_tensor_tensor(out=dst, in0=src, scalar=r, in1=dst, op0=ALU.mult,
                                                       op1=ALU.add).then_inc(S["y_done"], 1)
                                dve.wait_ge(S["y_done"], i + 1)
                                c = 4 * it["t"] + it["h"]
                                then(V.tensor_tensor_reduce(set1[:, 0:P], dst, dst, 1.0, 0.0, ALU.mult, ALU.add,
                                                            st32[:, c:c + 1]))
                    if extra:
                        extra(s)
                    if beside and s % 4 == 0 and s < 32:
                        split(beside[s // 16].first_unit + (s // 4) % 4 + LOOK)

            def merge(l, br, half):
                gate = by_name[(l, f"G{br}{half}")]

                def evac(b, t):
                    evacuated(gate, t)
                    cols = slice(half * SEQ, (half + 1) * SEQ)
                    if br == 0:
                        V.scalar_tensor_tensor(out=merged[:, t, cols], in0=gbuf[:, t, cols], scalar=1.0,
                                               in1=bank[t][:, :], op0=ALU.add, op1=ALU.mult).then_inc(free[t], 1)
                        return
                    V.scalar_tensor_tensor(out=sbufS[:, t % 2, :], in0=gbuf[:, t, cols], scalar=1.0,
                                           in1=bank[t][:, :], op0=ALU.add, op1=ALU.mult).then_inc(free[t], 1)
                    evacuated(b, t)
                    add = V.tensor_tensor(merged[:, t, cols], merged[:, t, cols], sbufS[:, t % 2, :], ALU.add)
                    if br == 3:
                        add.then_inc(S["y_ready"], 1)
                return evac

            for t in range(NT):
                dve.wait_ge(S[f"x_tile{t}"], 16)
            norm_mean(0, 2 * (NT - 1))
            to_xn()
            for u in range(LOOK):
                split(u)
            dve.wait_ge(S["ident_norm"], 32)
            lo_chunks(KD, hH, hL, lambda k: g_norm[0][:, k:k + 1])
            split(LOOK)
            dve.wait_ge(S["consts"], CONSTS)
            for dst, src in ((ident16, ident[:, :]), (causal16, gflat[:, 3072:3200]), (anti16, gflat[:, 3200:3328])):
                V.tensor_copy(dst[:, :], src)
            V.memset(row_nm[:, :].bitcast(F32), 0.0)
            V.tensor_tensor(row_sel[:, :], ident[:, 0:GATE_ROWS], ident[:, 64:64 + GATE_ROWS], ALU.add).then_inc(
                S["masks_ready"], 1)
            dve.wait_ge(S["masks_ready"], 1)
            for i in range(2 * DEPTH):
                ins = V.tensor_tensor_reduce(gflat[:, 2048 + DH * i:2048 + DH * (i + 1)], gflat[:, 2 * i * DH:(2 * i + 1) * DH],
                                             gflat[:, (2 * i + 1) * DH:(2 * i + 2) * DH], 1.0, 0.0, ALU.mult, ALU.add,
                                             lam_tmp[:, i:i + 1])
            V.tensor_tensor(lb, lbt, lbt, ALU.subtract).then_inc(S["lam_dot"], 1)
            dve.wait_ge(S["lam_exp"], 1)
            for l in range(DEPTH):
                then(V.tensor_tensor(lam[l], lam_tmp[:, 2 * l + 1:2 * l + 2], lam_tmp[:, 2 * l:2 * l + 1], ALU.subtract))
                V.tensor_scalar(lam[l], lam[l], -lambda_init(l), None, ALU.add)
            dve.wait_ge(S["lb_ready"], 1)
            then(V.reciprocal(oml, lb))
            then(V.tensor_tensor(lb, lb, oml, ALU.mult))
            then(V.tensor_tensor(lb, lb, lb, ALU.subtract))
            then(V.tensor_scalar(lb, lb, 0.0, 1.0 - 1e-6, ALU.max, ALU.min))
            then(V.tensor_scalar(oml, lb, -1.0, 1.0, ALU.mult, ALU.add))

            def fl_evac(b, t):
                f, tmp, e, ones = (yflat[0:8, 512 * i:512 * i + 512] for i in range(4))
                V.memset(ones, 1.0)
                V.tensor_scalar(f, bank[b.bank0][0:8, :], bf_col[0:8, :], None, ALU.add).then_inc(free[b.bank0], 1)
                evacuated(b, b.bank0)
                log_sigmoid(f, tmp, e)
                then(V.tensor_tensor_scan(tmp, ones, f, 0.0, ALU.mult, ALU.add))
                then(V.tensor_scalar(row_nm[0:8, :], tmp, -1.0 / SCALE, None, ALU.mult))
                V.scalar_tensor_tensor(out=row_nm[64:72, :], in0=tmp, scalar=-1.0 / SCALE,
                                       in1=row_nm[0:8, :].bitcast(F32), op0=ALU.mult, op1=ALU.subtract)
            ready(by_name[(0, "FL")], 0)
            fl_evac(by_name[(0, "FL")], 0)

            def bf_evac(b, t):
                if t < 2:
                    silu(qs[:, t, :], bank[t][:, :], b, t)
                else:
                    ins = V.tensor_scalar(gflat[:, (t - 2) * SEQ:(t - 1) * SEQ], bank[t][:, :], -80.0, None, ALU.max)
                    ins.then_inc(free[t], 1)
            dense(0, "BF", bf_evac)
            for t in range(4):
                evacuated(by_name[(0, "BF")], t)
            qs_f, ks_f, bflat = set1[:, 0:1024], set1[:, 1024:2048], set1[:, 2048:3072]
            V.tensor_scalar(qs_f, qs_f, 0.5 * DH ** -0.5, None, ALU.mult).then_inc(S["z_ready"], 1)

            def forget_gates(i):
                if i == 1:
                    dve.wait_ge(S["ez_ready"], 1)
                    then(V.tensor_scalar(gflat[:, 0:1024], gflat[:, 1024:2048], 1.0, None, ALU.add))
                    V.reciprocal(gflat[:, 0:512], gflat[:, 0:512])
                elif i == 2:
                    then(V.reciprocal(gflat[:, 512:1024], gflat[:, 512:1024]))
                elif i == 3:
                    for g in range(2):
                        cols_g = slice(g * SEQ, (g + 1) * SEQ)
                        V.tensor_scalar(gflat[:, 2048 + g * SEQ:2560 + g * SEQ], gflat[:, cols_g], oml[:, g:g + 1],
                                        lb[:, g:g + 1], ALU.mult, ALU.add)
                        then(V.scalar_tensor_tensor(out=ks[:, g, :], in0=gflat[:, 1024 + g * SEQ:1536 + g * SEQ],
                                                    scalar=oml[:, g:g + 1], in1=gflat[:, cols_g], op0=ALU.mult,
                                                    op1=ALU.mult))
                    then(V.tensor_scalar(gflat[:, 3072:4096], gflat[:, 2048:3072], 1e-30, 2.0 ** 60, ALU.max, ALU.mult))
                    then(V.tensor_scalar(gflat[:, 3072:4096], gflat[:, 3072:4096], 1.0, None, ALU.min))
                    V.tensor_scalar(gflat[:, 2048:3072], gflat[:, 2048:3072], 2.0 ** -60, None, ALU.max).then_inc(
                        S["z_ready"], 1)
            dense(0, "BI", lambda b, t: silu(merged[:, t, 256:512], bank[t][:, 256:512], b, t), between=forget_gates)

            def summed_gates(i):
                if i == 1:
                    V.memset(gflat[:, 0:1024], 1.0)
                    dve.wait_ge(S["ln_ready"], 2)
                    then(V.tensor_tensor(gflat[:, 2048:3072], gflat[:, 2048:3072], gflat[:, 3072:4096], ALU.add))
                    for c in range(8):
                        tok = slice(c * P, (c + 1) * P)
                        ins = V.tensor_tensor_scan(set1[:, 2048 + c * P:2048 + (c + 1) * P], gflat[:, tok],
                                                   gflat[:, 2048 + c * P:2048 + (c + 1) * P], 0.0, ALU.mult, ALU.add)
                    ins.then_inc(S["late"], 1)
                    dve.wait_ge(S["late"], 1)

            dense(0, "UV", between=summed_gates)
            uv = by_name[(0, "UV")]
            for t in range(NT + 1):
                if t < NT:
                    cube = sbufS[:, t % 2, :]
                    dve.wait_ge(S["gsq"], n("gsq"))
                    then(V.tensor_scalar(cube, cube, GELU_A, 1.0, ALU.mult, ALU.add))
                    V.tensor_tensor(cube, cube, bank[t][:, :], ALU.mult).then_inc(S["gin2"], 1)
                if t >= 1:
                    dve.wait_ge(S["tanh_ready"], n("tanh_ready"))
                    slot = tanhs[0] % 2
                    tanhs[0] += 1
                    V.scalar_tensor_tensor(out=uu[:, t - 1, :], in0=sbufPT[:, slot, 0:256], scalar=1.0,
                                           in1=bank[t - 1][:, 0:256], op0=ALU.add, op1=ALU.mult)
                    V.scalar_tensor_tensor(out=vv[:, t - 1, :], in0=sbufPT[:, slot, 256:512], scalar=1.0,
                                           in1=bank[t - 1][:, 256:512], op0=ALU.add, op1=ALU.mult).then_inc(
                        free[t - 1], 1)
            dense(0, "AZ", lambda b, t: silu(merged[:, t, 0:256], bank[t][:, 0:256], b, t))
            v_f = set1[:, 5120:6144]

            def gated_mlp(i):
                v_g, _, mean = per_group(v_f, v_f, st32c[:, 0:16], 16)
                if i == 0:
                    for t in range(NT):
                        evacuated(by_name[(0, "AZ")], t)
                    group_sums(st32c[:, 0:16], v_f, 16)
                    then(V.tensor_scalar(st32c[:, 0:16], st32c[:, 0:16], 1.0 / DH, None, ALU.mult))
                    V.tensor_tensor(v_g, v_g, mean, ALU.subtract).then_inc(S["ms_ready"], 1)
                elif i == 1:
                    dve.wait_ge(S["sq_ready"], n("sq_ready"))
                    group_sums(st32[:, 0:16], ptflat, 16)
                    V.tensor_scalar(st32[:, 0:16], st32[:, 0:16], 1.0 / DH, 4 * EPS, ALU.mult, ALU.add).then_inc(
                        S["ms_ready"], 1)
                elif i == 2:
                    dve.wait_ge(S["sd_ready"], n("sd_ready"))
                    then(V.reciprocal(st32b[:, 0:16], st32[:, 0:16]))
                    then(V.tensor_tensor(v_g, v_g, st32b[:, 0:16].unsqueeze(2).to_broadcast([P, 16, DH]), ALU.mult))
                    dve.wait_ge(S["gp_step"], 16 * 4)
                    then(V.tensor_tensor(gflat[:, 0:512], gflat[:, 0:512], gflat[:, 1024:1536], ALU.mult))
                elif i == 3:
                    then(V.tensor_tensor(vv, vv, gflat[:, 512:768].unsqueeze(1).to_broadcast([P, NT, 256]), ALU.mult))
                    V.tensor_tensor(vv, vv, gflat[:, 768:1024].unsqueeze(1).to_broadcast([P, NT, 256]),
                                    ALU.add).then_inc(S["vn_ready"], 1)
            dense(0, "CQ", between=gated_mlp)
            dense(0, "CK")
            b8 = bflat.rearrange("p (c t) -> p c t", t=P)

            def mixed_and_decays(i):
                if i == 0:
                    dve.wait_ge(S["mix_done"], 4)
                    for g in range(4):
                        tmp = view(sflat, 256 * g, (NT, DH))
                        then(V.scalar_tensor_tensor(
                            out=tmp, in0=bank[TP + g // 2][:, (g % 2) * 256:(g % 2) * 256 + 256].rearrange(
                                "p (n d) -> p n d", n=NT), scalar=bs_t[:, g:g + 1], in1=uu[:, :, g * DH:(g + 1) * DH],
                            op0=ALU.add, op1=ALU.mult))
                        dst = merged[:, :, g * DH:(g + 1) * DH]
                        ins = V.scalar_tensor_tensor(out=dst, in0=tmp, scalar=0.5, in1=dst, op0=ALU.mult, op1=ALU.mult)
                    ins.then_inc(S["mix_read"], 1)
                    V.tensor_tensor(gflat[:, 0:1024].rearrange("p (c t) -> p c t", t=P),
                                    b8[:, :, P - 1:P].to_broadcast([P, 8, P]), b8, ALU.subtract).then_inc(
                        S["d_ready"], 1)
                elif i == 2:
                    dve.wait_ge(S["ed_ready"], 1)
                    then(V.tensor_copy(ebl, gflat[:, 2048:3072].rearrange("p (c t) -> p c t", t=P)[:, :, P - 1]))
                    V.tensor_tensor(gflat[:, 2048:3072], gflat[:, 2048:3072], qs_f, ALU.mult)
                    V.tensor_tensor(gflat[:, 0:1024], gflat[:, 0:1024], ks_f, ALU.mult).then_inc(S["ke_ready"], 1)
            dense(0, "CV", between=mixed_and_decays)

            masks = tflat[:, 0:1024].rearrange("p (l t) -> p l t", t=P)

            def halves(lev, z):
                return z.rearrange("p (n h m) -> p n h m", h=2, m=CHUNK >> (lev + 1))

            def level_logs(lev):
                m = CHUNK >> (lev + 1)
                bh, dh = halves(lev, bflat), halves(lev, decay)
                border = bh[:, :, 0, m - 1:m].to_broadcast([P, 1024 // (2 * m), m])
                V.tensor_tensor(dh[:, :, 1, :], bh[:, :, 1, :], border, ALU.subtract)
                V.tensor_tensor(dh[:, :, 0, :], border, bh[:, :, 0, :], ALU.subtract).then_inc(S["d_ready"], 1)

            def level_products(lev):
                dve.wait_ge(S["ed_ready"], lev + 2)
                if lev >= 2:
                    dve.wait_ge(S["lvl_done"], 4 * (lev - 1))
                dh, both = halves(lev, decay), halves(lev, scaled[lev % 2])
                V.tensor_tensor(both[:, :, 1, :], halves(lev, qs_f)[:, :, 1, :], dh[:, :, 1, :], ALU.mult)
                V.tensor_tensor(both[:, :, 0, :], halves(lev, ks_f)[:, :, 0, :], dh[:, :, 0, :], ALU.mult).then_inc(
                    S["lvl_ready"], 1)
                dve.wait_ge(S["lvl_ready"], lev + 1)

            def level0(i):
                if i == 0:
                    level_logs(0)
                elif i == 2:
                    dve.wait_ge(S["keT_done"], 3)
                    level_products(0)
                elif i == 3:
                    V.memset(yflat, 0.0)
            dense(0, "CZ", lambda b, t: silu(merged[:, t, 512:1024], bank[t][:, :], b, t), between=level0)

            def hgrn_scores(s):
                if s == 1:
                    dve.wait_ge(S["upd_done"], 3)
                    for m in range(3):
                        for g in range(2):
                            for half in range(2):
                                r = slice(DH * half, DH * half + DH)
                                c0 = (2 * (m % 2) + g) * P + DH * half
                                upd = bank[2 + m // 2][r, c0:c0 + DH]
                                if m == 0:
                                    ins = V.tensor_copy(states[r, m, g, :], upd)
                                else:
                                    ins = V.scalar_tensor_tensor(out=states[r, m, g, :], in0=states[r, m - 1, g, :],
                                                                 scalar=ebl[r, 4 * g + m:4 * g + m + 1], in1=upd,
                                                                 op0=ALU.mult, op1=ALU.add)
                        if m < 2:
                            then(ins)
                    ins.then_inc(S["st_ready"], 1)
                if s % 4 == 0 and s // 4 + 1 < LEVELS:
                    level_logs(s // 4 + 1)
                if s % 4 == 2 and s // 4 + 1 < LEVELS:
                    level_products(s // 4 + 1)
                if 1 <= s <= 4 * (LEVELS + 1):
                    lev, h = (s - 1) // 4, (s - 1) % 4
                    dve.wait_ge(S["lvl_done"], s)
                    if lev:
                        dve.wait_ge(S["lvl_used"], s - 4)
                    V.copy_predicated(ssc[:, h, :, :], masks[:, lev, :].bitcast(U32).unsqueeze(1).to_broadcast([P, NT, P]),
                                      bank[(s - 1) % 4][:, :].rearrange("p (n t) -> p n t", n=NT)).then_inc(
                        S["lvl_used"], 1)
            softmax(0, fox_items(), [], extra=hgrn_scores)
            lo_chunks((0, 1), hH, hL, lambda k: 0.5)
            dve.wait_ge(S["sq_ready"], n("sq_ready"))
            group_sums(st32[:, 0:16], ptflat, 16)
            V.tensor_scalar(st32[:, 0:16], st32[:, 0:16], 1.0 / DH, EPS, ALU.mult, ALU.add).then_inc(S["ms_ready"], 1)
            lo_chunks((4, 5, 6, 7), hH, hL, lambda k: 0.5)

            def hgrn_norm(i):
                if i == 0:
                    dve.wait_ge(S["sd_ready"], n("sd_ready"))
                    then(V.reciprocal(st32b[:, 0:16], st32[:, 0:16]))
                    o_g, _, r_g = per_group(sflat, sflat, st32b[:, 0:16], 16)
                    then(V.tensor_tensor(o_g, o_g, r_g, ALU.mult))
                    then(V.tensor_tensor(o_g, o_g, onorm.unsqueeze(1).to_broadcast([P, 16, DH]), ALU.mult))
                elif i == 1:
                    V.tensor_tensor(merged[:, :, 256:512], merged[:, :, 256:512],
                                    sflat.rearrange("p (t d) -> p t d", t=NT), ALU.mult).then_inc(S["y_ready"], 1)
                elif i == 2:
                    lo_chunks((2, 3), hH, hL, lambda k: 0.5)
            dense(0, "O0", residual(0), between=hgrn_norm)
            dense(0, "O1", residual(1, True))

            def to_x(sem):
                def dst(t, r):
                    V.scalar_tensor_tensor(out=x[:, t, :], in0=x[:, t, :], scalar=r, in1=yflat[:, 0:D], op0=ALU.mult,
                                           op1=ALU.mult).then_inc(S[sem], 1)
                return dst
            dve.wait_ge(S["gp_step"], 16 * 5)
            norm_rows(to_x("x_ready"))
            dve.wait_ge(S["x_ready"], NT)

            for l in range(DEPTH):
                L = l + 1

                def B(*names):
                    return [by_name[(L, name)] for name in names]

                if l == 0:
                    norm_mean(0, 2 * (NT - 1))
                to_xn()
                lo_chunks(KD, hH, hL, lambda k: g_norm[1 + 2 * l][:, k:k + 1])
                for tc, ts, gain in ((cq_t, sq_t, g_q[l]), (ck_t, sk_t, g_k[l])):
                    V.tensor_tensor(tc, rope[:, 0, :, :], gain.unsqueeze(1).to_broadcast([P, NT, DH]), ALU.mult)
                    for j in range(2):
                        def pick(z, jj):
                            return z.rearrange("p t (g j d) -> p t g j d", g=2, j=2)[:, :, :, jj, :]
                        gsw = gain.rearrange("p (g j d) -> p g j d", g=2, j=2)[:, :, 1 - j, :]
                        for gg in range(2):
                            V.tensor_tensor(pick(ts, j)[:, :, gg, :], pick(rope[:, 1, :, :], j)[:, :, gg, :],
                                            gsw[:, gg, :].unsqueeze(1).to_broadcast([P, NT, 16]), ALU.mult)
                def ag_evac(b, t):
                    V.memset(row_b, 0.0)
                    V.tensor_scalar(row_i, bank[b.bank0][0:GATE_ROWS, :], g_bias[l][0:GATE_ROWS, 0:1], None, ALU.add)
                    V.tensor_scalar(row_f, bank[b.bank0][64:64 + GATE_ROWS, :], g_bias[l][0:GATE_ROWS, 1:2], None,
                                    ALU.add).then_inc(free[b.bank0], 1)
                    evacuated(b, b.bank0)
                    V.scalar_tensor_tensor(out=row_w, in0=row_f, scalar=-1.0, in1=row_f, op0=ALU.mult,
                                           op1=ALU.max).then_inc(S["row_abs"], 1)

                def gate_rows(stage):
                    ways = ((slice(0, 4), 1), (slice(32, 36), -1))
                    if stage == 0:
                        dve.wait_ge(S["row_log"], n("row_log"))
                        then(V.scalar_tensor_tensor(out=row_f, in0=row_f, scalar=0.0, in1=row_m, op0=ALU.min,
                                                    op1=ALU.subtract))
                        then(V.memset(row_w, 1.0))
                    elif stage == 1:
                        for r, d in ways:
                            then(V.tensor_tensor_scan(row_b[r, ::d], row_w[r, ::d], row_f[r, ::d], 0.0, ALU.mult,
                                                      ALU.add))
                    elif stage == 2:
                        then(V.tensor_tensor(row_w, row_i, row_b, ALU.subtract))
                    elif stage == 3:
                        for r, d in ways:
                            then(V.tensor_tensor_scan(row_f[r, ::d], row_w[r, ::d], row_w[r, ::d], 0.0, ALU.max,
                                                      ALU.max))
                    elif stage == 4:
                        V.tensor_tensor(row_m, row_b, row_f, ALU.add)
                        then(V.tensor_scalar(row_nm[0:GATE_ROWS, :], row_f, -1.0, None, ALU.mult))
                    elif stage == 5:
                        V.scalar_tensor_tensor(out=row_nm[64:64 + GATE_ROWS, :], in0=row_f, scalar=-1.0,
                                               in1=row_nm[0:GATE_ROWS, :].bitcast(F32), op0=ALU.mult, op1=ALU.subtract)
                        V.tensor_scalar(row_m, row_m, -1.0, 85.0, ALU.mult, ALU.min).then_inc(S["rows_ready"], 1)

                heads = [(q1, "AQ", h) for h in range(4)] + [(k1, "AK", h) for h in range(4)]

                def conv(c):
                    dst, name, h = heads[c]
                    evacuated(by_name[(L, name)], h)
                    tap = g_conv[l].rearrange("p (j c) -> p j c", j=3)[:, :, c:c + 1]
                    if c >= 2:
                        dve.wait_ge(S["qk_ready"], 9 * l + c)
                    u, src = sbufS[:, c % 2, :], dst[:, h, :]
                    then(V.tensor_scalar(u, src, tap[:, 1, :], None, ALU.mult))
                    then(V.scalar_tensor_tensor(out=u[:, 1:SEQ], in0=src[:, 0:SEQ - 1], scalar=tap[:, 0, :],
                                                in1=u[:, 1:SEQ], op0=ALU.mult, op1=ALU.add))
                    V.scalar_tensor_tensor(out=u[:, 0:SEQ - 1], in0=src[:, 1:SEQ], scalar=tap[:, 2, :],
                                           in1=u[:, 0:SEQ - 1], op0=ALU.mult, op1=ALU.add).then_inc(S["conv_done"], 1)

                def conv_silu(c):
                    dve.wait_ge(S["conv_tanh"], n("conv_tanh"))
                    dst, _, h = heads[c]
                    V.scalar_tensor_tensor(out=dst[:, h, :], in0=sbufPT[:, c % 2, :], scalar=1.0, in1=sbufS[:, c % 2, :],
                                           op0=ALU.add, op1=ALU.mult).then_inc(S["qk_ready"], 1)

                def rotate(t):
                    for z, heads, tc, ts, r, at_c in ((qraw[:, t, :], 8, cq_t, sq_t, st40[:, 8 * t:8 * t + 8], 0),
                                                      (kraw[:, t, :], 2, ck_t, sk_t, st40[:, 32 + 2 * t:34 + 2 * t], 0)):
                        w = heads * DH
                        xc, xs = rope_c[:, 0:w], rope_s[:, 0:w]
                        z3 = z.rearrange("p (h d) -> p h d", h=heads)
                        V.tensor_tensor(xc.rearrange("p (h d) -> p h d", h=heads), z3,
                                        tc[:, t, :].unsqueeze(1).to_broadcast([P, heads, DH]), ALU.mult)
                        for g in range(2):
                            for j in range(2):
                                lo = 32 * g + 16 * j
                                sw = 32 * g + 16 * (1 - j)
                                ins = V.tensor_tensor(xs.rearrange("p (h d) -> p h d", h=heads)[:, :, lo:lo + 16],
                                                      z3[:, :, sw:sw + 16],
                                                      ts[:, t, lo:lo + 16].unsqueeze(1).to_broadcast([P, heads, 16]), ALU.mult)
                        then(ins)
                        then(V.tensor_tensor(xc, xc, xs, ALU.add))
                        ins = V.tensor_tensor(z3, xc.rearrange("p (h d) -> p h d", h=heads),
                                              r.unsqueeze(2).to_broadcast([P, heads, DH]), ALU.mult)
                        if heads == 8:
                            then(ins)
                    ins.then_inc(S["ropeq_ready"], 1)
                    dve.wait_ge(S["ropeq_ready"], n("ropeq_ready"))

                V.memset(v1a[:, :, :, P:P + 1], 1.0).then_inc(S["qk_ready"], 1)
                dense(L, "AQ")
                dense(L, "AG", ag_evac)

                def bq_between(i):
                    conv(i)
                    if i >= 1:
                        conv_silu(i - 1)
                        gate_rows(i - 1)
                dense(L, "BQ", between=bq_between)

                def bkv_between(i):
                    if i == 0:
                        conv_silu(3)
                    if i < 3:
                        gate_rows(3 + i)
                    if i in (2, 3):
                        for t in (2 * i - 4, 2 * i - 3):
                            dve.wait_ge(S["sq_ready"], n("sq_ready"))
                            V.tensor_reduce(st40[:, 8 * t:8 * t + 8],
                                            sbufS[:, t % 2, :].rearrange("p (g d) -> p g d", g=8), AX,
                                            ALU.add).then_inc(S["sq_taken"], 1)
                dense(L, "BKV", between=bkv_between)

                def ak_between(i):
                    if i == 0:
                        dve.wait_ge(S["sq_ready"], n("sq_ready"))
                        group_sums(st40[:, 32:40], sbufPT[:, 0, :], 8)
                        n("sq_taken", NT)
                        V.tensor_scalar(st40, st40, 1.0 / DH, EPS, ALU.mult, ALU.add).then_inc(S["ms_ready"], 1)
                        dve.wait_ge(S["rowt_done"], l + 1)
                        rows_t = bank[TP][:, 0:8 * GATE_ROWS].rearrange("p (t w r) -> p t w r", t=NT, w=2)
                        for w, dst in ((0, wcol), (1, mcol)):
                            for d in range(2):
                                ins = V.tensor_copy(dst.rearrange("p (t d h) -> p t d h", t=NT, d=2)[:, :, d, :],
                                                    rows_t[:, :, w, 32 * d:32 * d + 4])
                        ins.then_inc(S["rowt_read"], 1)
                    else:
                        if i == 1:
                            dve.wait_ge(S["sd_ready"], n("sd_ready"))
                            then(V.reciprocal(st40, st40))
                        rotate(i - 1)
                dense(L, "AK", between=ak_between)

                def av_between(i):
                    if i == 0:
                        rotate(3)
                    if i < 3:
                        conv(4 + i)
                    if i in (1, 2):
                        conv_silu(3 + i)
                    if i == 2:
                        conv(7)
                        conv_silu(6)
                    if i == 3:
                        conv_silu(7)
                dense(L, "AV", between=av_between)
                n("tp", 5)
                dve.wait_ge(S["mcol_ready"], l + 1)
                for s in range(36):
                    c, j = s // 4, s % 4
                    if c < 8:
                        i, h, back = 32 * l + s, c // 2, c % 2
                        lo, hi = (0, (j + 1) * P) if back else (j * P, SEQ)
                        dve.wait_ge(S["e_done"], i + 1)
                        dve.wait_ge(S["qk_done"], i + 1)
                        if c >= 2:
                            dve.wait_ge(S["o_done"], 32 * l + 4 * (c - 1))
                        V.scalar_tensor_tensor(out=pmat[:, c % 2, j, lo:hi], in0=bank[SC + i % 2][:, lo:hi],
                                               scalar=0.25 * P ** -0.5, in1=sbufS[:, i % 2, lo:hi],
                                               op0=ALU.mult, op1=ALU.mult).then_inc(S["p_done"], 1)
                    if c >= 1:
                        i, h, back = 32 * l + s - 4, (c - 1) // 2, (c - 1) % 2
                        dve.wait_ge(S["o_done"], i + 1)
                        src = bank[PV - (s % 2 if s > 32 else 0)]
                        den = src[:, P:P + 1]
                        col = j * 8 + back * 4 + h
                        then(V.tensor_scalar(hden[:, 0:1], den, -1.0, None, ALU.mult))
                        then(V.scalar_tensor_tensor(out=hden[:, 1:2], in0=den, scalar=mcol[:, col:col + 1],
                                                    in1=hden[:, 0:1], op0=ALU.max, op1=ALU.max))
                        then(V.reciprocal(hden[:, 2:3], hden[:, 1:2]))
                        dst = ytok[:, j, h * P:(h + 1) * P]
                        if back:
                            V.scalar_tensor_tensor(out=dst, in0=src[:, 0:P], scalar=hden[:, 2:3], in1=dst,
                                                   op0=ALU.mult, op1=ALU.add).then_inc(S["hh_done"], 1)
                        else:
                            V.tensor_scalar(dst, src[:, 0:P], hden[:, 2:3], None, ALU.mult).then_inc(S["hh_done"], 1)
                        dve.wait_ge(S["hh_done"], i + 1)
                    if s % 4 == 0 and s < 32:
                        split(B("G00", "G01")[s // 16].first_unit + (s // 4) % 4 + LOOK)
                y_g, _, mean = per_group(yflat, yflat, st32c[:, 0:16], 16)

                def ln_mean(i):
                    if i == 0:
                        group_sums(st32c[:, 0:16], yflat, 16)
                        then(V.tensor_scalar(st32c[:, 0:16], st32c[:, 0:16], 1.0 / P, None, ALU.mult))
                    elif i == 1:
                        V.tensor_tensor(y_g, y_g, mean, ALU.subtract).then_inc(S["ms_ready"], 1)

                def ln_scales(i):
                    if i == 0:
                        dve.wait_ge(S["sq_ready"], n("sq_ready"))
                        group_sums(st32[:, 0:16], mflat[:, 0:2048], 16)
                        V.tensor_scalar(st32[:, 0:16], st32[:, 0:16], 1.0 / P, EPS, ALU.mult, ALU.add).then_inc(
                            S["ms_ready"], 1)
                    elif i == 2:
                        dve.wait_ge(S["sd_ready"], n("sd_ready"))
                        then(V.reciprocal(st32b[:, 0:16], st32[:, 0:16]))
                        then(V.tensor_scalar(st32b[:, 0:16], st32b[:, 0:16], 0.5, None, ALU.mult))
                dense(L, "CQ", between=ln_mean)

                def ao_evac(b, t):
                    silu(ytok[:, t, :], ytok[:, t, :], b, t)
                    evacuated(b, t)
                    z, _, r = per_group(ytok[:, t, :], ytok[:, t, :], st32b[:, 4 * t:4 * t + 4], 4)
                    V.tensor_tensor(z, z, r, ALU.mult).then_inc(S["y_ready"], 1)
                dense(L, "AO", ao_evac, ln_scales)
                lo_chunks(4, yH, yL, lambda k: g_anorm[l][:, k:k + 1])
                dense(L, "U00", merge(L, 0, 0))
                dense(L, "U01", merge(L, 0, 1))
                dense(L, "CK", between=first_rows(gqa_items(), q2, k2b))
                dense(L, "CV")
                softmax(l, gqa_items(), B("G10", "G11"), q2, k2b)
                lo_chunks(4, yH, yL, lambda k: 1.0)
                dense(L, "U10", merge(L, 1, 0))
                dense(L, "U11", merge(L, 1, 1))
                dense(L, "DQ", between=first_rows(nat_items(), q1, k1))
                dense(L, "DK", between=lambda i: nat_table(0, i - 2) if i >= 2 else None)
                softmax(l, nat_items(), B("G20", "G21"), q1, k1)
                lo_chunks(4, yH, yL, lambda k: 1.0)
                dense(L, "U20", merge(L, 2, 0))
                dense(L, "U21", merge(L, 2, 1))
                dense(L, "DV", between=first_rows(diff_items(), q2, k2))
                softmax(l, diff_items(), B("G30", "G31"), q2, k2)
                V.tensor_scalar(st32[:, 0:16], st32[:, 0:16], 1.0 / P, EPS, ALU.mult, ALU.add).then_inc(S["ms_ready"], 1)
                dve.wait_ge(S["sd_ready"], n("sd_ready"))
                then(V.reciprocal(st32b[:, 0:16], st32[:, 0:16]))
                then(V.tensor_scalar(st32b[:, 0:16], st32b[:, 0:16], 1.0 - lambda_init(l), None, ALU.mult))
                for h in range(4):
                    z = ytok[:, :, h * P:(h + 1) * P]
                    r = st32b[:, 0:16].rearrange("p (t h) -> p t h", h=4)[:, :, h:h + 1].to_broadcast([P, NT, P])
                    V.tensor_tensor(z, z, r, ALU.mult).then_inc(S["y_ready"], 1)
                lo_chunks(4, yH, yL, lambda k: g_sub[l])
                dense(L, "U30", merge(L, 3, 0))
                dense(L, "U31", merge(L, 3, 1))
                lo_chunks(KD, hH, hL, lambda k: 0.5)
                dense(L, "O0", residual(0))
                dense(L, "O1", residual(1, True))
                to_xn()
                lo_chunks(KD, hH, hL, lambda k: g_norm[2 + 2 * l][:, k:k + 1])
                for name in ffn_order():
                    if name[:2] == "FG":
                        dense(L, name, lambda b, t: silu(ytok[:, t, :], bank[t][:, :], b, t))
                    elif name[:2] == "FU":
                        def hid_lo(t):
                            dve.wait_ge(S["hid_hi"], n("hid_hi"))
                            V.tensor_tensor(yL[:, t, :], sbufS[:, t % 2, :], yH[:, t, :].bitcast(F32),
                                            ALU.subtract).then_inc(S["hid_ready"], 1)

                        def fu_evac(b, t):
                            if t >= 2:
                                dve.wait_ge(S["hid_ready"], n.at("hid_hi"))
                            V.scalar_tensor_tensor(out=sbufS[:, t % 2, :], in0=bank[t][:, :], scalar=0.5,
                                                   in1=ytok[:, t, :], op0=ALU.mult, op1=ALU.mult).then_inc(free[t], 1)
                            if t:
                                hid_lo(t - 1)
                        dense(L, name, fu_evac)
                        hid_lo(B(name)[0].banks - 1)
                    else:
                        dense(L, name, residual(int(name[3]), name == ffn_order()[-1]))
            dve.wait_ge(S["hid_ready"], 0 + n.at("hid_hi"))
            V.memset(rs[:, 2:3], 0.0).then_inc(S["late"], 1)
            dve.wait_ge(S["gp_step"], 16 * 6)
            norm_rows(to_x("x_done"))


def constants():
    i = np.arange(P)
    f = np.float32
    ident = np.eye(P, dtype=f)
    causal = np.where(i[None, :] > i[:, None], f(-BIG), f(0)).astype(f)
    c = np.arange(DH)
    start = np.clip(c - 8, 0, DH - 16)
    inside = (c[None, :] >= start[:, None]) & (c[None, :] < start[:, None] + 16)
    nat = np.where(inside[:, ::-1], f(0), f(-BIG)).astype(f)
    tok = np.arange(SEQ)
    inv = (f(10000.0) ** (-np.arange(16, dtype=f) / f(16))).astype(f)
    ang = [(z.astype(f)[:, None] * inv).astype(f) for z in (tok // 64, tok % 64)]
    cos = np.concatenate([np.cos(z) for z in ang for _ in range(2)], 1).astype(f)
    sin = np.concatenate([s * np.sin(z) for z in ang for s in (-1, 1)], 1).astype(f)
    rope = np.stack([z.reshape(NT, P, DH).transpose(1, 0, 2) for z in (cos, sin)], 1)
    masks = np.zeros((P, LEVELS + 1, P), f)
    s_, t_ = i[:, None], i[None, :]
    for lev in range(LEVELS):
        m = CHUNK >> (lev + 1)
        masks[:, lev] = (s_ // (2 * m) == t_ // (2 * m)) & (s_ % (2 * m) < m) & (t_ % (2 * m) >= m)
    masks[:, LEVELS] = s_ == t_
    slopes = 2.0 ** (-8.0 * np.arange(1, 5) / 4)
    dist = np.abs(np.arange(TABW)[None, :] + i[:, None] - 511)
    alibi = (-(slopes[:, None, None] * dist) / SCALE).astype(f)
    keep4 = np.repeat((t_ >= s_).astype(f)[:, None, :], 4, 1)
    return dict(ident=ident, causal=causal, anti=np.ascontiguousarray(causal.T), nat_mask=np.concatenate([nat, nat], 0),
                rope=rope, level_masks=masks, alibi=alibi, keep4=keep4)


def laid_out(inputs):
    g = {k: np.asarray(v) for k, v in inputs.items()}
    direct = ["x", "w_in", "w_out", "gmlp_ln_g", "gmlp_ln_b", "hgrn_onorm_g", "final_norm_g", "w_in_2", "b_qnorm_g_2",
              "b_knorm_g_2", "d_lambda_q1_2", "d_lambda_k1_2", "d_lambda_q2_2", "d_lambda_k2_2", "w_up_a_2", "w_up_b_2",
              "w_up_c_2", "w_up_d_2", "w_out_2", "w_ffn_gate_2", "w_ffn_up_2", "w_ffn_down_2", "final_g_2"]
    out = {k: g[k] for k in direct}
    out["gmlp_ln_g"] = g["gmlp_ln_g"].reshape(1, 256)
    out["gmlp_ln_b"] = g["gmlp_ln_b"].reshape(1, 256)
    out["norm_gT"] = g["norm_g"][0].reshape(KD, P).T
    out["norm1_gT"] = g["norm1_g_2"].reshape(DEPTH, KD, P).transpose(0, 2, 1)
    out["norm2_gT"] = g["norm2_g_2"].reshape(DEPTH, KD, P).transpose(0, 2, 1)
    out["convT"] = g["a_conv_w_2"].reshape(DEPTH, 3, KD, P).transpose(0, 3, 1, 2).reshape(DEPTH, P, 24)
    gb = g["a_gate_bias_2"].reshape(DEPTH, 2, 2, 4)
    rows = np.zeros((DEPTH, GATE_ROWS, 2), gb.dtype)
    rows[:, 0:4] = gb[:, 0].transpose(0, 2, 1)
    rows[:, 32:36] = gb[:, 1].transpose(0, 2, 1)
    out["gate_biasT"] = rows
    out["a_normT"] = g["a_norm_g_2"].reshape(DEPTH, 4, P).transpose(0, 2, 1)
    out["sublnT"] = g["d_subln_g_2"].reshape(DEPTH, P, 1)
    out["lbT"] = g["hgrn_lb"][0].reshape(2, P).T
    out["fox_bT"] = g["fox_b_f"].reshape(8, 1)
    out["bsT"] = g["gmlp_b_s"][0].T
    out["w_sT"] = g["gmlp_w_s"][0].transpose(2, 0, 1)
    rpb = g["c_rpb_2"].reshape(DEPTH, RPB_LEN)[:, ::-1]
    out["rpb_rev"] = np.pad(rpb, ((0, 0), (RPB_PAD, RPB_PAD)))
    out.update(constants())
    return {k: np.ascontiguousarray(v) for k, v in out.items()}


def kernel(**inputs):
    import concourse.bacc as _bacc
    from concourse.bass_utils import run_bass_kernel_spmd as _run

    nc = _bacc.Bacc("TRN2", target_bir_lowering=False, num_devices=1)
    arrays, aps = {}, {}
    for name, v in laid_out(inputs).items():
        arrays[f"in_{name}_dram"] = v
        aps[name] = nc.dram_tensor(f"in_{name}_dram", v.shape, mybir.dt.from_np(v.dtype), kind="ExternalInput").ap()
    out = nc.dram_tensor("out_0_dram", (1, SEQ, D), F32, kind="ExternalOutput").ap()
    build(nc, aps, out)
    r = _run(nc, [arrays], core_ids=[0])
    return r.results[0]["out_0_dram"]
```
